# Optimizing a Trainium2 kernel written in Bass

```python
import math
import jax, jax.numpy as jnp
from jax import lax
import numpy as np

D_MODEL = 1024
BATCH = 1
SEQ = 256
DEPTH = 2

D_MIX = D_MODEL
HEAD_DIM = 64
M_WIDTH = D_MIX // 2
M_HEAD_DIM = 128
M_HEADS = M_WIDTH // M_HEAD_DIM
M_CHUNK = 64
CONV_W = 4
B_WIDTH = D_MIX // 4
B_HEADS = B_WIDTH // HEAD_DIM
MOBA_BLOCK = 256
MOBA_TOPK = 3
N_WIDTH = D_MIX // 4
N_HEADS = N_WIDTH // HEAD_DIM
CMP_LEN = 32
CMP_STRIDE = 16
CMP_HIDDEN = 128
SEL_BLOCK = 64
SEL_TOPK = 16
WINDOW = 512
Q_BLOCK = 64
D_FF = 4 * D_MODEL
ROPE_THETA = 500000.0
ROT_DIM = HEAD_DIM // 4
NORM_EPS = 1e-6
NEG = -1e30
BIG = 1e9

SPLITS = ((M_WIDTH,) * 4 + (M_HEADS, M_HEADS)
          + (B_WIDTH,) * 3
          + (N_WIDTH,) + (HEAD_DIM,) * 6
          + (3 * N_HEADS,))
D_IN = sum(SPLITS)
SPLIT_POINTS = tuple(int(v) for v in np.cumsum(SPLITS)[:-1])


def rmsnorm(x, g):
    xf = x.astype(jnp.float32)
    y = xf * lax.rsqrt(jnp.mean(xf * xf, axis=-1, keepdims=True) + NORM_EPS)
    return (y * g.astype(jnp.float32)).astype(x.dtype)

def partial_rope(x):
    S = x.shape[-2]
    half = ROT_DIM // 2
    inv_freq = jnp.exp(-math.log(ROPE_THETA) * jnp.arange(half, dtype=jnp.float32) * (2.0 / ROT_DIM))
    ang = jnp.arange(S, dtype=jnp.float32)[:, None] * inv_freq[None, :]
    cos, sin = jnp.cos(ang), jnp.sin(ang)
    x1, x2, rest = x[..., :half], x[..., half:ROT_DIM], x[..., ROT_DIM:]
    return jnp.concatenate([x1 * cos - x2 * sin, x2 * cos + x1 * sin, rest], axis=-1)

def causal_conv(x, w):
    S = x.shape[1]
    xp = jnp.pad(x, ((0, 0), (CONV_W - 1, 0), (0, 0)))
    return sum(xp[:, j:j + S] * w[j] for j in range(CONV_W))

def masked_softmax(s, mask):
    p = jax.nn.softmax(jnp.where(mask, s, NEG), axis=-1)
    return jnp.where(mask, p, 0.0)

def mlstm(q, k, v, o_pre, i_pre, f_pre, norm_g):
    B, S, _ = q.shape
    NC, L, H, D = S // M_CHUNK, M_CHUNK, M_HEADS, M_HEAD_DIM

    def to_chunks(t):
        return t.reshape(B, NC, L, H, D).transpose(1, 0, 3, 2, 4)

    qc, kc, vc = to_chunks(q), to_chunks(k) * (D ** -0.5), to_chunks(v)
    lf = jax.nn.log_sigmoid(f_pre).reshape(B, NC, L, H).transpose(1, 0, 3, 2)
    li = i_pre.reshape(B, NC, L, H).transpose(1, 0, 3, 2)
    causal = jnp.tril(jnp.ones((L, L), dtype=bool))

    def step(carry, xs):
        C, n, m = carry
        qt, kt, vt, lft, lit = xs
        b = jnp.cumsum(lft, axis=-1)
        dmat = jnp.where(causal, b[..., :, None] - b[..., None, :] + lit[..., None, :], -jnp.inf)
        inter = b + m[..., None]
        m_t = jnp.maximum(inter, jnp.max(dmat, axis=-1))
        w_intra = jnp.exp(dmat - m_t[..., None])
        w_prev = jnp.exp(inter - m_t)
        s = jnp.einsum('bhtd,bhsd->bhts', qt, kt) * w_intra
        num = jnp.einsum('bhts,bhse->bhte', s, vt) + w_prev[..., None] * jnp.einsum('bhtd,bhde->bhte', qt, C)
        den = jnp.sum(s, axis=-1) + w_prev * jnp.einsum('bhtd,bhd->bht', qt, n)
        h = num / jnp.maximum(jnp.abs(den), jnp.exp(-m_t))[..., None]
        b_last = b[..., -1]
        g = b_last[..., None] - b + lit
        m_new = jnp.maximum(b_last + m, jnp.max(g, axis=-1))
        a = jnp.exp(b_last + m - m_new)
        w_s = jnp.exp(g - m_new[..., None])
        C = a[..., None, None] * C + jnp.einsum('bhs,bhsd,bhse->bhde', w_s, kt, vt)
        n = a[..., None] * n + jnp.einsum('bhs,bhsd->bhd', w_s, kt)
        return (C, n, m_new), h

    init = (jnp.zeros((B, H, D, D), jnp.float32), jnp.zeros((B, H, D), jnp.float32),
            jnp.zeros((B, H), jnp.float32))
    _, h = lax.scan(step, init, (qc, kc, vc, lf, li))
    h = h.transpose(1, 0, 3, 2, 4).reshape(B, S, H, D)
    h = rmsnorm(h, norm_g.reshape(H, D)).reshape(B, S, M_WIDTH)
    return jax.nn.sigmoid(o_pre) * h

def moba(q, k, v, q_g, k_g):
    B, S, _ = q.shape
    H, D, BS = B_HEADS, HEAD_DIM, MOBA_BLOCK
    heads = lambda t: t.reshape(B, S, H, D).transpose(0, 2, 1, 3)
    q = partial_rope(rmsnorm(heads(q), q_g))
    k = partial_rope(rmsnorm(heads(k), k_g))
    v = heads(v)
    NB = -(-S // BS)
    pad = NB * BS - S
    kp = jnp.pad(k, ((0, 0), (0, 0), (0, pad), (0, 0)))
    vp = jnp.pad(v, ((0, 0), (0, 0), (0, pad), (0, 0)))
    kb = kp.reshape(B, H, NB, BS, D)
    vb = vp.reshape(B, H, NB, BS, D)
    kmean = jnp.mean(kb, axis=3)
    topk = min(MOBA_TOPK, NB)
    scale = D ** -0.5
    gather = jax.vmap(jax.vmap(lambda blocks, idx: blocks[idx]))

    def block(j):
        t0 = j * Q_BLOCK
        tq = t0 + jnp.arange(Q_BLOCK)
        qj = lax.dynamic_slice_in_dim(q, t0, Q_BLOCK, axis=2)
        own = t0 // BS
        gs = jnp.einsum('bhqd,bhnd->bhqn', qj, kmean)
        gs = jnp.where(jnp.arange(NB) < own, gs, NEG)
        _, idx = lax.top_k(gs, topk)
        gk, gv = gather(kb, idx), gather(vb, idx)
        s_sel = jnp.einsum('bhqd,bhqrkd->bhqrk', qj, gk) * scale
        s_sel = jnp.where((jnp.arange(topk) < own)[:, None], s_sel, NEG).reshape(B, H, Q_BLOCK, topk * BS)
        ko = lax.dynamic_slice_in_dim(kp, own * BS, BS, axis=2)
        vo = lax.dynamic_slice_in_dim(vp, own * BS, BS, axis=2)
        s_own = jnp.einsum('bhqd,bhkd->bhqk', qj, ko) * scale
        s_own = jnp.where(own * BS + jnp.arange(BS)[None, :] <= tq[:, None], s_own, NEG)
        p = jax.nn.softmax(jnp.concatenate([s_sel, s_own], axis=-1), axis=-1)
        p_sel = p[..., :topk * BS].reshape(B, H, Q_BLOCK, topk, BS)
        p_own = p[..., topk * BS:]
        return (jnp.einsum('bhqrk,bhqrkd->bhqd', p_sel, gv)
                + jnp.einsum('bhqk,bhkd->bhqd', p_own, vo))

    out = lax.map(block, jnp.arange(S // Q_BLOCK))
    return out.transpose(1, 0, 3, 2, 4).reshape(B, S, B_WIDTH)

def nsa(q, kc, vc, ks, vs, kw, vw, g_pre, q_g, k_g, pe, w1, w2):
    B, S, _ = q.shape
    H, D = N_HEADS, HEAD_DIM
    scale = D ** -0.5
    q = rmsnorm(q.reshape(B, S, H, D), q_g).transpose(0, 2, 1, 3)
    qr = partial_rope(q)
    ks = partial_rope(rmsnorm(ks, k_g[1]))
    kw = partial_rope(rmsnorm(kw, k_g[2]))

    n_sub = CMP_LEN // CMP_STRIDE
    Nc = S // CMP_STRIDE - n_sub + 1

    def compress(t, pe_, w1_, w2_):
        c = t.reshape(B, S // CMP_STRIDE, CMP_STRIDE, D)
        blocks = jnp.concatenate([c[:, r:Nc + r] for r in range(n_sub)], axis=2) + pe_
        hid = jax.nn.silu(blocks.reshape(B, Nc, CMP_LEN * D) @ w1_)
        return hid @ w2_

    Kc = rmsnorm(compress(kc, pe[0], w1[0], w2[0]), k_g[0])
    Vc = compress(vc, pe[1], w1[1], w2[1])
    c_end = jnp.arange(Nc) * CMP_STRIDE + CMP_LEN - 1

    Nsel = S // SEL_BLOCK
    c_start = np.arange(Nc) * CMP_STRIDE
    s_start = np.arange(Nsel) * SEL_BLOCK
    overlap = jnp.asarray(((c_start[:, None] < s_start[None, :] + SEL_BLOCK)
                           & (c_start[:, None] + CMP_LEN > s_start[None, :])).astype(np.float32))
    ksb = ks.reshape(B, Nsel, SEL_BLOCK, D)
    vsb = vs.reshape(B, Nsel, SEL_BLOCK, D)
    ksel = min(SEL_TOPK, Nsel)
    gather_b = jax.vmap(lambda blocks, idx: blocks[idx])
    kw_pad = jnp.pad(kw, ((0, 0), (WINDOW, 0), (0, 0)))
    vw_pad = jnp.pad(vw, ((0, 0), (WINDOW, 0), (0, 0)))
    gates = jax.nn.sigmoid(g_pre).reshape(B, S, 3, H)

    def block(j):
        t0 = j * Q_BLOCK
        tq = t0 + jnp.arange(Q_BLOCK)
        qj = lax.dynamic_slice_in_dim(q, t0, Q_BLOCK, axis=2)
        qrj = lax.dynamic_slice_in_dim(qr, t0, Q_BLOCK, axis=2)
        s_c = jnp.einsum('bhqd,bcd->bhqc', qj, Kc) * scale
        p_c = masked_softmax(s_c, c_end[None, :] <= tq[:, None])
        o_c = jnp.einsum('bhqc,bcd->bhqd', p_c, Vc)
        imp = jnp.einsum('bhqc,cn->bqn', p_c, overlap)
        blk_q = tq // SEL_BLOCK
        jn = jnp.arange(Nsel)
        causal_blk = jn[None, :] <= blk_q[:, None]
        forced = causal_blk & ((jn[None, :] == 0) | (jn[None, :] >= blk_q[:, None] - 1))
        imp = jnp.where(forced, BIG, jnp.where(causal_blk, imp, NEG))
        _, sidx = lax.top_k(imp, ksel)
        gk, gv = gather_b(ksb, sidx), gather_b(vsb, sidx)
        pos = sidx[..., None] * SEL_BLOCK + jnp.arange(SEL_BLOCK)
        mask_s = (pos <= tq[None, :, None, None])[:, None]
        s_s = jnp.where(mask_s, jnp.einsum('bhqd,bqrkd->bhqrk', qrj, gk) * scale, NEG)
        p_s = jax.nn.softmax(s_s.reshape(B, H, Q_BLOCK, ksel * SEL_BLOCK), axis=-1)
        o_s = jnp.einsum('bhqrk,bqrkd->bhqd', p_s.reshape(B, H, Q_BLOCK, ksel, SEL_BLOCK), gv)
        kwj = lax.dynamic_slice_in_dim(kw_pad, t0, WINDOW + Q_BLOCK, axis=1)
        vwj = lax.dynamic_slice_in_dim(vw_pad, t0, WINDOW + Q_BLOCK, axis=1)
        posw = t0 - WINDOW + jnp.arange(WINDOW + Q_BLOCK)
        mask_w = ((posw[None, :] <= tq[:, None]) & (posw[None, :] > tq[:, None] - WINDOW)
                  & (posw[None, :] >= 0))
        s_w = jnp.where(mask_w, jnp.einsum('bhqd,bkd->bhqk', qrj, kwj) * scale, NEG)
        o_w = jnp.einsum('bhqk,bkd->bhqd', jax.nn.softmax(s_w, axis=-1), vwj)
        gj = lax.dynamic_slice_in_dim(gates, t0, Q_BLOCK, axis=1).transpose(0, 2, 3, 1)[..., None]
        return gj[:, 0] * o_c + gj[:, 1] * o_s + gj[:, 2] * o_w

    out = lax.map(block, jnp.arange(S // Q_BLOCK))
    return out.transpose(1, 0, 3, 2, 4).reshape(B, S, N_WIDTH)

def first_inputs(seed: int = 0) -> dict:
    key = jax.random.key(seed)
    ks = jax.random.split(key, 20)
    nrm = lambda k, shape, s: jax.random.normal(k, shape, jnp.float32) * s
    L = DEPTH
    b_i = nrm(ks[2], (L, M_HEADS), 0.1)
    b_f = jnp.linspace(3.0, 6.0, M_HEADS, dtype=jnp.float32)[None, :] + nrm(ks[3], (L, M_HEADS), 0.1)
    return {
        "x": nrm(ks[0], (BATCH, SEQ, D_MODEL), 1.0),
        "w_in": nrm(ks[1], (L, D_MODEL, D_IN), D_MODEL ** -0.5),
        "b_if": jnp.concatenate([b_i, b_f], axis=-1),
        "conv_qk": nrm(ks[4], (L, CONV_W, 2 * M_WIDTH), CONV_W ** -0.5),
        "m_norm": 1.0 + nrm(ks[5], (L, M_WIDTH), 0.02),
        "moba_qk_norm": 1.0 + nrm(ks[6], (L, 2, HEAD_DIM), 0.02),
        "nsa_q_norm": 1.0 + nrm(ks[7], (L, HEAD_DIM), 0.02),
        "nsa_k_norm": 1.0 + nrm(ks[8], (L, 3, HEAD_DIM), 0.02),
        "cmp_pe": nrm(ks[9], (L, 2, CMP_LEN, HEAD_DIM), 0.02),
        "cmp_w1": nrm(ks[10], (L, 2, CMP_LEN * HEAD_DIM, CMP_HIDDEN), (CMP_LEN * HEAD_DIM) ** -0.5),
        "cmp_w2": nrm(ks[11], (L, 2, CMP_HIDDEN, HEAD_DIM), CMP_HIDDEN ** -0.5),
        "w_out": nrm(ks[12], (L, D_MIX, D_MODEL), D_MIX ** -0.5),
        "norm_mix": 1.0 + nrm(ks[13], (L, D_MODEL), 0.02),
        "norm_ffn": 1.0 + nrm(ks[14], (L, D_MODEL), 0.02),
        "w_ff1": nrm(ks[15], (L, D_MODEL, D_FF), D_MODEL ** -0.5),
        "w_ff2": nrm(ks[16], (L, D_FF, D_MODEL), D_FF ** -0.5),
    }

def first_block(x, w_in, b_if, conv_qk, m_norm, moba_qk_norm, nsa_q_norm, nsa_k_norm,
              cmp_pe, cmp_w1, cmp_w2, w_out, norm_mix, norm_ffn, w_ff1, w_ff2):
    for l in range(DEPTH):
        h = rmsnorm(x, norm_mix[l])
        proj = jnp.einsum('bsd,de->bse', h, w_in[l]).astype(jnp.float32)
        (m_q, m_k, m_v, m_o, m_i, m_f, b_q, b_k, b_v,
         n_q, n_kc, n_vc, n_ks, n_vs, n_kw, n_vw, n_g) = jnp.split(proj, SPLIT_POINTS, axis=-1)
        qk = jax.nn.silu(causal_conv(jnp.concatenate([m_q, m_k], axis=-1), conv_qk[l]))
        gif = jnp.concatenate([m_i, m_f], axis=-1) + b_if[l]
        y_m = mlstm(qk[..., :M_WIDTH], qk[..., M_WIDTH:], m_v, m_o,
                    gif[..., :M_HEADS], gif[..., M_HEADS:], m_norm[l])
        y_b = moba(b_q, b_k, b_v, moba_qk_norm[l, 0], moba_qk_norm[l, 1])
        y_n = nsa(n_q, n_kc, n_vc, n_ks, n_vs, n_kw, n_vw, n_g, nsa_q_norm[l], nsa_k_norm[l],
                  cmp_pe[l], cmp_w1[l], cmp_w2[l])
        mix = jnp.concatenate([y_m, y_b, y_n], axis=-1).astype(x.dtype)
        x = x + jnp.einsum('bse,ed->bsd', mix, w_out[l])
        h = rmsnorm(x, norm_ffn[l])
        u = jnp.square(jax.nn.relu(jnp.einsum('bsd,df->bsf', h, w_ff1[l])))
        x = x + jnp.einsum('bsf,fd->bsd', u, w_ff2[l])
    return x


CHUNK = 64
Q_BLOCK_2 = 128
N_HEADS_DIFF = 4
DIFF_V_DIM = 2 * HEAD_DIM
N_HEADS_SB = 8
N_HEADS_FOX = 8
W_DIFF = N_HEADS_DIFF * DIFF_V_DIM
W_SB = N_HEADS_SB * HEAD_DIM
W_FOX = N_HEADS_FOX * HEAD_DIM
D_MIX_2 = W_DIFF + W_SB + W_FOX
ROT_DIM_2 = HEAD_DIM // 4
IN_SPLITS = [W_DIFF, W_DIFF, W_DIFF, W_DIFF,
             W_SB, W_SB, W_SB, W_SB,
             W_FOX, W_FOX, W_FOX, W_FOX,
             N_HEADS_FOX]
D_IN_2 = sum(IN_SPLITS)


def rms_norm(x, gain):
    xf = x.astype(jnp.float32)
    y = xf * lax.rsqrt(jnp.mean(xf * xf, axis=-1, keepdims=True) + NORM_EPS)
    return (y * gain.astype(jnp.float32)).astype(x.dtype)

def rope_tables(seq):
    pos = jnp.arange(seq, dtype=jnp.float32)
    inv_freq = ROPE_THETA ** (-jnp.arange(0, ROT_DIM_2, 2, dtype=jnp.float32) / ROT_DIM_2)
    ang = pos[:, None] * inv_freq[None, :]
    return jnp.cos(ang), jnp.sin(ang)

def apply_partial_rope(t, cos, sin):
    rot, rest = t[..., :ROT_DIM_2], t[..., ROT_DIM_2:]
    r1, r2 = rot[..., :ROT_DIM_2 // 2], rot[..., ROT_DIM_2 // 2:]
    rot = jnp.concatenate([r1 * cos - r2 * sin, r2 * cos + r1 * sin], axis=-1).astype(t.dtype)
    return jnp.concatenate([rot, rest], axis=-1)

def diff_attention(q, k, v, lam, lambda_init, sub_gain):
    seq = q.shape[3]
    scale = q.shape[-1] ** -0.5
    chunk_id = jnp.arange(seq) // CHUNK
    outs = []
    for i in range(seq // Q_BLOCK_2):
        q0, q1 = i * Q_BLOCK_2, (i + 1) * Q_BLOCK_2
        s = jnp.einsum('bhcqd,bhckd->bhcqk', q[:, :, :, q0:q1], k[:, :, :, :q1]).astype(jnp.float32) * scale
        allowed = chunk_id[:q1][None, :] <= chunk_id[q0:q1][:, None]
        p = jax.nn.softmax(jnp.where(allowed, s, -jnp.inf), axis=-1)
        w = p[:, :, 0] - lam * p[:, :, 1]
        outs.append(jnp.einsum('bhqk,bhkd->bhqd', w, v[:, :, :q1].astype(jnp.float32)))
    o = jnp.concatenate(outs, axis=2)
    return rms_norm(o, sub_gain) * (1.0 - lambda_init)

def stick_breaking_attention(q, k, v):
    seq = q.shape[2]
    scale = q.shape[-1] ** -0.5
    pos = jnp.arange(seq)
    outs = []
    for i in range(seq // Q_BLOCK_2):
        q0, q1 = i * Q_BLOCK_2, (i + 1) * Q_BLOCK_2
        z = jnp.einsum('bhqd,bhkd->bhqk', q[:, :, q0:q1], k[:, :, :q1]).astype(jnp.float32) * scale
        strict = pos[:q1][None, :] < pos[q0:q1][:, None]
        log_keep = jnp.where(strict, jax.nn.log_sigmoid(-z), 0.0)
        log_rest = lax.cumsum(log_keep, axis=3, reverse=True) - log_keep
        a = jnp.where(strict, jnp.exp(jax.nn.log_sigmoid(z) + log_rest), 0.0)
        outs.append(jnp.einsum('bhqk,bhkd->bhqd', a, v[:, :, :q1].astype(jnp.float32)))
    return jnp.concatenate(outs, axis=2)

def forgetting_attention(q, k, v, cum_log_f):
    seq = q.shape[2]
    scale = q.shape[-1] ** -0.5
    pos = jnp.arange(seq)
    outs = []
    for i in range(seq // Q_BLOCK_2):
        q0, q1 = i * Q_BLOCK_2, (i + 1) * Q_BLOCK_2
        logits = jnp.einsum('bhqd,bhkd->bhqk', q[:, :, q0:q1], k[:, :, :q1]).astype(jnp.float32) * scale
        logits = logits + cum_log_f[:, :, q0:q1, None] - cum_log_f[:, :, None, :q1]
        causal = pos[:q1][None, :] <= pos[q0:q1][:, None]
        p = jax.nn.softmax(jnp.where(causal, logits, -jnp.inf), axis=-1)
        outs.append(jnp.einsum('bhqk,bhkd->bhqd', p, v[:, :, :q1].astype(jnp.float32)))
    return jnp.concatenate(outs, axis=2)

def hybrid_layer(x, w_in, f_bias, lam_vec, subln, w_out, g_pre, g_post, layer_idx, cos, sin):
    b, s, _ = x.shape
    dt = x.dtype
    h = rms_norm(x, g_pre)
    p = h @ w_in
    split_at = np.cumsum(IN_SPLITS)[:-1].tolist()
    qa, ka, va, ga, qs, ks, vs, gs, qf, kf, vf, gf, ff = jnp.split(p, split_at, axis=-1)

    def heads(t, n, d):
        return t.reshape(b, s, n, d).transpose(0, 2, 1, 3)

    def merge(t):
        return t.transpose(0, 2, 1, 3).reshape(b, s, -1).astype(dt)

    qa = apply_partial_rope(qa.reshape(b, s, N_HEADS_DIFF, 2, HEAD_DIM).transpose(0, 2, 3, 1, 4), cos, sin)
    ka = apply_partial_rope(ka.reshape(b, s, N_HEADS_DIFF, 2, HEAD_DIM).transpose(0, 2, 3, 1, 4), cos, sin)
    lambda_init = 0.8 - 0.6 * math.exp(-0.3 * layer_idx)
    lv = lam_vec.astype(jnp.float32)
    lam = jnp.exp(jnp.sum(lv[0] * lv[1])) - jnp.exp(jnp.sum(lv[2] * lv[3])) + lambda_init
    ya = merge(diff_attention(qa, ka, heads(va, N_HEADS_DIFF, DIFF_V_DIM), lam, lambda_init, subln))
    ya = ya * jax.nn.silu(ga)

    yb = merge(stick_breaking_attention(heads(qs, N_HEADS_SB, HEAD_DIM), heads(ks, N_HEADS_SB, HEAD_DIM),
                                        heads(vs, N_HEADS_SB, HEAD_DIM)))
    yb = yb * jax.nn.silu(gs)

    log_f = jax.nn.log_sigmoid((ff + f_bias).astype(jnp.float32)).transpose(0, 2, 1)
    cum_log_f = jnp.cumsum(log_f, axis=-1)
    yc = merge(forgetting_attention(heads(qf, N_HEADS_FOX, HEAD_DIM), heads(kf, N_HEADS_FOX, HEAD_DIM),
                                    heads(vf, N_HEADS_FOX, HEAD_DIM), cum_log_f))
    yc = yc * jax.nn.silu(gf)

    y = jnp.concatenate([ya, yb, yc], axis=-1) @ w_out
    return x + rms_norm(y, g_post)

def second_inputs(seed: int = 0) -> dict:
    key = jax.random.key(seed)
    ks = jax.random.split(key, 8)
    x = jax.random.normal(ks[0], (BATCH, SEQ, D_MODEL), jnp.float32)
    w_in = jax.random.normal(ks[1], (DEPTH, D_MODEL, D_IN_2), jnp.float32) * D_MODEL ** -0.5
    forget_bias = jax.random.uniform(ks[2], (DEPTH, N_HEADS_FOX), jnp.float32, minval=1.0, maxval=4.0)
    diff_lambda = 0.1 * jax.random.normal(ks[3], (DEPTH, 4, HEAD_DIM), jnp.float32)
    diff_subln = 1.0 + 0.02 * jax.random.normal(ks[4], (DEPTH, DIFF_V_DIM), jnp.float32)
    w_out = jax.random.normal(ks[5], (DEPTH, D_MIX_2, D_MODEL), jnp.float32) * D_MIX_2 ** -0.5
    pre_norm = 1.0 + 0.02 * jax.random.normal(ks[6], (DEPTH, D_MODEL), jnp.float32)
    post_norm = 1.0 + 0.02 * jax.random.normal(ks[7], (DEPTH, D_MODEL), jnp.float32)
    return {"x": x, "w_in": w_in, "forget_bias": forget_bias, "diff_lambda": diff_lambda,
            "diff_subln": diff_subln, "w_out": w_out, "pre_norm": pre_norm, "post_norm": post_norm}

def second_block(x, w_in, forget_bias, diff_lambda, diff_subln, w_out, pre_norm, post_norm):
    cos, sin = rope_tables(x.shape[1])
    for l in range(DEPTH):
        x = hybrid_layer(x, w_in[l], forget_bias[l], diff_lambda[l], diff_subln[l], w_out[l],
                         pre_norm[l], post_norm[l], l, cos, sin)
    return x


def setup_inputs(seed=0):
    out = dict(first_inputs(seed))
    for name, value in second_inputs(seed + 1).items():
        if name != "x":
            out[name + "_2"] = value
    return out


def reference(
    x, w_in, b_if, conv_qk, m_norm, moba_qk_norm, nsa_q_norm, nsa_k_norm, cmp_pe, cmp_w1,
    cmp_w2, w_out, norm_mix, norm_ffn, w_ff1, w_ff2, w_in_2, forget_bias_2, diff_lambda_2,
    diff_subln_2, w_out_2, pre_norm_2, post_norm_2,
):
    x = first_block(
        x, w_in, b_if, conv_qk, m_norm, moba_qk_norm, nsa_q_norm, nsa_k_norm, cmp_pe, cmp_w1,
        cmp_w2, w_out, norm_mix, norm_ffn, w_ff1, w_ff2,
    )
    return second_block(
        x, w_in_2, forget_bias_2, diff_lambda_2, diff_subln_2, w_out_2, pre_norm_2, post_norm_2,
    )


_drawn_inputs = setup_inputs


def setup_inputs(seed=0):
    import zlib

    import numpy as np

    out = dict(_drawn_inputs(seed))
    spreads = {}
    factors = {'m_norm': 4.388,
     'moba_qk_norm': 8.0,
     'nsa_q_norm': 8.0,
     'nsa_k_norm': 8.0,
     'cmp_pe': 8.0,
     'diff_subln_2': 7.181,
     'pre_norm_2': 2.988,
     'post_norm_2': 4.612}
    for name, (base, spread) in spreads.items():
        noise = np.random.default_rng([zlib.crc32(name.encode()), seed]).standard_normal(out[name].shape)
        drawn = base * np.exp(spread * noise) if base else spread * noise
        out[name] = __import__('jax').numpy.asarray(drawn.astype(out[name].dtype))
    for name, factor in factors.items():
        out[name] = (out[name] * factor).astype(out[name].dtype)
    return out
```

```python
from contextlib import ExitStack

import numpy as np

import concourse.bass as bass
from concourse import mybir

F32 = mybir.dt.float32
BF16 = mybir.dt.bfloat16
ALU = mybir.AluOpType
ACT = mybir.ActivationFunctionType
AX = mybir.AxisListType
LOG_EXP = "natural_log_exp_and_others"

P = 128
T = 256
NT = T // P
D = 1024
KD = D // P
L = 2
DFF = 4096
HD = 64
EPS = 1e-6
NEG = -1e30
SCALE = HD ** -0.5
M_SCALE = 128 ** -0.5
MH = 4
NC_CMP = 15
COLS1 = 3476
COLS2 = 6152
REST0 = 2048
RESTW = COLS1 - REST0
NVEC = 22
KMIX2 = 12
SLOTS = 4
TILE = 8 * 512
PROJ1 = [4, 5, 6, 0, 1, 2, 3]
PROJ2 = [0, 1, 4, 5, 8, 9, 2, 6, 10, 3, 7, 11]
FEATURE1 = (0, 1)
FEATURE2 = (4, 5, 8, 9)
LAM_INIT = [0.8 - 0.6 * float(np.exp(-0.3 * l)) for l in range(L)]

C_ID, C_CAUSAL, C_CHUNK, C_STRICT, C_LE, C_RTRI, C_ONES, C_NONES = (128 * n for n in range(8))
C_COS = 1024
C_SIN = C_COS + NT * 8
C_CNEG = C_SIN + NT * 8
C_C01 = C_CNEG + NT * NC_CMP
C_END = C_C01 + NT * NC_CMP


def constants():
    c = np.zeros((P, C_END), np.float32)
    a, b = np.arange(P)[:, None], np.arange(P)[None, :]
    c[:, C_ID:C_ID + P] = a == b
    c[:, C_CAUSAL:C_CAUSAL + P] = np.where(b > a, np.float32(NEG), 0)
    c[:, C_CHUNK:C_CHUNK + P] = np.where(b // 64 > a // 64, np.float32(NEG), 0)
    c[:, C_STRICT:C_STRICT + P] = np.where(a >= b, np.float32(NEG), 0)
    c[:, C_LE:C_LE + P] = a <= b
    c[:, C_RTRI:C_RTRI + P] = np.where(a >= b, -1, 0)
    c[:, C_ONES:C_ONES + P] = 1
    c[:, C_NONES:C_NONES + P] = -1
    freq = np.exp(np.float32(-np.log(500000.0)) * np.arange(8, dtype=np.float32) * np.float32(2.0 / 16))
    tok = (np.arange(NT)[None, :] * P + np.arange(P)[:, None]).astype(np.float32)
    ang = (tok[:, :, None] * freq.astype(np.float32)).astype(np.float32)
    c[:, C_COS:C_COS + NT * 8] = np.cos(ang).reshape(P, -1)
    c[:, C_SIN:C_SIN + NT * 8] = np.sin(ang).reshape(P, -1)
    seen = (np.arange(NC_CMP) * 16 + 31)[None, None, :] <= tok[:, :, None]
    c[:, C_CNEG:C_CNEG + NT * NC_CMP] = np.where(seen, 0, np.float32(NEG)).reshape(P, -1)
    c[:, C_C01:C_C01 + NT * NC_CMP] = seen.reshape(P, -1)
    sel = np.zeros((8, 8 * P), np.float32)
    for h in range(8):
        sel[h, h * P:(h + 1) * P] = 1
    return c, sel


def hybrid_blocks(nc, x, w_in, b_if, conv_qk, m_norm, moba_qk_norm, nsa_q_norm, nsa_k_norm, cmp_pe,
                  cmp_w1, cmp_w2, w_out, norm_mix, norm_ffn, w_ff1, w_ff2, w_in_2, forget_bias_2,
                  diff_lambda_2, diff_subln_2, w_out_2, pre_norm_2, post_norm_2, consts, selector, out):
    bank_of, nth, uses = {}, {}, [0] * 8

    def plan(key, bank):
        bank_of[key], nth[key] = bank, uses[bank]
        uses[bank] += 1

    def plan_spread(name, n, banks):
        for u in range(n):
            plan((*name, u), banks[u % len(banks)])

    tiles, tile_no = [], {}

    def weight(key, halves, freed_by):
        tile_no[key] = len(tiles)
        tiles.append((halves, freed_by))

    partials = [0]

    def plan_out_proj(name, w, chunks):
        plan_spread((*name, "acc"), 4, [0, 1, 2, 3])
        for t in range(chunks // 4):
            rows = w[t * 512:(t + 1) * 512, :].rearrange("(k p) c -> p k c", p=P)
            if t < chunks // 4 - 1:
                partials[0] += 1
                by = ("partial", partials[0])
            else:
                by = ("bank", (*name, "acc", 3))
            weight((*name, t), [rows[:, 0:2, :], rows[:, 2:4, :]], by)

    def plan_proj(name, w, order, cols):
        for pos, j in enumerate(order):
            n = min(512, cols - 512 * j)
            src = w[:, 512 * j:512 * j + n].rearrange("(k p) c -> p k c", p=P)
            yield pos, j, src
            for i in range(2):
                plan((*name, j, i), 2 * (pos % 2) + i)
            weight((*name, j), [src[:, 0:4, :], src[:, 4:8, :]], ("bank", (*name, j, 1)))

    def plan_heads(name, n, groups):
        for h in range(n):
            plan((*name, "S", h), 4 + h % 2)
            plan((*name, "T", h), 6)
        for g in range(groups):
            plan((*name, "O", g), 7 if g % 2 == 0 else 3)

    plan(("params",), 4)
    for l in range(L):
        plan_spread(("norm", 2 * l), 4, [0, 1, 2, 3])
        for pos, j, src in plan_proj(("proj1", l), w_in[l], PROJ1, COLS1):
            if j == 1:
                plan(("gate_sum", l), 4)
            if j == 2:
                plan(("gate_row", l), 5)
                plan_spread(("vec", l), 6, [6, 7, 4, 5])
            if j == 3:
                plan(("m_col", l), 4)
                plan(("m_rows", l, 0), 5)
                plan(("m_rows", l, 1), 6)
                plan(("hidden", l), 7)
                w1 = cmp_w1[l].rearrange("v (a p) e -> p v a e", p=P)
                weight(("cmp", l), [w1[:, 0], w1[:, 1]], ("bank", ("hidden", l)))
                plan(("cmp_kv", l), 7)
        plan(("cmp_kT", l), 6)
        plan(("cmp_s", l, 0), 6)
        plan(("cmp_s", l, 1), 2)
        plan(("cmp_pT", l), 6)
        plan(("cmp_o", l), 6)
        for h in range(MH):
            plan(("mlstm", l, "S", h), 4 + h % 2)
            plan(("mlstm", l, "O", h), 7 if h % 2 == 0 else 3)
        plan_heads(("att1", l), 12, 3)
        plan_spread(("mixT1", l), 4, [0, 1, 2, 3])
        plan_out_proj(("out1", l), w_out[l], 8)
        plan_spread(("norm", 2 * l + 1), 4, [0, 1, 2, 3])
        for t in range(8):
            src = w_ff1[l][:, 512 * t:512 * t + 512].rearrange("(k p) c -> p k c", p=P)
            for i in range(2):
                plan(("ff1", l, t, i), 2 * (t % 2) + i)
            weight(("ff1", l, t), [src[:, 0:4, :], src[:, 4:8, :]], ("bank", ("ff1", l, t, 1)))
        plan_out_proj(("ff2", l), w_ff2[l], 32)
    for l in range(L):
        plan_spread(("norm", 4 + l), 4, [0, 1, 2, 3])
        plan(("forget_f", l), 4)
        for pos, j, src in plan_proj(("proj2", l), w_in_2[l], PROJ2, 6144):
            if j == 4:
                plan(("forget_sum", l), 5)
            if j == 8:
                plan(("forget_row", l), 4)
                plan_spread(("vec2", l), 4, [5, 6, 7, 4])
        plan_heads(("diff", l), 8, 4)
        plan_heads(("fox", l), 8, 2)
        for h in range(8):
            plan(("stick", l, "Z", h), 4 + h % 3)
            plan(("stick", l, "R", h), 4 + h % 3)
        plan(("stick", l, "O", 0), 7)
        plan(("stick", l, "O", 1), 3)
        plan_spread(("mixT2", l), 6, [0, 1, 2, 3])
        plan_out_proj(("out2", l), w_out_2[l], KMIX2)

    with ExitStack() as ctx:
        def sb(name, shape, dt=F32):
            return ctx.enter_context(nc.sbuf_tensor(name, shape, dt))

        def sem(name):
            return ctx.enter_context(nc.semaphore(name))

        bank = [ctx.enter_context(nc.psum_tensor(f"bank{b}", [P, 512], F32)) for b in range(8)]
        bank_filled = [sem(f"bank_filled{b}") for b in range(8)]
        bank_freed = [sem(f"bank_freed{b}") for b in range(8)]

        ring = sb("ring", [P, SLOTS, TILE])
        const = sb("const", [P, C_END])
        sel = sb("sel", [8, 8 * P])
        masks = sb("masks", [P, 4 * P], BF16)
        x_sb = sb("x_sb", [P, NT, D])
        xn = sb("xn", [P, NT, D])
        hT = sb("hT", [P, KMIX2, T])
        mix = sb("mix", [P, NT, KMIX2 * P])
        arena = sb("arena", [P, 10240])
        vec = sb("vec", [P, NT, 24, HD])
        vecT = sb("vecT", [P, 12, T])
        probs = sb("probs", [P, 2, 384])
        probsT = sb("probsT", [P, 2, 384])
        ones2 = sb("ones2", [P, NT, MH])
        prm = sb("prm", [P, 192])
        bif = sb("bif", [P, L, 8])
        g_vec = sb("g_vec", [P, L, 6, HD])
        m_gain = sb("m_gain", [P, L, 512])
        w2c = sb("w2c", [P, L, 2, HD])
        ff_w = sb("ff_w", [P, L, KD, 8])
        f_bias = sb("f_bias", [P, L, 8])
        lam_v = sb("lam_v", [P, L, 4, HD])
        sub_gain = sb("sub_gain", [P, L, P])
        blocksT = sb("blocksT", [P, 2, 16, NC_CMP])
        kc_n = sb("kc_n", [NC_CMP, 2, HD])
        kcT = sb("kcT", [P, NC_CMP])
        vc_diag = sb("vc_diag", [P, 4, HD])
        p_cmp = sb("p_cmp", [P, NT, 4, 32])
        hid = sb("hid", [P, 2, 2, 16])
        small = sb("small", [P, 512])
        at = [0]

        def few(*shape, rows=P):
            n = int(np.prod(shape))
            a = small[0:rows, at[0]:at[0] + n]
            at[0] += n
            names = " ".join("abcd"[:len(shape)])
            return a.rearrange(f"p ({names}) -> p {names}", **{"abcd"[k]: shape[k] for k in range(1, len(shape))}) if len(shape) > 1 else a

        ss, ms, rstd = few(NT), few(NT), few(NT)
        half_neg = few(8)
        v_ss, v_ms, v_r, v_t = few(NT, NVEC), few(NT, NVEC), few(NT, NVEC), few(NT, NVEC)
        gif, g_e, g_lf, g_F, g_a, m_tok, e_m, m_den = (few(NT, 8) for _ in range(8))
        n_gate = few(NT, 12)
        row_nb = few(2, NT)
        row_mx = few(2, NT)
        row_sum = few(2, 4, NT)
        row_inv = few(4, NT)
        kc_s = few(4)
        c_mx, c_sum = few(NT, 4), few(NT, 4)
        h_ss, h_ms, h_rs = few(NT, MH), few(NT, MH), few(NT, MH)
        lam = few(4)
        y_ss = few(4)
        rows = sb("rows", [8, 3, T])

        def part(lo, *shape):
            n = int(np.prod(shape))
            names = " ".join("abcd"[:len(shape)])
            return arena[:, lo:lo + n].rearrange(f"p ({names}) -> p {names}", **{"abcd"[k]: shape[k] for k in range(1, len(shape))})

        rest = part(0, NT, RESTW)
        squares = part(2856, NT, NVEC, HD)
        intra = part(5672, MH, 384)
        conv_in = part(2856, KD, T + 3)
        h_num = part(2856, NT, MH, 129)
        h_sq = part(2856 + 1032, NT, MH, P)
        m_qk = xn[:, :, :].rearrange("p i (c t) -> p (i c) t", t=T)
        p_cmpT = part(4912, NT, P)
        o_gate = part(7208, NT, MH, P)
        v_aug = part(8232, NT, MH, 130)
        uT = part(0, 32, T)
        relu = xn[:, :, :].rearrange("p i (a t) -> p (i a) t", t=512)
        values = part(0, 3, NT, 512)
        gates = part(3072, NT, 3, 512)
        featT = part(6144, 16, T)
        y_diff = xn[:, :, 0:512].rearrange("p i (h d) -> p i h d", d=P)
        y_tmp = xn[:, :, 512:1024].rearrange("p i (h d) -> p i h d", d=P)
        spare = vec[:, :, :, :].rearrange("p i s d -> p (i s d)")
        keep = spare[:, 0:3 * 384].rearrange("p (b t) -> p b t", b=3)
        post_gain = spare[:, 3 * 384:3 * 384 + D]
        softp = vecT[:, 8:11, :].rearrange("p s t -> p (s t)").rearrange("p (b t) -> p b t", b=2)
        o_tmp = sb("o_tmp", [P, 512])
        prm_rows = o_tmp[:, 0:2 * P]

        ident = const[:, C_ID:C_ID + P]
        ident_b, causal_b, chunk_b, strict_b = (masks[:, n * P:(n + 1) * P] for n in range(4))

        def gain_col(n, k):
            return prm[:, n * 8 + k:n * 8 + k + 1]

        def conv_col(l, tap, c):
            n = 48 + (l * 4 + tap) * 8 + c
            return prm[:, n:n + 1]

        ring_half = [[sem(f"ring{s}_half{k}") for k in range(2)] for s in range(SLOTS)]
        partial_sums = sem("partial_sums")
        x_loaded, prm_loaded, prm_rows_loaded, post_loaded = sem("x_loaded"), sem("prm_loaded"), sem("prm_rows_loaded"), sem("post_loaded")
        prepared = sem("prepared")
        out_stored = sem("out_stored")
        vector_step, scalar_step, pool_step = sem("vector_step"), sem("scalar_step"), sem("pool_step")
        x_ready, sumsq_ready, rstd_ready, xn_ready = sem("x_ready"), sem("sumsq_ready"), sem("rstd_ready"), sem("xn_ready")
        gate_abs, gate_log = sem("gate_abs"), sem("gate_log")
        squared, vec_ms, vec_rstd, vec_ready = sem("squared"), sem("vec_ms"), sem("vec_rstd"), sem("vec_ready")
        logf_ready, a_ready, m_ready = sem("logf_ready"), sem("a_ready"), sem("m_ready")
        conv_done, conv_silu = sem("conv_done"), sem("conv_silu")
        exponent_ready, intra_exp, intra_masked = sem("exponent_ready"), sem("intra_exp"), sem("intra_masked")
        m_col_ready, stabilizer = sem("m_col_ready"), sem("stabilizer")
        blocks_ready, hid_exp, hid_ready = sem("blocks_ready"), sem("hid_exp"), sem("hid_ready")
        kc_ms, kc_rstd, kc_ready = sem("kc_ms"), sem("kc_rstd"), sem("kc_ready")
        cmp_shifted, cmp_exp, cmp_ready = sem("cmp_shifted"), sem("cmp_exp"), sem("cmp_ready")
        nsa_gated = sem("nsa_gated")
        max_ready = sem("max_ready")
        h_inv, h_normed, h_ms_ready, h_rstd_ready, mlstm_mixed = (sem(s) for s in ("h_inv", "h_normed", "h_ms_ready", "h_rstd_ready", "mlstm_mixed"))
        mix_ready = sem("mix_ready")
        relu_ready, u_ready = sem("relu_ready"), sem("u_ready")
        proj_copied = sem("proj_copied")
        lam_dots, lam_exp = sem("lam_dots"), sem("lam_exp")
        stick_log = sem("stick_log")
        y_sumsq, y_ms, y_rstd = sem("y_sumsq"), sem("y_ms"), sem("y_rstd")
        post_free = sem("post_free")
        d_squared = sem("d_squared")

        def filled(eng, key):
            eng.wait_ge(bank_filled[bank_of[key]], nth[key] + 1)

        def drained(eng, key):
            eng.wait_ge(bank_freed[bank_of[key]], nth[key] + 1)

        def tile_ap(key):
            return ring[:, tile_no[key] % SLOTS, :]

        block = ctx.enter_context(nc.Block())

        @block.sync
        def _(sp):
            for n, (halves, _) in enumerate(tiles):
                if n >= SLOTS:
                    kind, what = tiles[n - SLOTS][1]
                    if kind == "bank":
                        filled(sp, what)
                    else:
                        sp.wait_ge(partial_sums, what)
                lo = 0
                for k, src in enumerate(halves):
                    size = src.shape[1] * src.shape[2]
                    dst = ring[:, n % SLOTS, lo:lo + size].rearrange("p (k c) -> p k c", c=src.shape[2])
                    sp.dma_start(dst, src).then_inc(ring_half[n % SLOTS][k], 16)
                    lo += size
            sp.wait_ge(x_ready, 3 * L)
            sp.dma_start(out.rearrange("b (i p) d -> p (b i) d", p=P), x_sb[:, :, :]).then_inc(out_stored, 16)
            sp.wait_ge(out_stored, 16)

        @block.tensor
        def _(pe):
            def open_bank(key):
                if nth[key]:
                    pe.wait_ge(bank_freed[bank_of[key]], nth[key])
                return bank[bank_of[key]]

            def close(mm, key):
                mm.then_inc(bank_filled[bank_of[key]], 1)

            def half_arrived(key, k):
                n = tile_no[key]
                pe.wait_ge(ring_half[n % SLOTS][k], 16 * (n // SLOTS + 1))

            def transpose_rows(name, src, chunks):
                for u in range(chunks // 2):
                    ps = open_bank((*name, u))
                    for c in range(2):
                        for i in range(NT):
                            k = 2 * u + c
                            mm = pe.transpose(ps[:, (2 * c + i) * P:(2 * c + i + 1) * P],
                                              src[:, i, k * P:(k + 1) * P], ident)
                    close(mm, (*name, u))

            def norm_rows(n):
                pe.wait_ge(xn_ready, n + 1)
                transpose_rows(("norm", n), xn, KD)

            def proj_block(name, j, n_name, feature):
                key = (*name, j)
                w = tile_ap(key)
                n = tiles[tile_no[key]][0][0].shape[2]
                w = w[:, 0:8 * n].rearrange("p (k c) -> p k c", c=n)
                for i in range(2):
                    ps = open_bank((*key, i))
                    parts = range(2) if feature else range(1)
                    for c in parts:
                        for k in range(KD):
                            if i == 0 and c == 0 and k % 4 == 0:
                                half_arrived(key, k // 4)
                            if i == 0 and c == 0 and k % 2 == 0:
                                drained(pe, (*n_name, k // 2))
                            if feature:
                                col = (2 * i + c) * P
                                mm = pe.matmul(ps[:, c * T:(c + 1) * T], w[:, k, col:col + P], hT[:, k, :],
                                               start=(k == 0), stop=(k == KD - 1))
                            else:
                                mm = pe.matmul(ps[:, 0:n], hT[:, k, i * P:(i + 1) * P], w[:, k, :],
                                               start=(k == 0), stop=(k == KD - 1))
                    close(mm, (*key, i))

            def out_proj(name, src, chunks, ready):
                ps = [open_bank((*name, "acc", a)) for a in range(4)]
                n_tiles = chunks // 4
                for t in range(n_tiles):
                    w = tile_ap((*name, t)).rearrange("p (k c) -> p k c", c=D)
                    for a in range(4):
                        i, half = a // 2, a % 2
                        for k in range(4):
                            if a == 0 and k % 2 == 0:
                                half_arrived((*name, t), k // 2)
                            if a == 0:
                                ready(4 * t + k)
                            f = 4 * t + k
                            mm = pe.matmul(ps[a][:, :], src[:, f, i * P:(i + 1) * P],
                                           w[:, k, half * 512:(half + 1) * 512],
                                           start=(f == 0), stop=(f == chunks - 1))
                        if t == n_tiles - 1:
                            close(mm, (*name, "acc", a))
                    if t < n_tiles - 1:
                        mm.then_inc(partial_sums, 1)

            def running_sum(key, src, n):
                ps = open_bank(key)
                le, ones = const[:, C_LE:C_LE + P], const[:, C_ONES:C_ONES + P]
                pe.matmul(ps[:, 0:n], le, src[:, 0, 0:n], start=True, stop=True)
                pe.matmul(ps[:, n:2 * n], ones, src[:, 0, 0:n], start=True, stop=False)
                close(pe.matmul(ps[:, n:2 * n], le, src[:, 1, 0:n], start=False, stop=True), key)

            def softmax_heads(name, heads, groups_of):
                n = len(heads)

                def scores(h):
                    q, k, mask, _, _, extra = heads[h]
                    ps = open_bank((*name, "S", h))
                    for lo, i in ((0, 0), (P, 1)):
                        cols = (i + 1) * P
                        pe.matmul(ps[:, lo:lo + cols], q[:, i * P:(i + 1) * P], k[:, 0:cols], start=True, stop=False)
                        if extra is not None:
                            pe.matmul(ps[:, lo:lo + cols], sel[0:8, extra * P:(extra + 1) * P],
                                      rows[0:8, 0, 0:cols], start=False, stop=False)
                        mm = pe.matmul(ps[:, lo + cols - P:lo + cols], ident_b, mask, start=False, stop=True)
                    close(mm, (*name, "S", h))

                scores(0)
                scores(1)
                for h in range(n):
                    drained(pe, (*name, "S", h))
                    ps = open_bank((*name, "T", h))
                    for b in range(3):
                        mm = pe.transpose(ps[:, b * P:(b + 1) * P], probs[:, h % 2, b * P:(b + 1) * P], ident)
                    close(mm, (*name, "T", h))
                    if h + 2 < n:
                        scores(h + 2)
                    g, r = divmod(h, groups_of)
                    if r == 0:
                        open_bank((*name, "O", g))
                    ps = bank[bank_of[(*name, "O", g)]]
                    value, width = heads[h][3], heads[h][4]
                    drained(pe, (*name, "T", h))
                    lo = r * 2 * width
                    pe.matmul(ps[:, lo:lo + width], probsT[:, h % 2, 0:P], value(0), start=True, stop=True)
                    pe.matmul(ps[:, lo + width:lo + 2 * width], probsT[:, h % 2, P:2 * P], value(0), start=True, stop=False)
                    mm = pe.matmul(ps[:, lo + width:lo + 2 * width], probsT[:, h % 2, 2 * P:3 * P], value(1), start=False, stop=True)
                    if r == groups_of - 1:
                        close(mm, (*name, "O", g))

            pe.wait_ge(prm_loaded, 16 * PRM_LOADS)
            pe.wait_ge(prm_rows_loaded, 16 * PRM_ROW_LOADS)
            ps = open_bank(("params",))
            pe.transpose(ps[:, 0:112], prm_rows[0:112, 0:P], const[0:112, C_ID:C_ID + 112])
            close(pe.transpose(ps[:, 112:176], prm_rows[0:64, P:2 * P], const[0:64, C_ID:C_ID + 64]), ("params",))
            pe.wait_ge(prepared, 1)

            for l in range(L):
                norm_rows(2 * l)
                n_name = ("norm", 2 * l)
                for j in PROJ1:
                    if j == 1:
                        pe.wait_ge(logf_ready, l + 1)
                        running_sum(("gate_sum", l), g_lf, 4)
                    if j == 2:
                        ps = open_bank(("gate_row", l))
                        pe.wait_ge(a_ready, l + 1)
                        for i in range(NT):
                            mm = pe.transpose(ps[0:4, i * P:(i + 1) * P], g_a[:, i, 0:4], ident)
                        close(mm, ("gate_row", l))
                        pe.wait_ge(vec_ready, l + 1)
                        transpose_rows(("vec", l), vec[:, :, :, :].rearrange("p i s d -> p i (s d)"), 12)
                    if j == 3:
                        pe.wait_ge(m_ready, l + 1)
                        ps = open_bank(("m_col", l))
                        for i in range(NT):
                            mm = pe.transpose(ps[:, 4 * i:4 * i + 4], rows[0:4, 1, i * P:(i + 1) * P], ident[0:4, 0:4])
                        close(mm, ("m_col", l))
                        for u in range(2):
                            ps = open_bank(("m_rows", l, u))
                            for c in range(2):
                                h = 2 * u + c
                                mm = pe.matmul(ps[:, c * T:(c + 1) * T], sel[0:4, h * P:(h + 1) * P], rows[0:4, 1, :],
                                               start=True, stop=True)
                            close(mm, ("m_rows", l, u))
                        ps = open_bank(("hidden", l))
                        w = tile_ap(("cmp", l)).rearrange("p (v a e) -> p v a e", v=2, a=16)
                        pe.wait_ge(blocks_ready, l + 1)
                        for v in range(2):
                            half_arrived(("cmp", l), v)
                            for a in range(16):
                                mm = pe.matmul(ps[:, 16 * v:16 * v + NC_CMP], w[:, v, a, :], blocksT[:, v, a, :],
                                               start=(a == 0), stop=(a == 15))
                        close(mm, ("hidden", l))
                    proj_block(("proj1", l), j, n_name, j in FEATURE1)
                    if j == 2:
                        pass
                ps = open_bank(("cmp_kv", l))
                pe.wait_ge(hid_ready, l + 1)
                for v in range(2):
                    mm = pe.matmul(ps[0:NC_CMP, v * HD:(v + 1) * HD], hid[:, 1, v, 0:NC_CMP], w2c[:, l, v, :],
                                   start=True, stop=True)
                close(mm, ("cmp_kv", l))

                def m_scores(h):
                    q, k = m_qk[:, h, :], m_qk[:, MH + h, :]
                    ps = open_bank(("mlstm", l, "S", h))
                    pe.matmul(ps[:, 0:T], k[:, 0:P], q, start=True, stop=True)
                    close(pe.matmul(ps[:, T:T + P], k[:, P:T], q[:, P:T], start=True, stop=True), ("mlstm", l, "S", h))

                def m_values(h):
                    ps = open_bank(("mlstm", l, "O", h))
                    drained(pe, ("mlstm", l, "S", h))
                    p = probs[:, h % 2, :]
                    pe.matmul(ps[:, 0:129], p[:, 0:P], v_aug[:, 0, h, 0:129], start=True, stop=True)
                    pe.matmul(ps[:, 129:258], p[:, P:T], v_aug[:, 0, h, 0:129], start=True, stop=False)
                    close(pe.matmul(ps[:, 129:258], p[:, T:T + P], v_aug[:, 1, h, 0:129], start=False, stop=True),
                          ("mlstm", l, "O", h))

                pe.wait_ge(conv_silu, 4 * (l + 1))
                m_scores(0)
                m_scores(1)
                drained(pe, ("proj1", l, 2, 1))
                m_values(0)
                ps = open_bank(("cmp_kT", l))
                pe.wait_ge(kc_ready, l + 1)
                close(pe.transpose(ps[:, 0:NC_CMP], kc_n[:, :, :].rearrange("c r d -> c (r d)"),
                                   ident[0:NC_CMP, 0:NC_CMP]), ("cmp_kT", l))
                m_scores(2)
                m_values(1)
                drained(pe, ("cmp_kT", l))
                for odd in range(2):
                    ps = open_bank(("cmp_s", l, odd))
                    b = HD * odd
                    for i in range(NT):
                        for h in range(2):
                            lo = (i * 2 + h) * 16
                            mm = pe.matmul(ps[:, lo:lo + NC_CMP], vecT[b:b + HD, 10 + h, i * P:(i + 1) * P],
                                           kcT[b:b + HD, :], start=True, stop=True)
                    close(mm, ("cmp_s", l, odd))
                m_scores(3)
                m_values(2)
                ps = open_bank(("cmp_pT", l))
                pe.wait_ge(cmp_ready, l + 1)
                for i in range(NT):
                    mm = pe.transpose(ps[:, i * P:(i + 1) * P], p_cmp[:, i, :, :].rearrange("p h c -> p (h c)"), ident)
                close(mm, ("cmp_pT", l))
                m_values(3)
                ps = open_bank(("cmp_o", l))
                drained(pe, ("cmp_pT", l))
                for i in range(NT):
                    mm = pe.matmul(ps[:, i * T:(i + 1) * T], p_cmpT[:, i, :],
                                   vc_diag[:, :, :].rearrange("p h d -> p (h d)"), start=True, stop=True)
                close(mm, ("cmp_o", l))

                def pair(p, b):
                    return vecT[b:b + HD, p, :]

                def col(c):
                    return lambda i: rest[:, i, c:c + HD]

                heads = []
                for h in range(4):
                    b = HD * (h % 2)
                    heads.append((pair(h // 2, b), pair(2 + h // 2, b), causal_b, col(520 + HD * h), HD, None))
                for p, c in ((6, 1224), (7, 1352)):
                    for h in range(4):
                        b = HD * (h % 2)
                        heads.append((pair(4 + h // 2, b), pair(p, b), causal_b, col(c), HD, None))
                softmax_heads(("att1", l), heads, 4)

                pe.wait_ge(mix_ready, l + 1)
                pe.wait_ge(mlstm_mixed, l + 1)
                transpose_rows(("mixT1", l), mix, 8)

                def mix_there(f):
                    if f % 2 == 0:
                        drained(pe, ("mixT1", l, f // 2))

                out_proj(("out1", l), hT, 8, mix_there)

                norm_rows(2 * l + 1)
                for t in range(8):
                    w = tile_ap(("ff1", l, t)).rearrange("p (k c) -> p k c", c=512)
                    for i in range(2):
                        ps = open_bank(("ff1", l, t, i))
                        for c in range(2):
                            col0 = (2 * i + c) * P
                            for k in range(KD):
                                if i == 0 and c == 0:
                                    if k % 4 == 0:
                                        half_arrived(("ff1", l, t), k // 4)
                                    if t == 0 and k % 2 == 0:
                                        drained(pe, ("norm", 2 * l + 1, k // 2))
                                mm = pe.matmul(ps[:, c * T:(c + 1) * T], w[:, k, col0:col0 + P], hT[:, k, :],
                                               start=(k == 0), stop=(k == KD - 1))
                        close(mm, ("ff1", l, t, i))

                def u_there(f):
                    if f % 2 == 0:
                        pe.wait_ge(u_ready, 16 * l + f // 2 + 1)

                out_proj(("ff2", l), uT, 32, u_there)

            for l in range(L):
                norm_rows(4 + l)
                n_name = ("norm", 4 + l)
                ps = open_bank(("forget_f", l))
                for i in range(NT):
                    for k in range(KD):
                        if k % 2 == 0 and i == 0:
                            drained(pe, (*n_name, k // 2))
                        mm = pe.matmul(ps[:, 8 * i:8 * i + 8], hT[:, k, i * P:(i + 1) * P], ff_w[:, l, k, :],
                                       start=(k == 0), stop=(k == KD - 1))
                close(mm, ("forget_f", l))
                for j in PROJ2:
                    if j == 4:
                        pe.wait_ge(logf_ready, L + l + 1)
                        running_sum(("forget_sum", l), g_lf, 8)
                    if j == 8:
                        ps = open_bank(("forget_row", l))
                        pe.wait_ge(a_ready, L + l + 1)
                        for i in range(NT):
                            mm = pe.transpose(ps[0:8, i * P:(i + 1) * P], g_a[:, i, 0:8], ident)
                        close(mm, ("forget_row", l))
                        pe.wait_ge(vec_ready, L + l + 1)
                        transpose_rows(("vec2", l), vec[:, :, :, :].rearrange("p i s d -> p i (s d)"), 8)
                    proj_block(("proj2", l), j, n_name, j in FEATURE2)

                def pair2(t, p, b):
                    return t[b:b + HD, p, :]

                def value2(s, c, w):
                    return lambda i: values[:, s, i, c:c + w]

                pe.wait_ge(proj_copied, l + 1)
                softmax_heads(("diff", l), [
                    (pair2(vecT, h // 2, HD * (h % 2)), pair2(vecT, 4 + h // 2, HD * (h % 2)), chunk_b,
                     value2(0, P * (h // 2), P), P, None) for h in range(8)], 2)
                softmax_heads(("fox", l), [
                    (pair2(featT, 8 + h // 2, HD * (h % 2)), pair2(featT, 12 + h // 2, HD * (h % 2)), causal_b,
                     value2(2, HD * h, HD), HD, h) for h in range(8)], 4)

                def logits(h):
                    b = HD * (h % 2)
                    q, k = featT[b:b + HD, h // 2, :], featT[b:b + HD, 4 + h // 2, :]
                    ps = open_bank(("stick", l, "Z", h))
                    pe.matmul(ps[:, 0:T], k[:, 0:P], q, start=True, stop=False, skip_group_check=True)
                    pe.matmul(ps[:, T:T + P], k[:, P:T], q[:, P:T], start=False, stop=False, skip_group_check=True)
                    pe.matmul(ps[:, 0:P], ident_b, strict_b, start=False, stop=False, skip_group_check=True)
                    close(pe.matmul(ps[:, T:T + P], ident_b, strict_b, start=False, stop=False, skip_group_check=True),
                          ("stick", l, "Z", h))

                def subtract_rest(h):
                    ps = open_bank(("stick", l, "R", h))
                    kp = keep[:, h % 3, :]
                    rtri, nones = const[:, C_RTRI:C_RTRI + P], const[:, C_NONES:C_NONES + P]
                    pe.matmul(ps[:, 0:T], rtri, kp[:, 0:T], start=False, stop=False, skip_group_check=True)
                    pe.matmul(ps[:, P:T], nones, kp[:, T:T + P], start=False, stop=False, skip_group_check=True)
                    close(pe.matmul(ps[:, T:T + P], rtri, kp[:, T:T + P], start=False, stop=True, skip_group_check=True),
                          ("stick", l, "R", h))

                def stick_values(h):
                    g, r = divmod(h, 4)
                    if r == 0:
                        open_bank(("stick", l, "O", g))
                    drained(pe, ("stick", l, "R", h))
                    ps = bank[bank_of[("stick", l, "O", g)]]
                    a, lo = probs[:, h % 2, :], r * 2 * HD
                    v0, v1 = (values[:, 1, i, HD * h:HD * (h + 1)] for i in range(2))
                    pe.matmul(ps[:, lo:lo + HD], a[:, 0:P], v0, start=True, stop=True)
                    pe.matmul(ps[:, lo + HD:lo + 2 * HD], a[:, P:T], v0, start=True, stop=False)
                    mm = pe.matmul(ps[:, lo + HD:lo + 2 * HD], a[:, T:T + P], v1, start=False, stop=True)
                    if r == 3:
                        close(mm, ("stick", l, "O", g))

                logits(0)
                logits(1)
                for h in range(8):
                    subtract_rest(h)
                    if h >= 1:
                        stick_values(h - 1)
                    if h + 2 < 8:
                        logits(h + 2)
                stick_values(7)

                pe.wait_ge(mix_ready, L + l + 1)
                pe.wait_ge(mlstm_mixed, L + l + 1)
                transpose_rows(("mixT2", l), mix, KMIX2)

                def mix2_there(f):
                    if f % 2 == 0:
                        drained(pe, ("mixT2", l, f // 2))

                out_proj(("out2", l), hT, KMIX2, mix2_there)

        @block.scalar
        def _(act):
            step = [0]

            def link(ins):
                step[0] += 1
                ins.then_inc(scalar_step, 1)
                act.wait_ge(scalar_step, step[0])

            def free(ins, key):
                ins.then_inc(bank_freed[bank_of[key]], 1)
                drained(act, key)

            def src(key):
                filled(act, key)
                return bank[bank_of[key]]

            def evac_norm(n):
                for u in (0, 2):
                    ps = src(("norm", n, u))
                    link(act.activation(hT[:, 2 * u, :], ps[:, 0:T], ACT.Copy, scale=gain_col(n, 2 * u)))
                    free(act.activation(hT[:, 2 * u + 1, :], ps[:, T:2 * T], ACT.Copy, scale=gain_col(n, 2 * u + 1)),
                         ("norm", n, u))

            def evac_turned(name, dst, which):
                for u in which:
                    ps = src((*name, u))
                    free(act.activation(dst[:, 2 * u:2 * u + 2, :], ps[:, :].rearrange("p (c t) -> p c t", c=2), ACT.Copy),
                         (*name, u))

            def sum_squares(n):
                if n:
                    act.wait_ge(x_ready, n)
                else:
                    act.wait_ge(x_loaded, 16)
                link(act.activation(xn[:, 0, :], x_sb[:, 0, :], ACT.Square, accum_out=ss[:, 0:1]))
                act.activation(xn[:, 1, :], x_sb[:, 1, :], ACT.Square, accum_out=ss[:, 1:2]).then_inc(sumsq_ready, 1)

            heads_seen = [0]

            def softmax_heads(name, n, groups_of):
                def exps(h):
                    ps = src((*name, "S", h))
                    heads_seen[0] += 1
                    act.wait_ge(max_ready, heads_seen[0])
                    g, r = divmod(h, groups_of)
                    for lo, i in ((0, 0), (P, 1)):
                        cols = (i + 1) * P
                        ins = act.activation(probs[:, h % 2, lo:lo + cols], ps[:, lo:lo + cols], ACT.Exp, scale=SCALE,
                                             bias=row_nb[:, h % 2, i:i + 1], accum_out=row_sum[:, g % 2, r, i:i + 1])
                        if i == 0:
                            link(ins)
                        else:
                            free(ins, (*name, "S", h))

                def evac(h):
                    ps = src((*name, "T", h))
                    free(act.activation(probsT[:, h % 2, :], ps[:, 0:384], ACT.Copy), (*name, "T", h))

                exps(0)
                for h in range(n):
                    if h + 1 < n:
                        exps(h + 1)
                    evac(h)

            act.dma_start(x_sb[:, :, :], x.rearrange("b (i p) d -> p (b i) d", p=P)).then_inc(x_loaded, 16)
            row_loads = [(prm_rows[16 * l:16 * l + 8, 0:P], norm_mix[l].rearrange("(k p) -> k p", p=P)) for l in range(L)]
            row_loads += [(prm_rows[16 * l + 8:16 * l + 16, 0:P], norm_ffn[l].rearrange("(k p) -> k p", p=P)) for l in range(L)]
            row_loads += [(prm_rows[32:48, 0:P], pre_norm_2.rearrange("l (k p) -> (l k) p", p=P)),
                          (prm_rows[48:112, 0:P], conv_qk.rearrange("l w (k p) -> (l w k) p", p=P)),
                          (prm_rows[0:64, P:2 * P], cmp_pe.rearrange("l v (a b) d -> (l v a) (b d)", b=2))]
            assert len(row_loads) == PRM_ROW_LOADS
            for dst, s in row_loads:
                act.dma_start(dst, s).then_inc(prm_rows_loaded, 16)

            def wide(a):
                return a.partition_broadcast(P)

            loads = [(const[:, :], consts), (sel[:, :], selector), (bif[:, :, :], wide(b_if)),
                     (g_vec[:, :, 0:2, :], wide(moba_qk_norm)), (g_vec[:, :, 2, :], wide(nsa_q_norm)),
                     (g_vec[:, :, 3:6, :], wide(nsa_k_norm)), (m_gain[:, :, :], wide(m_norm)),
                     (w2c[:, :, :, :], cmp_w2.rearrange("l v e d -> e l v d")),
                     (f_bias[:, :, :], wide(forget_bias_2)), (lam_v[:, :, :, :], wide(diff_lambda_2)),
                     (sub_gain[:, :, :], wide(diff_subln_2))]
            loads += [(ff_w[:, l, :, :], w_in_2[l][:, 6144:6152].rearrange("(k p) c -> p k c", p=P)) for l in range(L)]
            assert len(loads) == PRM_LOADS
            for dst, s in loads:
                act.dma_start(dst, s).then_inc(prm_loaded, 16)

            act.preload_act_table_set(LOG_EXP)
            free(act.activation(prm[:, 0:176], src(("params",))[:, 0:176], ACT.Copy), ("params",))

            for l in range(L):
                sum_squares(2 * l)
                evac_norm(2 * l)

                def evac_rest(j):
                    c0 = 512 * j - REST0
                    n = min(512, COLS1 - 512 * j)
                    for i in range(NT):
                        ps = src(("proj1", l, j, i))
                        free(act.activation(rest[:, i, c0:c0 + n], ps[:, 0:n], ACT.Copy), ("proj1", l, j, i))

                evac_rest(4)
                evac_rest(5)
                act.wait_ge(gate_abs, l + 1)
                link(act.activation(g_e[:, :, 0:4], g_e[:, :, 0:4], ACT.Exp))
                act.activation(g_e[:, :, 0:4], g_e[:, :, 0:4], ACT.Ln, bias=1.0).then_inc(gate_log, 1)
                evac_rest(6)
                act.activation(squares.rearrange("p i s d -> p i (s d)"), rest[:, :, 8:8 + NVEC * HD], ACT.Square).then_inc(squared, 1)
                act.wait_ge(vec_ms, l + 1)
                link(act.activation(v_r, v_ms, ACT.Ln))
                act.activation(v_r, v_r, ACT.Exp, scale=-0.5).then_inc(vec_rstd, 1)
                for j in FEATURE1:
                    for i in range(2):
                        ps = src(("proj1", l, j, i))
                        if i == 0 and j == 0:
                            act.wait_ge(vec_ready, l + 1)
                        free(act.activation(conv_in[:, 4 * j + 2 * i:4 * j + 2 * i + 2, 3:3 + T],
                                            ps[:, :].rearrange("p (c t) -> p c t", c=2), ACT.Copy), ("proj1", l, j, i))
                    for i in range(2):
                        act.wait_ge(conv_done, 4 * l + 2 * j + i + 1)
                        c = 4 * j + 2 * i
                        act.activation(m_qk[:, c:c + 2, :], m_qk[:, c:c + 2, :], ACT.Silu).then_inc(conv_silu, 1)
                for u in (0, 1, 2, 3, 5):
                    evac_turned(("vec", l), vecT, [u])
                for i in range(NT):
                    ps = src(("proj1", l, 2, i))
                    free(act.activation(v_aug[:, i, :, 0:P], ps[:, :].rearrange("p (h d) -> p h d", d=P), ACT.Copy),
                         ("proj1", l, 2, i))
                act.preload_act_table_set(LOG_EXP)
                act.wait_ge(m_col_ready, l + 1)
                act.activation(e_m[:, :, 0:4], m_tok[:, :, 0:4], ACT.Exp).then_inc(stabilizer, 1)
                for h in range(MH):
                    act.wait_ge(exponent_ready, MH * l + h + 1)
                    act.activation(intra[:, h, :], intra[:, h, :], ACT.Exp).then_inc(intra_exp, 1)
                ps = src(("hidden", l))
                act.activation(hid[:, 0, :, 0:NC_CMP], ps[:, 0:32].rearrange("p (v c) -> p v c", c=16)[:, :, 0:NC_CMP],
                               ACT.Exp, scale=-1.0).then_inc(hid_exp, 1)
                act.wait_ge(conv_done, 4 * (l + 1))
                for i in range(NT):
                    ps = src(("proj1", l, 3, i))
                    free(act.activation(o_gate[:, i, :, :], ps[:, :].rearrange("p (h d) -> p h d", d=P), ACT.Sigmoid),
                         ("proj1", l, 3, i))
                act.activation(n_gate, rest[:, :, 1416:1428], ACT.Sigmoid).then_inc(nsa_gated, 1)
                act.preload_act_table_set(LOG_EXP)

                def m_evac(h):
                    ps = src(("mlstm", l, "O", h))
                    free(act.activation(h_num[:, :, h, :], ps[:, 0:258].rearrange("p (i d) -> p i d", i=NT), ACT.Copy),
                         ("mlstm", l, "O", h))

                m_evac(0)
                ps = src(("cmp_kT", l))
                free(act.activation(kcT[:, :], ps[:, 0:NC_CMP], ACT.Copy), ("cmp_kT", l))
                m_evac(1)
                act.wait_ge(cmp_shifted, l + 1)
                act.activation(p_cmp[:, :, :, 0:NC_CMP], p_cmp[:, :, :, 0:NC_CMP], ACT.Exp, scale=SCALE).then_inc(cmp_exp, 1)
                m_evac(2)
                ps = src(("cmp_pT", l))
                free(act.activation(p_cmpT[:, :, :], ps[:, 0:T].rearrange("p (i t) -> p i t", i=NT), ACT.Copy), ("cmp_pT", l))
                m_evac(3)
                softmax_heads(("att1", l), 12, 4)
                evac_turned(("mixT1", l), hT, (0, 2))
                sum_squares(2 * l + 1)
                evac_norm(2 * l + 1)
                for t in range(8):
                    for i in range(2):
                        n = 16 * l + 2 * t + i
                        ps = src(("ff1", l, t, i))
                        if n >= 2:
                            act.wait_ge(u_ready, n - 1)
                        free(act.activation(relu[:, i, :], ps[:, :], ACT.Relu), ("ff1", l, t, i))

            for l in range(L):
                sum_squares(4 + l)
                evac_norm(4 + l)
                act.wait_ge(gate_abs, L + l + 1)
                link(act.activation(g_e, g_e, ACT.Exp))
                act.activation(g_e, g_e, ACT.Ln, bias=1.0).then_inc(gate_log, 1)
                act.wait_ge(lam_dots, l + 1)
                act.activation(lam[:, 0:2], lam[:, 0:2], ACT.Exp).then_inc(lam_exp, 1)

                def evac_feature(j, c0, scale):
                    for i in range(2):
                        ps = src(("proj2", l, j, i))
                        free(act.activation(featT[:, c0 + 2 * i:c0 + 2 * i + 2, :],
                                            ps[:, :].rearrange("p (c t) -> p c t", c=2), ACT.Copy, scale=scale),
                             ("proj2", l, j, i))

                for j in PROJ2:
                    if j == 8:
                        ps = src(("forget_row", l))
                        free(act.activation(rows[0:8, 0, :], ps[0:8, 0:T], ACT.Copy), ("forget_row", l))
                        evac_turned(("vec2", l), vecT, range(4))
                        act.dma_start(post_gain, post_norm_2[l].partition_broadcast(P)).then_inc(post_loaded, 16)
                    for i in range(NT):
                        key = ("proj2", l, j, i)
                        if j in FEATURE2:
                            break
                        ps = src(key)
                        if j < 2:
                            dst = vec[:, i, 8 * j:8 * j + 8, :].rearrange("p s d -> p (s d)")
                            if i == 0:
                                free(act.activation(dst, ps[:, :], ACT.Copy), key)
                            else:
                                free(act.activation(dst, ps[:, :], ACT.Copy), key)
                        elif j % 4 == 2:
                            free(act.activation(values[:, j // 4, i, :], ps[:, :], ACT.Copy), key)
                        else:
                            ins = act.activation(gates[:, i, j // 4, :], ps[:, :], ACT.Silu)
                            free(ins, key)
                    if j in FEATURE2:
                        evac_feature(j, {4: 0, 5: 4, 8: 8, 9: 12}[j], SCALE if j == 4 else 1.0)
                act.preload_act_table_set(LOG_EXP)
                act.activation(o_tmp[:, 0:1], ones2[:, 0, 0:1], ACT.Copy).then_inc(proj_copied, 1)
                softmax_heads(("diff", l), 8, 2)
                softmax_heads(("fox", l), 8, 4)

                def softplus(h):
                    ps = src(("stick", l, "Z", h))
                    if h >= 2:
                        drained(act, ("stick", l, "Z", h - 2))
                    link(act.activation(softp[:, h % 2, :], ps[:, 0:384], ACT.Abs))
                    link(act.activation(softp[:, h % 2, :], softp[:, h % 2, :], ACT.Exp, scale=-1.0))
                    act.activation(softp[:, h % 2, :], softp[:, h % 2, :], ACT.Ln, bias=1.0).then_inc(stick_log, 1)

                def weigh(h):
                    ps = src(("stick", l, "R", h))
                    if h >= 3:
                        filled(act, ("stick", l, "R", h))
                    free(act.activation(probs[:, h % 2, :], ps[:, 0:384], ACT.Exp), ("stick", l, "R", h))

                softplus(0)
                for h in range(8):
                    if h + 1 < 8:
                        softplus(h + 1)
                    weigh(h)
                evac_turned(("mixT2", l), hT, (0, 2, 4))
                for a in range(4):
                    ps = src(("out2", l, "acc", a))
                    ins = act.activation(xn[:, a // 2, (a % 2) * 512:(a % 2 + 1) * 512], ps[:, :], ACT.Square,
                                         accum_out=y_ss[:, a:a + 1])
                    ins.then_inc(y_sumsq, 1)

        @block.gpsimd
        def _(pool):
            step = [0]

            def link(ins):
                step[0] += 1
                ins.then_inc(pool_step, 1)
                pool.wait_ge(pool_step, step[0])

            def row_rstd(n):
                pool.wait_ge(sumsq_ready, n + 1)
                link(pool.tensor_scalar(ms, ss, 1.0 / D, EPS, ALU.mult, ALU.add))
                pool.tensor_tensor(rstd, ms, half_neg[:, 0:2], ALU.pow).then_inc(rstd_ready, 1)

            link(pool.memset(half_neg, -0.5))
            for l in range(L):
                row_rstd(2 * l)
                for h in range(MH):
                    pool.wait_ge(intra_exp, MH * l + h + 1)
                    le = const[:, C_LE:C_LE + P]
                    if h == 0 and l == 0:
                        pool.wait_ge(prm_loaded, 16 * PRM_LOADS)
                    link(pool.tensor_tensor(intra[:, h, 0:P], intra[:, h, 0:P], le, ALU.mult))
                    pool.tensor_tensor(intra[:, h, 2 * P:3 * P], intra[:, h, 2 * P:3 * P], le, ALU.mult).then_inc(intra_masked, 1)
                pool.wait_ge(kc_ms, l + 1)
                pool.tensor_tensor(kc_s[0:NC_CMP, 2:3], kc_s[0:NC_CMP, 1:2], half_neg[0:NC_CMP, 0:1], ALU.pow).then_inc(kc_rstd, 1)
                pool.wait_ge(h_inv, l + 1)
                inv = m_den[:, :, 4:8].unsqueeze(3).broadcast_to([P, NT, MH, P])
                link(pool.tensor_tensor(h_num[:, :, :, 0:P], h_num[:, :, :, 0:P], inv, ALU.mult))
                pool.tensor_tensor(h_sq, h_num[:, :, :, 0:P], h_num[:, :, :, 0:P], ALU.mult).then_inc(h_normed, 1)
                pool.wait_ge(h_ms_ready, l + 1)
                link(pool.tensor_tensor(h_rs.rearrange("p a b -> p (a b)"), h_ms.rearrange("p a b -> p (a b)"), half_neg, ALU.pow))
                link(pool.tensor_tensor(h_num[:, :, :, 0:P], h_num[:, :, :, 0:P],
                                        h_rs.unsqueeze(3).broadcast_to([P, NT, MH, P]), ALU.mult))
                pool.wait_ge(nsa_gated, l + 1)
                link(pool.tensor_tensor(h_num[:, :, :, 0:P], h_num[:, :, :, 0:P], o_gate, ALU.mult))
                mg = m_gain[:, l, :].rearrange("p (h d) -> p h d", d=P)
                for i in range(NT):
                    ins = pool.tensor_tensor(mix[:, i, 0:512].rearrange("p (h d) -> p h d", d=P), h_num[:, i, :, 0:P], mg, ALU.mult)
                    if i == 0:
                        link(ins)
                    else:
                        ins.then_inc(mlstm_mixed, 1)
                row_rstd(2 * l + 1)
            for l in range(L):
                row_rstd(4 + l)
                pool.wait_ge(h_ms_ready, L + l + 1)
                link(pool.tensor_tensor(h_rs.rearrange("p a b -> p (a b)"), h_ms.rearrange("p a b -> p (a b)"), half_neg, ALU.pow))
                link(pool.tensor_tensor(y_diff, y_diff, h_rs.unsqueeze(3).broadcast_to([P, NT, MH, P]), ALU.mult))
                sg = sub_gain[:, l, :]
                for i in range(NT):
                    link(pool.tensor_tensor(y_diff[:, i], y_diff[:, i], sg.unsqueeze(1).broadcast_to([P, MH, P]), ALU.mult))
                    link(pool.tensor_scalar(y_diff[:, i], y_diff[:, i], 1.0 - LAM_INIT[l], None, ALU.mult))
                pool.tensor_tensor(mix[:, :, 0:512].rearrange("p i (h d) -> p i h d", d=P), y_diff,
                                   gates[:, :, 0, :].rearrange("p i (h d) -> p i h d", d=P), ALU.mult).then_inc(mlstm_mixed, 1)
                pool.wait_ge(y_ms, l + 1)
                pool.tensor_tensor(rstd, ms, half_neg[:, 0:2], ALU.pow).then_inc(y_rstd, 1)

        @block.vector
        def _(dve):
            step = [0]

            def link(ins):
                step[0] += 1
                ins.then_inc(vector_step, 1)
                dve.wait_ge(vector_step, step[0])

            def free(ins, key):
                ins.then_inc(bank_freed[bank_of[key]], 1)
                drained(dve, key)

            def src(key):
                filled(dve, key)
                return bank[bank_of[key]]

            def tt(out, a, b, op):
                link(dve.tensor_tensor(out, a, b, op))

            def norm_rows(n):
                dve.wait_ge(rstd_ready, n + 1)
                link(dve.tensor_scalar(xn[:, 0, :], x_sb[:, 0, :], rstd[:, 0:1], None, ALU.mult))
                dve.tensor_scalar(xn[:, 1, :], x_sb[:, 1, :], rstd[:, 1:2], None, ALU.mult).then_inc(xn_ready, 1)
                for u in (1, 3):
                    ps = src(("norm", n, u))
                    link(dve.tensor_scalar(hT[:, 2 * u, :], ps[:, 0:T], gain_col(n, 2 * u), None, ALU.mult))
                    free(dve.tensor_scalar(hT[:, 2 * u + 1, :], ps[:, T:2 * T], gain_col(n, 2 * u + 1), None, ALU.mult),
                         ("norm", n, u))

            def evac_turned(name, dst, which):
                for u in which:
                    ps = src((*name, u))
                    free(dve.tensor_copy(dst[:, 2 * u:2 * u + 2, :], ps[:, :].rearrange("p (c t) -> p c t", c=2)), (*name, u))

            def residual(name):
                for a in range(4):
                    ps = src((*name, "acc", a))
                    xs = x_sb[:, a // 2, (a % 2) * 512:(a % 2 + 1) * 512]
                    free(dve.tensor_tensor(xs, xs, ps[:, :], ALU.add), (*name, "acc", a))
                dve.tensor_copy(o_tmp[:, 1:2], ones2[:, 0, 1:2]).then_inc(x_ready, 1)

            def log_sigmoid(n, f, idx):
                dve.scalar_tensor_tensor(g_e[:, :, 0:n], f, -1.0, f, ALU.mult, ALU.min).then_inc(gate_abs, 1)
                dve.wait_ge(gate_log, idx + 1)
                link(dve.tensor_scalar(g_lf[:, :, 0:n], f, 0.0, None, ALU.min))
                dve.tensor_tensor(g_lf[:, :, 0:n], g_lf[:, :, 0:n], g_e[:, :, 0:n], ALU.subtract).then_inc(logf_ready, 1)

            def rope(n):
                a, b = vec[:, :, 0:n, 0:8], vec[:, :, 0:n, 8:16]
                cos = const[:, C_COS:C_COS + NT * 8].rearrange("p (i d) -> p i d", i=NT).unsqueeze(2).broadcast_to([P, NT, n, 8])
                sin = const[:, C_SIN:C_SIN + NT * 8].rearrange("p (i d) -> p i d", i=NT).unsqueeze(2).broadcast_to([P, NT, n, 8])
                t = [o_tmp[:, 0:256], o_tmp[:, 256:512], softp[:, 0, 0:256], softp[:, 1, 0:256]]
                t = [y[:, 0:NT * n * 8].rearrange("p (i s d) -> p i s d", i=NT, d=8) for y in t]
                tt(t[0], a, cos, ALU.mult)
                tt(t[1], b, sin, ALU.mult)
                tt(t[2], b, cos, ALU.mult)
                tt(t[3], a, sin, ALU.mult)
                tt(a, t[0], t[1], ALU.subtract)
                dve.tensor_tensor(b, t[2], t[3], ALU.add).then_inc(vec_ready, 1)

            def softmax_heads(name, n, groups_of, epilogue):
                def row_max(h):
                    ps = src((*name, "S", h))
                    link(dve.tensor_reduce(row_mx[:, h % 2, 0:1], ps[:, 0:P], AX.X, ALU.max))
                    link(dve.tensor_reduce(row_mx[:, h % 2, 1:2], ps[:, P:3 * P], AX.X, ALU.max))
                    dve.tensor_scalar(row_nb[:, h % 2, :], row_mx[:, h % 2, :], -SCALE, None, ALU.mult).then_inc(max_ready, 1)

                done = 0
                for h in range(n):
                    row_max(h)
                    if h >= groups_of + 1 and (h - 1) % groups_of == 0:
                        epilogue(done)
                        done += 1
                while done < n // groups_of:
                    epilogue(done)
                    done += 1

            link(dve.memset(ones2[:, :, :], 1.0))
            link(dve.memset(vc_diag[:, :, :], 0.0))
            link(dve.memset(p_cmp[:, :, :, :], 0.0))
            link(dve.memset(vec[:, :, :, :], 0.0))
            dve.wait_ge(prm_loaded, 16 * PRM_LOADS)
            for n, c in enumerate((C_ID, C_CAUSAL, C_CHUNK)):
                link(dve.tensor_copy(masks[:, n * P:(n + 1) * P], const[:, c:c + P]))
            dve.tensor_copy(masks[:, 3 * P:4 * P], const[:, C_STRICT:C_STRICT + P]).then_inc(prepared, 1)
            drained(dve, ("params",))

            for l in range(L):
                norm_rows(2 * l)
                link(dve.memset(v_aug[:, :, :, 128:130], 1.0))
                drained(dve, ("proj1", l, 4, 1))
                drained(dve, ("proj1", l, 4, 0))
                tt(gif, rest[:, :, 0:8], bif[:, l, :].unsqueeze(1).broadcast_to([P, NT, 8]), ALU.add)
                log_sigmoid(4, gif[:, :, 4:8], l)
                dve.wait_ge(squared, l + 1)
                link(dve.tensor_reduce(v_ss, squares, AX.X, ALU.add))
                dve.tensor_scalar(v_ms, v_ss, 1.0 / HD, EPS, ALU.mult, ALU.add).then_inc(vec_ms, 1)
                dve.wait_ge(vec_rstd, l + 1)
                tt(v_t, v_r, v_r, ALU.mult)
                tt(v_t, v_t, v_ms, ALU.mult)
                link(dve.tensor_scalar(v_t, v_t, -0.5, 1.5, ALU.mult, ALU.add))
                tt(v_r, v_r, v_t, ALU.mult)
                rv = rest[:, :, 8:8 + NVEC * HD].rearrange("p i (s d) -> p i s d", d=HD)

                def scaled(dst, s0, n, gain):
                    o = vec[:, :, dst:dst + n, :]
                    tt(o, rv[:, :, s0:s0 + n, :], v_r[:, :, s0:s0 + n].unsqueeze(3).broadcast_to([P, NT, n, HD]), ALU.mult)
                    tt(o, o, g_vec[:, l, gain, :].unsqueeze(1).unsqueeze(1).broadcast_to([P, NT, n, HD]), ALU.mult)

                scaled(0, 0, 4, 0)
                scaled(4, 4, 4, 1)
                scaled(20, 12, 4, 2)
                scaled(12, 18, 1, 4)
                scaled(14, 20, 1, 5)
                link(dve.tensor_copy(vec[:, :, 8:12, :], vec[:, :, 20:24, :]))
                link(dve.tensor_copy(vec[:, :, 13, :], vec[:, :, 12, :]))
                link(dve.tensor_copy(vec[:, :, 15, :], vec[:, :, 14, :]))
                for s in range(4):
                    link(dve.tensor_copy(vec[:, :, 16 + s, :], rv[:, :, 16 + s // 2, :]))
                link(dve.memset(conv_in[:, :, 0:3], 0.0))
                rope(16)
                ps = src(("gate_sum", l))
                Fv = ps[:, 0:8].rearrange("p (i h) -> p i h", i=NT)
                link(dve.tensor_copy(g_F[:, :, 0:4], Fv))
                free(dve.tensor_tensor(g_a[:, :, 0:4], gif[:, :, 0:4], Fv, ALU.subtract), ("gate_sum", l))
                dve.tensor_copy(o_tmp[:, 1:2], ones2[:, 0, 1:2]).then_inc(a_ready, 1)
                for j in FEATURE1:
                    for i in range(2):
                        drained(dve, ("proj1", l, j, i))
                        for c in (4 * j + 2 * i, 4 * j + 2 * i + 1):
                            acc = m_qk[:, c, :]
                            link(dve.tensor_scalar(acc, conv_in[:, c, 0:T], conv_col(l, 0, c), None, ALU.mult))
                            for tap in range(1, 4):
                                ins = dve.scalar_tensor_tensor(acc, conv_in[:, c, tap:tap + T], conv_col(l, tap, c), acc,
                                                               ALU.mult, ALU.add)
                                if tap == 3 and c % 2 == 1:
                                    ins.then_inc(conv_done, 1)
                                else:
                                    link(ins)
                ps = src(("gate_row", l))
                free(dve.tensor_copy(rows[0:4, 2, :], ps[0:4, 0:T]), ("gate_row", l))
                link(dve.tensor_tensor_scan(rows[0:4, 0, :], rows[0:4, 2, :], rows[0:4, 2, :], 0.0, ALU.max, ALU.max))
                dve.tensor_scalar(rows[0:4, 1, :], rows[0:4, 0, :], -1.0, None, ALU.mult).then_inc(m_ready, 1)
                ps = src(("vec", l, 4))
                for v in range(2):
                    for half in range(2):
                        lo = HD * half
                        t = ps[lo:lo + HD, v * T:(v + 1) * T]
                        pe_col = prm[lo:lo + HD, 112 + (l * 2 + v) * 16:112 + (l * 2 + v) * 16 + 16]
                        for r in range(2):
                            tok = t[:, 16 * r:16 * r + 240].rearrange("p (c a b) -> p a c b", a=8, b=2)[:, :, :, half]
                            ins = dve.tensor_tensor(blocksT[lo:lo + HD, v, 8 * r:8 * r + 8, :], tok,
                                                    pe_col[:, 8 * r:8 * r + 8].unsqueeze(2).broadcast_to([HD, 8, NC_CMP]), ALU.add)
                            if v == 1 and half == 1 and r == 1:
                                free(ins, ("vec", l, 4))
                            else:
                                link(ins)
                dve.tensor_copy(o_tmp[:, 1:2], ones2[:, 0, 1:2]).then_inc(blocks_ready, 1)
                ps = src(("m_col", l))
                free(dve.tensor_tensor(m_tok[:, :, 0:4], ps[:, 0:8].rearrange("p (i h) -> p i h", i=NT), g_F[:, :, 0:4],
                                       ALU.subtract), ("m_col", l))
                dve.tensor_copy(o_tmp[:, 1:2], ones2[:, 0, 1:2]).then_inc(m_col_ready, 1)
                for h in range(MH):
                    u, c = divmod(h, 2)
                    ps = src(("m_rows", l, u))[:, c * T:(c + 1) * T]
                    link(dve.tensor_scalar(intra[:, h, 0:T], ps, g_a[:, 0, h:h + 1], 0.0, ALU.add, ALU.min))
                    ins = dve.tensor_scalar(intra[:, h, T:T + P], ps[:, P:T], g_a[:, 1, h:h + 1], 0.0, ALU.add, ALU.min)
                    if c == 1:
                        free(ins, ("m_rows", l, u))
                    else:
                        link(ins)
                    dve.tensor_copy(o_tmp[:, 1:2], ones2[:, 0, 1:2]).then_inc(exponent_ready, 1)
                dve.wait_ge(hid_exp, l + 1)
                link(dve.tensor_scalar(hid[:, 0, :, 0:NC_CMP], hid[:, 0, :, 0:NC_CMP], 1.0, None, ALU.add))
                link(dve.reciprocal(hid[:, 0, :, 0:NC_CMP], hid[:, 0, :, 0:NC_CMP]))
                ps = src(("hidden", l))
                free(dve.tensor_tensor(hid[:, 1, :, 0:NC_CMP], hid[:, 0, :, 0:NC_CMP],
                                       ps[:, 0:32].rearrange("p (v c) -> p v c", c=16)[:, :, 0:NC_CMP], ALU.mult), ("hidden", l))
                dve.tensor_copy(o_tmp[:, 1:2], ones2[:, 0, 1:2]).then_inc(hid_ready, 1)
                ps = src(("cmp_kv", l))
                link(dve.tensor_copy(kc_n[:, 0, :], ps[0:NC_CMP, 0:HD]))
                for h in range(4):
                    ins = dve.tensor_copy(vc_diag[32 * h:32 * h + NC_CMP, h, :], ps[0:NC_CMP, HD:2 * HD])
                    if h < 3:
                        link(ins)
                    else:
                        free(ins, ("cmp_kv", l))
                tt(kc_n[:, 1, :], kc_n[:, 0, :], kc_n[:, 0, :], ALU.mult)
                link(dve.tensor_reduce(kc_s[0:NC_CMP, 0:1], kc_n[:, 1, :], AX.X, ALU.add))
                dve.tensor_scalar(kc_s[0:NC_CMP, 1:2], kc_s[0:NC_CMP, 0:1], 1.0 / HD, EPS, ALU.mult, ALU.add).then_inc(kc_ms, 1)
                dve.wait_ge(kc_rstd, l + 1)
                link(dve.tensor_scalar(kc_n[:, 0, :], kc_n[:, 0, :], kc_s[0:NC_CMP, 2:3], None, ALU.mult))
                tt(kc_n[:, 0, :], kc_n[:, 0, :], g_vec[0:NC_CMP, l, 3, :], ALU.mult)
                dve.tensor_copy(kc_n[:, 1, :], kc_n[:, 0, :]).then_inc(kc_ready, 1)

                def m_weigh(h):
                    dve.wait_ge(intra_masked, MH * l + h + 1)
                    ps = src(("mlstm", l, "S", h))
                    free(dve.scalar_tensor_tensor(probs[:, h % 2, :], ps[:, 0:384], M_SCALE, intra[:, h, :],
                                                  ALU.mult, ALU.mult), ("mlstm", l, "S", h))

                m_weigh(0)
                m_weigh(1)
                m_weigh(2)
                pc = p_cmp[:, :, :, 0:NC_CMP]

                def cmask(c, n):
                    return const[:, c:c + NT * NC_CMP].rearrange("p (i c) -> p i c", i=NT).unsqueeze(2).broadcast_to([P, NT, n, NC_CMP])

                for odd in range(2):
                    ps = src(("cmp_s", l, odd))
                    free(dve.tensor_tensor(p_cmp[:, :, odd:4:2, 0:NC_CMP],
                                           ps[:, 0:64].rearrange("p (i h c) -> p i h c", i=NT, h=2)[:, :, :, 0:NC_CMP],
                                           cmask(C_CNEG, 2), ALU.add), ("cmp_s", l, odd))
                link(dve.tensor_reduce(c_mx, pc, AX.X, ALU.max))
                dve.tensor_tensor(pc, pc, c_mx.unsqueeze(3).broadcast_to([P, NT, 4, NC_CMP]), ALU.subtract).then_inc(cmp_shifted, 1)
                dve.wait_ge(cmp_exp, l + 1)
                link(dve.tensor_reduce(c_sum, pc, AX.X, ALU.add))
                link(dve.reciprocal(c_sum, c_sum))
                dve.wait_ge(nsa_gated, l + 1)
                tt(c_sum, c_sum, n_gate[:, :, 0:4], ALU.mult)
                tt(pc, pc, c_sum.unsqueeze(3).broadcast_to([P, NT, 4, NC_CMP]), ALU.mult)
                dve.tensor_tensor(pc, pc, cmask(C_C01, 4), ALU.mult).then_inc(cmp_ready, 1)
                m_weigh(3)
                for h in range(MH):
                    drained(dve, ("mlstm", l, "O", h))
                dve.wait_ge(stabilizer, l + 1)
                den = h_num[:, :, :, 128]
                link(dve.scalar_tensor_tensor(m_den[:, :, 0:4], den, -1.0, den, ALU.mult, ALU.max))
                tt(m_den[:, :, 0:4], m_den[:, :, 0:4], e_m[:, :, 0:4], ALU.max)
                dve.reciprocal(m_den[:, :, 4:8], m_den[:, :, 0:4]).then_inc(h_inv, 1)
                ps = src(("cmp_o", l))
                free(dve.tensor_copy(mix[:, :, 768:1024], ps[:, :].rearrange("p (i c) -> p i c", i=NT)), ("cmp_o", l))

                def epilogue1(g):
                    name = ("att1", l, "O", g)
                    ps = src(name)
                    ov = ps[:, :].rearrange("p (h i d) -> p h i d", h=4, i=NT)
                    link(dve.reciprocal(row_inv, row_sum[:, g % 2]))
                    lo = 512 if g == 0 else 768
                    dst = mix[:, :, lo:lo + 256].rearrange("p i (h d) -> p h i d", d=HD)
                    if g:
                        gate = n_gate[:, :, 4 * g:4 * g + 4].rearrange("p i h -> p h i")
                        tt(row_inv, row_inv, gate, ALU.mult)
                    f = row_inv.unsqueeze(3).broadcast_to([P, 4, NT, HD])
                    if g == 0:
                        free(dve.tensor_tensor(dst, ov, f, ALU.mult), name)
                        dve.wait_ge(h_normed, l + 1)
                        link(dve.tensor_reduce(h_ss, h_sq, AX.X, ALU.add))
                        dve.tensor_scalar(h_ms, h_ss, 1.0 / P, EPS, ALU.mult, ALU.add).then_inc(h_ms_ready, 1)
                        return
                    t = o_tmp[:, :].rearrange("p (h i d) -> p h i d", h=4, i=NT)
                    free(dve.tensor_tensor(t, ov, f, ALU.mult), name)
                    ins = dve.tensor_tensor(dst, dst, t, ALU.add)
                    if g == 2:
                        ins.then_inc(mix_ready, 1)
                    else:
                        link(ins)

                softmax_heads(("att1", l), 12, 4, epilogue1)
                evac_turned(("mixT1", l), hT, (1, 3))
                residual(("out1", l))
                norm_rows(2 * l + 1)
                for t in range(8):
                    for i in range(2):
                        drained(dve, ("ff1", l, t, i))
                        r = relu[:, i, :].rearrange("p (c t) -> p c t", c=2)
                        f = 4 * t + 2 * i
                        dve.tensor_tensor(uT[:, f:f + 2, :], r, r, ALU.mult).then_inc(u_ready, 1)
                residual(("ff2", l))

            for l in range(L):
                norm_rows(4 + l)
                ps = src(("forget_f", l))
                free(dve.tensor_tensor(gif, ps[:, 0:16].rearrange("p (i h) -> p i h", i=NT),
                                       f_bias[:, l, :].unsqueeze(1).broadcast_to([P, NT, 8]), ALU.add), ("forget_f", l))
                log_sigmoid(8, gif, L + l)
                prod = o_tmp[:, 0:2 * HD].rearrange("p (a d) -> p a d", a=2)
                lv = lam_v[:, l, :, :].rearrange("p (a b) d -> p a b d", b=2)
                tt(prod, lv[:, :, 0, :], lv[:, :, 1, :], ALU.mult)
                dve.tensor_reduce(lam[:, 0:2], prod, AX.X, ALU.add).then_inc(lam_dots, 1)
                dve.wait_ge(lam_exp, l + 1)
                tt(lam[:, 2:3], lam[:, 1:2], lam[:, 0:1], ALU.subtract)
                link(dve.tensor_scalar(lam[:, 3:4], lam[:, 2:3], -LAM_INIT[l], None, ALU.add))
                for j in (0, 1):
                    for i in range(NT):
                        drained(dve, ("proj2", l, j, i))
                rope(16)
                ps = src(("forget_sum", l))
                free(dve.tensor_scalar(g_a, ps[:, 0:16].rearrange("p (i h) -> p i h", i=NT), -1.0 / SCALE, None, ALU.mult),
                     ("forget_sum", l))
                dve.tensor_copy(o_tmp[:, 1:2], ones2[:, 0, 1:2]).then_inc(a_ready, 1)

                def epilogue_diff(g):
                    name = ("diff", l, "O", g)
                    ps = src(name)
                    ov = ps[:, :].rearrange("p (c i d) -> p c i d", c=2, i=NT)
                    inv = row_inv[:, 0:2, :]
                    link(dve.reciprocal(inv, row_sum[:, g % 2, 0:2, :]))
                    link(dve.tensor_scalar(inv[:, 1, :], inv[:, 1, :], lam[:, 3:4], None, ALU.mult))
                    t = o_tmp[:, :].rearrange("p (c i d) -> p c i d", c=2, i=NT)
                    free(dve.tensor_tensor(t, ov, inv.unsqueeze(3).broadcast_to([P, 2, NT, P]), ALU.mult), name)
                    tt(y_diff[:, :, g, :], t[:, 0], t[:, 1], ALU.add)
                    if g == 3:
                        tt(y_tmp, y_diff, y_diff, ALU.mult)
                        link(dve.tensor_reduce(h_ss, y_tmp, AX.X, ALU.add))
                        dve.tensor_scalar(h_ms, h_ss, 1.0 / P, EPS, ALU.mult, ALU.add).then_inc(h_ms_ready, 1)

                softmax_heads(("diff", l), 8, 2, epilogue_diff)

                def gated(name, s, g, weights):
                    ps = src(name)
                    ov = ps[:, :].rearrange("p (h i d) -> p h i d", h=4, i=NT)
                    lo = 512 * s + 256 * g
                    dst = mix[:, :, lo:lo + 256].rearrange("p i (h d) -> p h i d", d=HD)
                    gate = gates[:, :, s, 256 * g:256 * g + 256].rearrange("p i (h d) -> p h i d", d=HD)
                    if weights is None:
                        free(dve.tensor_tensor(dst, ov, gate, ALU.mult), name)
                        return
                    link(dve.reciprocal(row_inv, weights))
                    t = o_tmp[:, :].rearrange("p (h i d) -> p h i d", h=4, i=NT)
                    free(dve.tensor_tensor(t, ov, row_inv.unsqueeze(3).broadcast_to([P, 4, NT, HD]), ALU.mult), name)
                    tt(dst, t, gate, ALU.mult)

                softmax_heads(("fox", l), 8, 4, lambda g: gated(("fox", l, "O", g), 2, g, row_sum[:, g % 2]))

                def soft_plus(h):
                    dve.wait_ge(stick_log, 8 * l + h + 1)
                    ps = src(("stick", l, "Z", h))
                    free(dve.scalar_tensor_tensor(keep[:, h % 3, :], ps[:, 0:384], 0.0, softp[:, h % 2, :], ALU.max, ALU.add),
                         ("stick", l, "Z", h))

                for h in range(8):
                    soft_plus(h)
                    if h == 5:
                        gated(("stick", l, "O", 0), 1, 0, None)
                gated(("stick", l, "O", 1), 1, 1, None)
                dve.tensor_copy(o_tmp[:, 1:2], ones2[:, 0, 1:2]).then_inc(mix_ready, 1)
                evac_turned(("mixT2", l), hT, (1, 3, 5))
                dve.wait_ge(y_sumsq, 4 * (l + 1))
                yv = y_ss.rearrange("p (i a) -> p i a", a=2)
                tt(ss, yv[:, :, 0], yv[:, :, 1], ALU.add)
                dve.tensor_scalar(ms, ss, 1.0 / D, EPS, ALU.mult, ALU.add).then_inc(y_ms, 1)
                dve.wait_ge(y_rstd, l + 1)
                dve.wait_ge(post_loaded, 16 * (l + 1))
                for a in range(4):
                    i, half = divmod(a, 2)
                    ps = src(("out2", l, "acc", a))
                    free(dve.scalar_tensor_tensor(o_tmp[:, :], ps[:, :], rstd[:, i:i + 1], post_gain[:, half * 512:(half + 1) * 512],
                                                  ALU.mult, ALU.mult), ("out2", l, "acc", a))
                    xs = x_sb[:, i, half * 512:(half + 1) * 512]
                    ins = dve.tensor_tensor(xs, xs, o_tmp[:, :], ALU.add)
                    if a < 3:
                        link(ins)
                    else:
                        ins.then_inc(x_ready, 1)


PRM_LOADS = 11 + L
PRM_ROW_LOADS = 2 * L + 3

_INS = ['x', 'w_in', 'b_if', 'conv_qk', 'm_norm', 'moba_qk_norm', 'nsa_q_norm', 'nsa_k_norm', 'cmp_pe', 'cmp_w1',
        'cmp_w2', 'w_out', 'norm_mix', 'norm_ffn', 'w_ff1', 'w_ff2', 'w_in_2', 'forget_bias_2', 'diff_lambda_2',
        'diff_subln_2', 'w_out_2', 'pre_norm_2', 'post_norm_2']


def kernel(**inputs):
    import concourse.bacc as bacc
    from concourse.bass_utils import run_bass_kernel_spmd

    nc = bacc.Bacc("TRN2", target_bir_lowering=False, num_devices=1)
    table, selector = constants()
    arrays, args = {}, []
    for name, a in [(n, inputs[n]) for n in _INS] + [("consts", table), ("selector", selector)]:
        a = np.ascontiguousarray(a)
        arrays[f"in_{name}"] = a
        args.append(nc.dram_tensor(f"in_{name}", a.shape, mybir.dt.from_np(a.dtype), kind="ExternalInput").ap())
    args.append(nc.dram_tensor("out_x", (1, T, D), F32, kind="ExternalOutput").ap())
    hybrid_blocks(nc, *args)
    r = run_bass_kernel_spmd(nc, [arrays], core_ids=[0])
    return r.results[0]["out_x"]
```

```python
from contextlib import ExitStack

import numpy as np

import concourse.bass as bass
from concourse import mybir

F32 = mybir.dt.float32
F32R = mybir.dt.float32r
BF16 = mybir.dt.bfloat16
ALU = mybir.AluOpType
ACT = mybir.ActivationFunctionType
AX = mybir.AxisListType
LOG_EXP = "natural_log_exp_and_others"

P = 128
T = 256
NT = T // P
D = 1024
KD = D // P
L = 2
DFF = 4096
HD = 64
EPS = 1e-6
NEG = -1e30
SCALE = HD ** -0.5
M_SCALE = 128 ** -0.5
MH = 4
NC_CMP = 15
COLS1 = 3476
COLS2 = 6152
REST0 = 2048
RESTW = COLS1 - REST0
NVEC = 22
KMIX2 = 12
SLOTS = 4
UNIT = 1024
AHEAD = 3
ARENA = 10240
PROJ1 = [4, 5, 6, 0, 1, 2, 3]
PROJ2 = list(range(12))
FEATURE1 = (0, 1)
FEATURE2 = (4, 5, 8, 9)
LAM_INIT = [0.8 - 0.6 * float(np.exp(-0.3 * l)) for l in range(L)]

C_ID, C_CAUSAL, C_CHUNK, C_STRICT, C_LE, C_RTRI, C_ONES, C_NONES = (128 * n for n in range(8))
C_COS = 1024
C_SIN = C_COS + NT * 8
C_CNEG = C_SIN + NT * 8
C_C01 = C_CNEG + NT * NC_CMP
C_END = C_C01 + NT * NC_CMP


def constants():
    c = np.zeros((P, C_END), np.float32)
    a, b = np.arange(P)[:, None], np.arange(P)[None, :]
    c[:, C_ID:C_ID + P] = a == b
    c[:, C_CAUSAL:C_CAUSAL + P] = np.where(b > a, np.float32(NEG), 0)
    c[:, C_CHUNK:C_CHUNK + P] = np.where(b // 64 > a // 64, np.float32(NEG), 0)
    c[:, C_STRICT:C_STRICT + P] = np.where(a >= b, np.float32(NEG), 0)
    c[:, C_LE:C_LE + P] = a <= b
    c[:, C_RTRI:C_RTRI + P] = np.where(a >= b, -1, 0)
    c[:, C_ONES:C_ONES + P] = 1
    c[:, C_NONES:C_NONES + P] = -1
    freq = np.exp(np.float32(-np.log(500000.0)) * np.arange(8, dtype=np.float32) * np.float32(2.0 / 16))
    tok = (np.arange(NT)[None, :] * P + np.arange(P)[:, None]).astype(np.float32)
    ang = (tok[:, :, None] * freq.astype(np.float32)).astype(np.float32)
    c[:, C_COS:C_COS + NT * 8] = np.cos(ang).reshape(P, -1)
    c[:, C_SIN:C_SIN + NT * 8] = np.sin(ang).reshape(P, -1)
    seen = (np.arange(NC_CMP) * 16 + 31)[None, None, :] <= tok[:, :, None]
    c[:, C_CNEG:C_CNEG + NT * NC_CMP] = np.where(seen, 0, np.float32(NEG)).reshape(P, -1)
    c[:, C_C01:C_C01 + NT * NC_CMP] = seen.reshape(P, -1)
    sel = np.zeros((8, 8 * P), np.float32)
    for h in range(8):
        sel[h, h * P:(h + 1) * P] = 1
    return c, sel


def hybrid_blocks(nc, x, w_in, b_if, conv_qk, m_norm, moba_qk_norm, nsa_q_norm, nsa_k_norm, cmp_pe,
                  cmp_w1, cmp_w2, w_out, norm_mix, norm_ffn, w_ff1, w_ff2, w_in_2, forget_bias_2,
                  diff_lambda_2, diff_subln_2, w_out_2, pre_norm_2, post_norm_2, consts, selector, out):
    bank_of, nth, at_unit, uses = {}, {}, {}, [0] * 8
    units, unit_no = [], {}
    counts = {"unit": 0}
    timeline = [[[] for _ in range(L)] for _ in range(2)]
    steps = None

    def use(key, bank):
        bank_of[key], nth[key] = bank, uses[bank]
        uses[bank] += 1
        at_unit[key] = len(units)

    def done(key):
        at_unit[key] = len(units)

    def unit(key, src, split=True, closes=None, lo_on="vector"):
        if closes is None:
            counts["unit"] += 1
        unit_no[key] = len(units)
        units.append(dict(key=key, src=src, split=split, closes=closes, n_done=counts["unit"], lo_on=lo_on))
        steps.append(key)

    def step(*key):
        steps.append(key)

    def norm_steps(n):
        for i in range(NT):
            for u in range(2):
                use(("norm", n, i, u), 4 + 2 * i + u)
                step("norm", n, i, u)

    def proj_unit(b, l, w, j, bp, q, cols, lo_on):
        n = min(512, cols - 512 * j)
        src = w[256 * q:256 * q + 256, 512 * j:512 * j + n].rearrange("(k p) c -> p k c", p=P)
        for i in range(2):
            if q == 0:
                use(("proj", b, l, j, i), 2 * (bp % 2) + i)
        unit(("proj", b, l, j, q), src, closes=("proj", b, l, j, 1) if q == 3 else None, lo_on=lo_on)
        if q == 3:
            done(("proj", b, l, j, 0))
            done(("proj", b, l, j, 1))

    def out_unit(name, w, f, first, last):
        if first:
            for a in range(4):
                use((*name, "acc", a), a)
        unit((*name, "unit", f), w[P * f:P * f + P, :].unsqueeze(1).rearrange("p k c -> p k c"), closes=(*name, "acc", 3) if last else None)
        if last:
            for a in range(4):
                done((*name, "acc", a))

    def head_steps(name, h, stage, groups_of):
        if stage == "S":
            use((*name, "S", h), 4 + h % 2)
        elif stage == "T":
            use((*name, "T", h), 6)
        else:
            g, r = divmod(h, groups_of)
            if r == 0:
                use((*name, "O", g), 7)
            if r == groups_of - 1:
                done((*name, "O", g))
        step(*name, stage, h)

    def stick_steps(l, h, stage):
        if stage == "Z":
            use(("stick", l, "Z", h), 4 + h % 3)
        elif stage == "R":
            use(("stick", l, "R", h), 4 + h % 3)
        else:
            if h % 4 == 0:
                use(("stick", l, "O", h // 4), 7)
            if h % 4 == 3:
                done(("stick", l, "O", h // 4))
        step("stick", l, stage, h)

    def single(bank, *key):
        use(key, bank)
        step(*key)

    use(("params",), 4)
    for l in range(L):
        steps = timeline[0][l]
        norm_steps(2 * l)
        start = [12, 13, 14, 15] + [14 + h for h in range(4, 12)]

        def heads1(p):
            for stage, lag in (("V", 3), ("T", 2), ("S", 0)):
                for h in range(12):
                    if start[h] + lag == p:
                        head_steps(("att1", l), h, stage, 4)

        def m_scores(h):
            single(2, "mlstm", l, "S", h)

        def m_values(h):
            single(3, "mlstm", l, "O", h)

        for bp, j in enumerate(PROJ1):
            for q in range(4):
                p = 4 * bp + q
                proj_unit(0, l, w_in[l], j, bp, q, COLS1, "pool" if p % 3 == 2 and p >= 8 else "vector")
                if q == 3:
                    step("evac", 0, l, j)
                heads1(p)
                if p == 3:
                    step("gate_log", l)
                if p == 5:
                    single(0, "gate_sum", l)
                if p == 7:
                    step("vec_a", l, 0)
                if p == 8:
                    single(2, "gate_row", l)
                    step("vec_a", l, 1)
                if p == 9:
                    step("vec_a", l, 2)
                if p == 11:
                    single(4, "turn", l, 0)
                    single(5, "turn", l, 1)
                    step("vec_b", l, 0)
                if p == 12:
                    single(0, "m_col", l)
                    single(1, "m_rows", l, 0)
                    step("vec_b", l, 1)
                if p == 13:
                    single(0, "m_rows", l, 1)
                    step("vec_b", l, 2)
                if p == 14:
                    step("vec_b", l, 3)
                if p == 16:
                    single(2, "turn", l, 2)
                    single(3, "turn", l, 3)
                    step("conv", l, 0)
                if p == 17:
                    single(2, "turn", l, 4)
                    single(3, "turn", l, 5)
                    step("conv", l, 1)
                if p == 18:
                    use(("hidden", l), 2)
                    for v in range(2):
                        w1 = cmp_w1[l, v].rearrange("(a p) e -> p a e", p=P)
                        for half in range(2):
                            unit(("cmp", l, v, half), w1[:, 8 * half:8 * half + 8, :], split=False,
                                 closes=("hidden", l) if v and half else None)
                    done(("hidden", l))
                    step("hidden", l)
                if p == 20:
                    single(0, "cmp_kv", l)
                    step("conv", l, 2)
                if p == 21:
                    single(1, "cmp_kT", l)
                    step("conv", l, 3)
                if p == 22:
                    single(0, "cmp_s", l, 0)
                    single(1, "cmp_s", l, 1)
                    step("cmp_soft", l)
                    step("conv_silu", l)
                if p == 24:
                    m_scores(0)
                    single(3, "cmp_pT", l)
                if p == 25:
                    single(3, "cmp_o", l)
                    m_scores(1)
                if p == 26:
                    m_values(0)
                    m_scores(2)
                if p == 27:
                    m_values(1)
                    m_scores(3)
        heads1(28)
        m_values(2)
        m_values(3)
        for i in range(NT):
            single(4 + i, "mix_turn", 0, l, 1, i)
        step("mlstm_end", l)
        for f in (4, 5, 6, 7):
            out_unit(("out", 0, l), w_out[l], f, f == 4, False)
        for i in range(NT):
            single(6 + i, "mix_turn", 0, l, 0, i)
        for f in (0, 1, 2, 3):
            out_unit(("out", 0, l), w_out[l], f, False, f == 3)
        step("residual", ("out", 0, l))
        norm_steps(2 * l + 1)

        def ff1(t):
            for i in range(2):
                use(("ff1", l, t, i), 4 + 2 * (t % 2) + i)
            for q in range(4):
                src = w_ff1[l][256 * q:256 * q + 256, 512 * t:512 * t + 512].rearrange("(k p) c -> p k c", p=P)
                unit(("ff1", l, t, q), src, closes=("ff1", l, t, 1) if q == 3 else None)
            for i in range(2):
                done(("ff1", l, t, i))
            step("square", l, t)

        def ff2(t):
            for f in range(4 * t, 4 * t + 4):
                out_unit(("ff2", l), w_ff2[l], f, f == 0, f == 31)

        ff1(0)
        for t in range(1, 8):
            ff1(t)
            ff2(t - 1)
        ff2(7)
        step("residual", ("ff2", l))

    for l in range(L):
        steps = timeline[1][l]
        norm_steps(4 + l)

        def side2(p):
            for name, first, sp, groups_of in ((("diff", l), 12, 1.5, 2), (("fox", l), 41, 1.25, 4)):
                for stage, lag in (("V", 3), ("T", 2), ("S", 0)):
                    for h in range(8):
                        if int(first + sp * h) + lag == p:
                            head_steps(name, h, stage, groups_of)
            for stage, lag in (("V", 3), ("R", 2), ("Z", 0)):
                for h in range(8):
                    if int(26 + 1.5 * h) + lag == p:
                        stick_steps(l, h, stage)
            if p == 0:
                single(2, "forget_f", l)
                step("forget_log", l)
            if p == 5:
                single(0, "forget_sum", l)
            if p == 8:
                step("rope2", l)
                single(2, "forget_row", l)
            if p in (10, 11):
                for u in (0, 1):
                    single(4 + 2 * (p - 10) + u, "turn2", l, 2 * (p - 10) + u)
            if p == 44:
                for i in range(NT):
                    single(i, "mix_turn", 1, l, 0, i)
            if p == 46:
                for i in range(NT):
                    single(i, "mix_turn", 1, l, 1, i)
            if p == 55:
                for i in range(NT):
                    single(4 + i, "mix_turn", 1, l, 2, i)

        for bp, j in enumerate(PROJ2):
            for q in range(4):
                proj_unit(1, l, w_in_2[l], j, bp, q, 6144, "vector")
                if q == 3:
                    step("evac", 1, l, j)
                side2(4 * bp + q)
        for f in range(KMIX2):
            out_unit(("out", 1, l), w_out_2[l], f, f == 0, f == KMIX2 - 1)
            side2(48 + f)
        step("post_norm", l)

    seen = {"vector": 0, "pool": 0, "hi": 0}
    for u in units:
        if u["split"]:
            seen["hi"] += 1
            seen[u["lo_on"]] += 1
            u["n_hi"], u["n_lo"] = seen["hi"], seen[u["lo_on"]]

    with ExitStack() as ctx:
        def sb(name, shape, dt=F32):
            return ctx.enter_context(nc.sbuf_tensor(name, shape, dt))

        def sem(name):
            return ctx.enter_context(nc.semaphore(name))

        bank = [ctx.enter_context(nc.psum_tensor(f"bank{b}", [P, 512], F32)) for b in range(8)]
        bank_filled = [sem(f"bank_filled{b}") for b in range(8)]
        bank_freed = [sem(f"bank_freed{b}") for b in range(8)]

        raw = sb("raw", [P, SLOTS, UNIT])
        w_hi = sb("w_hi", [P, SLOTS, UNIT], F32R)
        w_lo = sb("w_lo", [P, SLOTS, UNIT], F32R)
        h_hi = sb("h_hi", [P, KD, T], F32R)
        h_lo = sb("h_lo", [P, KD, T], F32R)
        const = sb("const", [P, C_END])
        sel = sb("sel", [8, 8 * P])
        masks = sb("masks", [P, 4 * P], BF16)
        x_sb = sb("x_sb", [P, NT, D])
        xn = sb("xn", [P, NT, D])
        mix = sb("mix", [P, NT, KMIX2 * P])
        gain = sb("gain", [P, D])
        arena = sb("arena", [P, ARENA])
        arena_at = nc.sbuf_base - 4 * ARENA
        vecs = sb("vecs", [P, 2 * 3072])
        vecs_at = nc.sbuf_base - 4 * 2 * 3072
        vec = vecs[:, 0:3072].rearrange("p (i s d) -> p i s d", i=NT, d=HD)
        vecT = vecs[:, 3072:6144].rearrange("p (s t) -> p s t", t=T)
        probs = sb("probs", [P, 3, 384])
        probsT = sb("probsT", [P, 2, 384])
        prm = sb("prm", [P, 128])
        bif = sb("bif", [P, L, 8])
        g_vec = sb("g_vec", [P, L, 6, HD])
        m_gain = sb("m_gain", [P, L, 512])
        w2c = sb("w2c", [P, L, 2, HD])
        ff_w = sb("ff_w", [P, L * KD * 8])
        ff_hi = sb("ff_hi", [P, L, KD, 8], F32R)
        ff_lo = sb("ff_lo", [P, L, KD, 8], F32R)
        f_bias = sb("f_bias", [P, L, 8])
        lam_v = sb("lam_v", [P, L, 4, HD])
        sub_gain = sb("sub_gain", [P, L, P])
        blocksT = sb("blocksT", [P, 2, 16, NC_CMP])
        kc_n = sb("kc_n", [NC_CMP, 2, HD])
        kcT = sb("kcT", [P, NC_CMP])
        vc_diag = sb("vc_diag", [P, 4, HD])
        p_cmp = sb("p_cmp", [P, NT, 4, 32])
        hid = sb("hid", [P, 2, 2, 16])
        small = sb("small", [P, 512])
        rows = sb("rows", [8, 3, T])
        o_tmp = sb("o_tmp", [P, 512])
        flag = sb("flag", [P, 2])
        sq_out = sb("sq_out", [P, P])
        at = [0]

        def shaped(a, shape):
            if len(shape) == 1:
                return a
            names = "abcd"[:len(shape)]
            return a.rearrange(f"p ({' '.join(names)}) -> p {' '.join(names)}", **{names[k]: shape[k] for k in range(1, len(shape))})

        def few(*shape):
            n = int(np.prod(shape))
            a = small[:, at[0]:at[0] + n]
            at[0] += n
            return shaped(a, shape)

        def part(lo, *shape):
            return shaped(arena[:, lo:lo + int(np.prod(shape))], shape)

        def exact(name, base, lo, *shape):
            return nc.alloc_sbuf_tensor_at(name, [P, *shape], F32R, offset=base + 4 * lo)

        ss, ms, rstd = few(NT), few(NT), few(NT)
        half_neg = few(8)
        v_ss, v_ms, v_r, v_t = few(NT, NVEC), few(NT, NVEC), few(NT, NVEC), few(NT, NVEC)
        gif, g_e, g_lf, g_F, g_a, m_tok, e_m, m_den = (few(NT, 8) for _ in range(8))
        n_gate = few(NT, 12)
        row_nb, row_mx = few(2, NT), few(2, NT)
        row_sum, row_inv = few(2, 4, NT), few(4, NT)
        kc_s = few(4)
        c_mx, c_sum = few(NT, 4), few(NT, 4)
        h_ss, h_ms, h_rs = few(NT, MH), few(NT, MH), few(NT, MH)
        lam, y_ss = few(4), few(4)

        rest = part(0, NT, RESTW)
        squares = part(2856, NT, NVEC, HD)
        conv_in = part(2856, KD, T + 3)
        h_num = part(2856, NT, MH, 129)
        m_probs = part(3888, 2, 384)
        p_cmpT = part(4928, NT, P)
        intra = part(5672, MH, 384)
        o_gate = part(7208, NT, MH, P)
        v_aug = part(8232, NT, MH, 130)
        m_qk = xn[:, :, :].rearrange("p i (c t) -> p (i c) t", t=T)
        u_hi = [exact(f"u_hi{b}", arena_at, 2048 * b, 4, T) for b in range(2)]
        u_lo = [exact(f"u_lo{b}", arena_at, 2048 * b + 1024, 4, T) for b in range(2)]
        u_full = part(4096, 2, 512)
        relu = part(5120, 2, 512)
        values = part(0, 3, NT, 512)
        gates = part(3072, NT, 3, 512)
        featT = part(6144, 16, T)
        y_diff = xn[:, :, 0:512].rearrange("p i (h d) -> p i h d", d=P)
        y_tmp = xn[:, :, 512:1024].rearrange("p i (h d) -> p i h d", d=P)
        mixT_hi = [exact("mixT_hi0", vecs_at, 3072, 4, T), exact("mixT_hi1", arena_at, 6144, 4, T), h_hi]
        mixT_lo = [exact("mixT_lo0", vecs_at, 4096, 4, T), exact("mixT_lo1", arena_at, 7168, 4, T), h_lo]
        softp = vecs[:, 3072 + 2048:3072 + 2048 + 768].rearrange("p (b t) -> p b t", b=2)
        keep = vecs[:, 0:3 * 384].rearrange("p (b t) -> p b t", b=3)
        post_gain = vecs[:, 3 * 384:3 * 384 + D]
        prm_rows = o_tmp[:, 0:2 * P]

        ident = const[:, C_ID:C_ID + P]
        ident_b, causal_b, chunk_b, strict_b = (masks[:, n * P:(n + 1) * P] for n in range(4))

        def conv_col(l, tap, c):
            n = (l * 4 + tap) * 8 + c
            return prm[:, n:n + 1]

        raw_arrived = [sem(f"raw_arrived{s}") for s in range(SLOTS)]
        unit_done = sem("unit_done")
        hi_ready = sem("hi_ready")
        lo_ready = {"vector": sem("lo_ready_vector"), "pool": sem("lo_ready_pool")}
        x_loaded, prm_loaded, prm_rows_loaded, post_loaded = sem("x_loaded"), sem("prm_loaded"), sem("prm_rows_loaded"), sem("post_loaded")
        const_loaded, gain_loaded = sem("const_loaded"), sem("gain_loaded")
        prepared, half_neg_set = sem("prepared"), sem("half_neg_set")
        out_stored = sem("out_stored")
        vector_step, scalar_step, pool_step = sem("vector_step"), sem("scalar_step"), sem("pool_step")
        x_tile_ready, sumsq_ready, rstd_ready, xn_ready = sem("x_tile_ready"), sem("sumsq_ready"), sem("rstd_ready"), sem("xn_ready")
        turned_hi = sem("turned_hi")
        gate_abs, gate_log = sem("gate_abs"), sem("gate_log")
        squared, vec_ms, vec_rstd, vec_ready = sem("squared"), sem("vec_ms"), sem("vec_rstd"), sem("vec_ready")
        logf_ready, a_ready, m_ready = sem("logf_ready"), sem("a_ready"), sem("m_ready")
        conv_done, conv_silu = sem("conv_done"), sem("conv_silu")
        exponent_ready, intra_exp, intra_masked = sem("exponent_ready"), sem("intra_exp"), sem("intra_masked")
        m_col_ready, stabilizer = sem("m_col_ready"), sem("stabilizer")
        blocks_ready, hid_exp, hid_ready = sem("blocks_ready"), sem("hid_exp"), sem("hid_ready")
        kc_ms, kc_rstd, kc_ready = sem("kc_ms"), sem("kc_rstd"), sem("kc_ready")
        cmp_shifted, cmp_exp, cmp_ready = sem("cmp_shifted"), sem("cmp_exp"), sem("cmp_ready")
        nsa_gated, o_gained = sem("nsa_gated"), sem("o_gained")
        max_ready = sem("max_ready")
        h_squared, h_ms_ready, h_rstd_ready = sem("h_squared"), sem("h_ms_ready"), sem("h_rstd_ready")
        diff_mixed = sem("diff_mixed")
        mix_ready = sem("mix_ready")
        relu_ready, u_full_ready, u_hi_ready, u_ready = sem("relu_ready"), sem("u_full_ready"), sem("u_hi_ready"), sem("u_ready")
        lam_dots, lam_exp = sem("lam_dots"), sem("lam_exp")
        stick_log = sem("stick_log")
        y_sumsq, y_ms, y_rstd = sem("y_sumsq"), sem("y_ms"), sem("y_rstd")

        def filled(eng, key):
            eng.wait_ge(bank_filled[bank_of[key]], nth[key] + 1)

        def drained(eng, key):
            eng.wait_ge(bank_freed[bank_of[key]], nth[key] + 1)

        def released(eng, n):
            u = units[n]
            if u["closes"] is None:
                eng.wait_ge(unit_done, u["n_done"])
            else:
                filled(eng, u["closes"])

        def slot(store, u):
            n, k, c = unit_no[u["key"]], u["src"].shape[1], u["src"].shape[2]
            return store[:, n % SLOTS, 0:k * c].rearrange("p (k c) -> p k c", c=c)

        def heads_of(kind, l):
            def pair(t, p, h):
                b = HD * (h % 2)
                return t[b:b + HD, p, :]

            if kind == "att1":
                def col(c):
                    return lambda i: rest[:, i, c:c + HD]
                moba = [(pair(vecT, h // 2, h), pair(vecT, 2 + h // 2, h), causal_b, col(520 + HD * h), HD, None) for h in range(4)]
                nsa = [(pair(vecT, 4 + h // 2, h), pair(vecT, p, h), causal_b, col(c), HD, None)
                       for p, c in ((6, 1224), (7, 1352)) for h in range(4)]
                return moba + nsa
            if kind == "diff":
                return [(pair(vecT, h // 2, h), pair(vecT, 4 + h // 2, h), chunk_b,
                         (lambda c: lambda i: values[:, 0, i, c:c + P])(P * (h // 2)), P, None) for h in range(8)]
            return [(pair(featT, 8 + h // 2, h), pair(featT, 12 + h // 2, h), causal_b,
                     (lambda c: lambda i: values[:, 2, i, c:c + HD])(HD * h), HD, h) for h in range(8)]

        GROUPS = {"att1": 4, "diff": 2, "fox": 4}

        block = ctx.enter_context(nc.Block())

        @block.sync
        def _(sp):
            sp.dma_start(x_sb[:, :, :], x.rearrange("b (i p) d -> p (b i) d", p=P)).then_inc(x_loaded, 16)
            for n, u in enumerate(units):
                if n >= SLOTS:
                    old = units[n - SLOTS]
                    if old["split"]:
                        sp.wait_ge(lo_ready[old["lo_on"]], old["n_lo"])
                    else:
                        released(sp, n - SLOTS)
                sp.dma_start(slot(raw, u), u["src"]).then_inc(raw_arrived[n % SLOTS], 16)
            sp.wait_ge(x_tile_ready, 2 * 3 * L)
            sp.dma_start(out.rearrange("b (i p) d -> p (b i) d", p=P), x_sb[:, :, :]).then_inc(out_stored, 16)
            sp.wait_ge(out_stored, 16)

        @block.tensor
        def _(pe):
            def open_bank(key):
                if nth[key]:
                    pe.wait_ge(bank_freed[bank_of[key]], nth[key])
                return bank[bank_of[key]]

            def close(mm, key):
                mm.then_inc(bank_filled[bank_of[key]], 1)

            def weights(key):
                u = units[unit_no[key]]
                pe.wait_ge(lo_ready[u["lo_on"]], u["n_lo"])
                return slot(w_hi, u), slot(w_lo, u)

            def finish_unit(mm, key):
                if units[unit_no[key]]["closes"] is None:
                    mm.then_inc(unit_done, 1)
                else:
                    close(mm, units[unit_no[key]]["closes"])

            def exact_product(out_ap, stat, mov, start, stop, **kw):
                (s_hi, s_lo), (m_hi, m_lo) = stat, mov
                pe.matmul(out_ap, s_hi, m_hi, start=start, stop=False, **kw)
                pe.matmul(out_ap, s_hi, m_lo, start=False, stop=False, **kw)
                return pe.matmul(out_ap, s_lo, m_hi, start=False, stop=stop, **kw)

            def features_there(n):
                def there(i, k):
                    drained(pe, ("norm", n, i, k // 4))
                return there

            def token_unit(key, uses_of, q, there):
                hi, lo = weights(key)
                n = hi.shape[2]
                for i in range(NT):
                    ps = open_bank(uses_of[i]) if q == 0 else bank[bank_of[uses_of[i]]]
                    for kk in range(2):
                        k = 2 * q + kk
                        if there and k % 4 == 0:
                            there(i, k)
                        t = slice(i * P, (i + 1) * P)
                        mm = exact_product(ps[:, 0:n], (h_hi[:, k, t], h_lo[:, k, t]), (hi[:, kk, :], lo[:, kk, :]),
                                           k == 0, k == KD - 1)
                    if q == 3 and i == 0:
                        close(mm, uses_of[0])
                finish_unit(mm, key)

            def feature_unit(key, uses_of, q, there):
                hi, lo = weights(key)
                for c in range(4):
                    ps = open_bank(uses_of[c // 2]) if q == 0 and c % 2 == 0 else bank[bank_of[uses_of[c // 2]]]
                    for kk in range(2):
                        k = 2 * q + kk
                        if there and k % 4 == 0 and c == 0:
                            there(0, k)
                            there(1, k)
                        f = slice(c * P, (c + 1) * P)
                        mm = exact_product(ps[:, (c % 2) * T:(c % 2 + 1) * T], (hi[:, kk, f], lo[:, kk, f]),
                                           (h_hi[:, k, :], h_lo[:, k, :]), k == 0 and c % 2 == 0, k == KD - 1,
                                           skip_group_check=True)
                    if q == 3 and c == 1:
                        close(mm, uses_of[0])
                finish_unit(mm, key)

            def out_unit_products(key, name, hi_f, lo_f, first, last):
                hi, lo = weights(key)
                for a in range(4):
                    i, half = divmod(a, 2)
                    ps = open_bank((*name, "acc", a)) if first else bank[bank_of[(*name, "acc", a)]]
                    t, c = slice(i * P, (i + 1) * P), slice(half * 512, (half + 1) * 512)
                    mm = exact_product(ps[:, :], (hi_f[:, t], lo_f[:, t]), (hi[:, 0, c], lo[:, 0, c]), first, last)
                    if last and a < 3:
                        close(mm, (*name, "acc", a))
                finish_unit(mm, key)

            def turn(key, src, chunks):
                ps = open_bank(key)
                for n, (k, i) in enumerate(chunks):
                    mm = pe.transpose(ps[:, n * P:(n + 1) * P], src[:, i, k * P:(k + 1) * P], ident)
                close(mm, key)

            def running_sum(key, src, n):
                ps = open_bank(key)
                le, ones = const[:, C_LE:C_LE + P], const[:, C_ONES:C_ONES + P]
                pe.matmul(ps[:, 0:n], le, src[:, 0, 0:n], start=True, stop=True)
                pe.matmul(ps[:, n:2 * n], ones, src[:, 0, 0:n], start=True, stop=False)
                close(pe.matmul(ps[:, n:2 * n], le, src[:, 1, 0:n], start=False, stop=True), key)

            def head_inputs(kind, l, stage, h):
                both = range(NT)
                inputs = {
                    ("att1", "S", 0): [("turn", l, 0), ("turn", l, 1)],
                    ("att1", "S", 4): [("turn", l, 2), ("turn", l, 3)],
                    ("att1", "V", 0): [("proj", 0, l, j, i) for j in (5, 6) for i in both],
                    ("diff", "S", 0): [("turn2", l, u) for u in range(4)],
                    ("diff", "V", 0): [("proj", 1, l, 2, i) for i in both],
                    ("stick", "Z", 0): [("proj", 1, l, j, i) for j in (4, 5) for i in both],
                    ("stick", "V", 0): [("proj", 1, l, 6, i) for i in both],
                    ("fox", "S", 0): [("forget_row", l)] + [("proj", 1, l, j, i) for j in (8, 9) for i in both],
                    ("fox", "V", 0): [("proj", 1, l, 10, i) for i in both]}
                for key in inputs.get((kind, stage, h), []):
                    drained(pe, key)

            def head_stage(kind, l, stage, h):
                name = (kind, l)
                head_inputs(kind, l, stage, h)
                q, k, mask, value, width, extra = heads_of(kind, l)[h]
                if stage == "S":
                    ps = open_bank((*name, "S", h))
                    for lo, i in ((0, 0), (P, 1)):
                        cols = (i + 1) * P
                        pe.matmul(ps[:, lo:lo + cols], q[:, i * P:(i + 1) * P], k[:, 0:cols], start=True, stop=False)
                        if extra is not None:
                            pe.matmul(ps[:, lo:lo + cols], sel[0:8, extra * P:(extra + 1) * P],
                                      rows[0:8, 0, 0:cols], start=False, stop=False)
                        mm = pe.matmul(ps[:, lo + cols - P:lo + cols], ident_b, mask, start=False, stop=True)
                    close(mm, (*name, "S", h))
                elif stage == "T":
                    drained(pe, (*name, "S", h))
                    ps = open_bank((*name, "T", h))
                    for b in range(3):
                        mm = pe.transpose(ps[:, b * P:(b + 1) * P], probs[:, h % 3, b * P:(b + 1) * P], ident)
                    close(mm, (*name, "T", h))
                else:
                    g, r = divmod(h, GROUPS[kind])
                    drained(pe, (*name, "T", h))
                    ps = open_bank((*name, "O", g)) if r == 0 else bank[bank_of[(*name, "O", g)]]
                    lo = r * 2 * width
                    pe.matmul(ps[:, lo:lo + width], probsT[:, h % 2, 0:P], value(0), start=True, stop=True)
                    pe.matmul(ps[:, lo + width:lo + 2 * width], probsT[:, h % 2, P:2 * P], value(0), start=True, stop=False)
                    mm = pe.matmul(ps[:, lo + width:lo + 2 * width], probsT[:, h % 2, 2 * P:3 * P], value(1), start=False, stop=True)
                    if r == GROUPS[kind] - 1:
                        close(mm, (*name, "O", g))

            pe.wait_ge(const_loaded, 32)
            pe.wait_ge(prm_rows_loaded, 16 * PRM_ROW_LOADS)
            ps = open_bank(("params",))
            pe.transpose(ps[:, 0:64], prm_rows[0:64, 0:P], const[0:64, C_ID:C_ID + 64])
            close(pe.transpose(ps[:, 64:128], prm_rows[0:64, P:2 * P], const[0:64, C_ID:C_ID + 64]), ("params",))

            for l in range(L):
                n0 = 2 * l
                for s in timeline[0][l]:
                    kind = s[0]
                    if kind == "norm":
                        _, n, i, u = s
                        pe.wait_ge(xn_ready, NT * n + i + 1)
                        turn(s, xn, [(4 * u + c, i) for c in range(4)])
                    elif kind == "proj":
                        _, b, _, j, q = s
                        both = [("proj", b, l, j, i) for i in range(2)]
                        there = features_there(n0) if j == PROJ1[0] else None
                        (feature_unit if j in FEATURE1 else token_unit)(s, both, q, there)
                    elif kind == "gate_sum":
                        pe.wait_ge(logf_ready, l + 1)
                        running_sum(s, g_lf, 4)
                    elif kind == "gate_row":
                        pe.wait_ge(a_ready, l + 1)
                        ps = open_bank(s)
                        for i in range(NT):
                            mm = pe.transpose(ps[0:4, i * P:(i + 1) * P], g_a[:, i, 0:4], ident)
                        close(mm, s)
                    elif kind == "turn":
                        pe.wait_ge(vec_ready, 2 * l + (1 if s[2] < 2 else 2))
                        turn(s, vec[:, :, :, :].rearrange("p i s d -> p i (s d)"),
                             [(2 * s[2] + c, i) for c in range(2) for i in range(NT)])
                    elif kind == "m_col":
                        pe.wait_ge(m_ready, l + 1)
                        ps = open_bank(s)
                        for i in range(NT):
                            mm = pe.transpose(ps[:, 4 * i:4 * i + 4], rows[0:4, 1, i * P:(i + 1) * P], ident[0:4, 0:4])
                        close(mm, s)
                    elif kind == "m_rows":
                        ps = open_bank(s)
                        for c in range(2):
                            h = 2 * s[2] + c
                            mm = pe.matmul(ps[:, c * T:(c + 1) * T], sel[0:4, h * P:(h + 1) * P], rows[0:4, 1, :],
                                           start=True, stop=True)
                        close(mm, s)
                    elif kind == "cmp":
                        _, _, v, half = s
                        u = units[unit_no[s]]
                        if v == 0 and half == 0:
                            ps = open_bank(("hidden", l))
                            pe.wait_ge(blocks_ready, l + 1)
                        pe.wait_ge(raw_arrived[unit_no[s] % SLOTS], 16 * (unit_no[s] // SLOTS + 1))
                        w = slot(raw, u)
                        for a in range(8):
                            mm = pe.matmul(ps[:, 16 * v:16 * v + NC_CMP], w[:, a, :], blocksT[:, v, 8 * half + a, :],
                                           start=(half == 0 and a == 0), stop=(half == 1 and a == 7))
                        finish_unit(mm, s)
                    elif kind == "cmp_kv":
                        ps = open_bank(s)
                        pe.wait_ge(hid_ready, l + 1)
                        for v in range(2):
                            mm = pe.matmul(ps[0:NC_CMP, v * HD:(v + 1) * HD], hid[:, 1, v, 0:NC_CMP], w2c[:, l, v, :],
                                           start=True, stop=True)
                        close(mm, s)
                    elif kind == "cmp_kT":
                        ps = open_bank(s)
                        pe.wait_ge(kc_ready, l + 1)
                        close(pe.transpose(ps[:, 0:NC_CMP], kc_n[:, :, :].rearrange("c r d -> c (r d)"),
                                           ident[0:NC_CMP, 0:NC_CMP]), s)
                    elif kind == "cmp_s":
                        if s[2] == 0:
                            drained(pe, ("turn", l, 5))
                            drained(pe, ("cmp_kT", l))
                        ps = open_bank(s)
                        b = HD * s[2]
                        for i in range(NT):
                            for h in range(2):
                                lo = (i * 2 + h) * 16
                                mm = pe.matmul(ps[:, lo:lo + NC_CMP], vecT[b:b + HD, 10 + h, i * P:(i + 1) * P],
                                               kcT[b:b + HD, :], start=True, stop=True)
                        close(mm, s)
                    elif kind == "cmp_pT":
                        ps = open_bank(s)
                        pe.wait_ge(cmp_ready, l + 1)
                        for i in range(NT):
                            mm = pe.transpose(ps[:, i * P:(i + 1) * P], p_cmp[:, i, :, :].rearrange("p h c -> p (h c)"), ident)
                        close(mm, s)
                    elif kind == "cmp_o":
                        drained(pe, ("cmp_pT", l))
                        ps = open_bank(s)
                        for i in range(NT):
                            mm = pe.matmul(ps[:, i * T:(i + 1) * T], p_cmpT[:, i, :],
                                           vc_diag[:, :, :].rearrange("p h d -> p (h d)"), start=True, stop=True)
                        close(mm, s)
                    elif kind == "mlstm" and s[2] == "S":
                        h = s[3]
                        if h == 0:
                            pe.wait_ge(conv_silu, l + 1)
                        q, k = m_qk[:, h, :], m_qk[:, MH + h, :]
                        ps = open_bank(s)
                        pe.matmul(ps[:, 0:T], k[:, 0:P], q, start=True, stop=True)
                        close(pe.matmul(ps[:, T:T + P], k[:, P:T], q[:, P:T], start=True, stop=True), s)
                    elif kind == "mlstm":
                        h = s[3]
                        drained(pe, ("mlstm", l, "S", h))
                        if h == 0:
                            drained(pe, ("proj", 0, l, 2, 0))
                            drained(pe, ("proj", 0, l, 2, 1))
                        ps = open_bank(s)
                        p = m_probs[:, h % 2, :]
                        pe.matmul(ps[:, 0:129], p[:, 0:P], v_aug[:, 0, h, 0:129], start=True, stop=True)
                        pe.matmul(ps[:, 129:258], p[:, P:T], v_aug[:, 0, h, 0:129], start=True, stop=False)
                        close(pe.matmul(ps[:, 129:258], p[:, T:T + P], v_aug[:, 1, h, 0:129], start=False, stop=True), s)
                    elif kind == "att1":
                        head_stage(kind, l, s[2], s[3])
                    elif kind == "mix_turn":
                        _, _, _, g, i = s
                        pe.wait_ge(mix_ready, 2 * l + (1 if g == 1 else 2))
                        turn(s, mix, [(4 * g + c, i) for c in range(4)])
                    elif kind == "out":
                        f = s[4]
                        if f % 4 == 0:
                            for i in range(NT):
                                drained(pe, ("mix_turn", 0, l, f // 4, i))
                        out_unit_products(s, ("out", 0, l), h_hi[:, f, :], h_lo[:, f, :], f == 4, f == 3)
                    elif kind == "ff1":
                        _, _, t, q = s
                        there = features_there(n0 + 1) if t == 0 else None
                        feature_unit(s, [("ff1", l, t, i) for i in range(2)], q, there)
                    elif kind == "ff2":
                        f = s[3]
                        if f % 2 == 0:
                            pe.wait_ge(u_ready, 16 * l + f // 2 + 1)
                        t = f // 4
                        out_unit_products(s, ("ff2", l), u_hi[t % 2][:, f % 4, :], u_lo[t % 2][:, f % 4, :], f == 0, f == 31)

            for l in range(L):
                for s in timeline[1][l]:
                    kind = s[0]
                    if kind == "norm":
                        _, n, i, u = s
                        pe.wait_ge(xn_ready, NT * n + i + 1)
                        turn(s, xn, [(4 * u + c, i) for c in range(4)])
                    elif kind == "proj":
                        _, b, _, j, q = s
                        both = [("proj", b, l, j, i) for i in range(2)]
                        there = features_there(4 + l) if j == PROJ2[0] else None
                        (feature_unit if j in FEATURE2 else token_unit)(s, both, q, there)
                    elif kind == "forget_f":
                        ps = open_bank(s)
                        for i in range(NT):
                            for k in range(KD):
                                if k % 4 == 0:
                                    drained(pe, ("norm", 4 + l, i, k // 4))
                                t = slice(i * P, (i + 1) * P)
                                mm = exact_product(ps[:, 8 * i:8 * i + 8], (h_hi[:, k, t], h_lo[:, k, t]),
                                                   (ff_hi[:, l, k, :], ff_lo[:, l, k, :]), k == 0, k == KD - 1)
                        close(mm, s)
                    elif kind == "forget_sum":
                        pe.wait_ge(logf_ready, L + l + 1)
                        running_sum(s, g_lf, 8)
                    elif kind == "forget_row":
                        pe.wait_ge(a_ready, L + l + 1)
                        ps = open_bank(s)
                        for i in range(NT):
                            mm = pe.transpose(ps[0:8, i * P:(i + 1) * P], g_a[:, i, 0:8], ident)
                        close(mm, s)
                    elif kind == "turn2":
                        pe.wait_ge(vec_ready, 2 * L + l + 1)
                        turn(s, vec[:, :, :, :].rearrange("p i s d -> p i (s d)"),
                             [(2 * s[2] + c, i) for c in range(2) for i in range(NT)])
                    elif kind in ("diff", "fox"):
                        head_stage(kind, l, s[2], s[3])
                    elif kind == "stick" and s[2] == "Z":
                        h = s[3]
                        head_inputs(kind, l, "Z", h)
                        b = HD * (h % 2)
                        q, k = featT[b:b + HD, h // 2, :], featT[b:b + HD, 4 + h // 2, :]
                        ps = open_bank(("stick", l, "Z", h))
                        pe.matmul(ps[:, 0:T], k[:, 0:P], q, start=True, stop=False, skip_group_check=True)
                        pe.matmul(ps[:, T:T + P], k[:, P:T], q[:, P:T], start=False, stop=False, skip_group_check=True)
                        pe.matmul(ps[:, 0:P], ident_b, strict_b, start=False, stop=False, skip_group_check=True)
                        close(pe.matmul(ps[:, T:T + P], ident_b, strict_b, start=False, stop=False, skip_group_check=True), s)
                    elif kind == "stick" and s[2] == "R":
                        h = s[3]
                        ps = open_bank(("stick", l, "R", h))
                        kp = keep[:, h % 3, :]
                        rtri, nones = const[:, C_RTRI:C_RTRI + P], const[:, C_NONES:C_NONES + P]
                        pe.matmul(ps[:, 0:T], rtri, kp[:, 0:T], start=False, stop=False, skip_group_check=True)
                        pe.matmul(ps[:, P:T], nones, kp[:, T:T + P], start=False, stop=False, skip_group_check=True)
                        close(pe.matmul(ps[:, T:T + P], rtri, kp[:, T:T + P], start=False, stop=True, skip_group_check=True), s)
                    elif kind == "stick":
                        h = s[3]
                        g, r = divmod(h, 4)
                        head_inputs(kind, l, "V", h)
                        drained(pe, ("stick", l, "R", h))
                        ps = open_bank(("stick", l, "O", g)) if r == 0 else bank[bank_of[("stick", l, "O", g)]]
                        a, lo = probs[:, h % 3, :], r * 2 * HD
                        v0, v1 = (values[:, 1, i, HD * h:HD * (h + 1)] for i in range(2))
                        pe.matmul(ps[:, lo:lo + HD], a[:, 0:P], v0, start=True, stop=True)
                        pe.matmul(ps[:, lo + HD:lo + 2 * HD], a[:, P:T], v0, start=True, stop=False)
                        mm = pe.matmul(ps[:, lo + HD:lo + 2 * HD], a[:, T:T + P], v1, start=False, stop=True)
                        if r == 3:
                            close(mm, ("stick", l, "O", g))
                    elif kind == "mix_turn":
                        _, _, _, g, i = s
                        if g == 0:
                            pe.wait_ge(diff_mixed, l + 1)
                        else:
                            pe.wait_ge(mix_ready, 2 * L + 2 * l + g)
                        turn(s, mix, [(4 * g + c, i) for c in range(4)])
                    elif kind == "out":
                        f = s[4]
                        if f % 4 == 0:
                            for i in range(NT):
                                drained(pe, ("mix_turn", 1, l, f // 4, i))
                        g = f // 4
                        out_unit_products(s, ("out", 1, l), mixT_hi[g][:, f % 4, :], mixT_lo[g][:, f % 4, :],
                                          f == 0, f == KMIX2 - 1)

        @block.scalar
        def _(act):
            step = [0]
            n_split = [0]
            n_turned = [0]
            n_heads = [0]

            def link(ins):
                step[0] += 1
                ins.then_inc(scalar_step, 1)
                act.wait_ge(scalar_step, step[0])

            def free(ins, key):
                ins.then_inc(bank_freed[bank_of[key]], 1)
                drained(act, key)

            def split_to(n):
                while n_split[0] <= min(n, len(units) - 1):
                    m = n_split[0]
                    n_split[0] += 1
                    u = units[m]
                    if not u["split"]:
                        continue
                    act.wait_ge(raw_arrived[m % SLOTS], 16 * (m // SLOTS + 1))
                    if m >= SLOTS:
                        released(act, m - SLOTS)
                    act.activation(slot(w_hi, u), slot(raw, u), ACT.Copy).then_inc(hi_ready, 1)

            def src(key):
                split_to(at_unit[key] + AHEAD - 1)
                filled(act, key)
                return bank[bank_of[key]]

            def turned(key, dst):
                ps = src(key)
                act.activation(dst, ps[:, :].rearrange("p (c t) -> p c t", c=4), ACT.Copy).then_inc(turned_hi, 1)

            def norm_step(n, i, u):
                if u == 0:
                    if n == 0:
                        act.wait_ge(x_loaded, 16)
                    else:
                        act.wait_ge(x_tile_ready, NT * (n - 1) + i + 1)
                    act.activation(xn[:, i, :], x_sb[:, i, :], ACT.Square, accum_out=ss[:, i:i + 1]).then_inc(sumsq_ready, 1)
                    return
                for v in range(2):
                    turned(("norm", n, i, v), h_hi[:, 4 * v:4 * v + 4, i * P:(i + 1) * P])
                if i == NT - 1 and n + 1 < 3 * L:
                    act.dma_start(gain[:, :], GAINS[n + 1].partition_broadcast(P)).then_inc(gain_loaded, 16)

            def softmax_stage(kind, l, stage, h):
                name = (kind, l)
                if stage == "S":
                    ps = src((*name, "S", h))
                    n_heads[0] += 1
                    act.wait_ge(max_ready, n_heads[0])
                    g, r = divmod(h, GROUPS[kind])
                    link(act.activation(probs[:, h % 3, 0:P], ps[:, 0:P], ACT.Exp, scale=SCALE,
                                        bias=row_nb[:, h % 2, 0:1], accum_out=row_sum[:, g % 2, r, 0:1]))
                    free(act.activation(probs[:, h % 3, P:3 * P], ps[:, P:3 * P], ACT.Exp, scale=SCALE,
                                        bias=row_nb[:, h % 2, 1:2], accum_out=row_sum[:, g % 2, r, 1:2]), (*name, "S", h))
                elif stage == "T":
                    ps = src((*name, "T", h))
                    free(act.activation(probsT[:, h % 2, :], ps[:, 0:384], ACT.Copy), (*name, "T", h))

            GAINS = []
            for l in range(L):
                GAINS += [norm_mix[l], norm_ffn[l]]
            GAINS += [pre_norm_2[l] for l in range(L)]

            def wide(a):
                return a.partition_broadcast(P)

            act.dma_start(const[:, :], consts).then_inc(const_loaded, 16)
            act.dma_start(gain[:, :], wide(GAINS[0])).then_inc(gain_loaded, 16)
            act.dma_start(sel[:, :], selector).then_inc(const_loaded, 16)
            row_loads = [(prm_rows[0:64, 0:P], conv_qk.rearrange("l w (k p) -> (l w k) p", p=P)),
                         (prm_rows[0:64, P:2 * P], cmp_pe.rearrange("l v (a b) d -> (l v a) (b d)", b=2))]
            assert len(row_loads) == PRM_ROW_LOADS
            for dst, a in row_loads:
                act.dma_start(dst, a).then_inc(prm_rows_loaded, 16)
            act.preload_act_table_set(LOG_EXP)
            loads = [(bif[:, :, :], wide(b_if)),
                     (g_vec[:, :, 0:2, :], wide(moba_qk_norm)), (g_vec[:, :, 2, :], wide(nsa_q_norm)),
                     (g_vec[:, :, 3:6, :], wide(nsa_k_norm)), (m_gain[:, :, :], wide(m_norm)),
                     (w2c[:, :, :, :], cmp_w2.rearrange("l v e d -> e l v d")),
                     (f_bias[:, :, :], wide(forget_bias_2)), (lam_v[:, :, :, :], wide(diff_lambda_2)),
                     (sub_gain[:, :, :], wide(diff_subln_2))]
            loads += [(ff_w[:, 64 * l:64 * l + 64].rearrange("p (k c) -> p k c", c=8),
                       w_in_2[l][:, 6144:6152].rearrange("(k p) c -> p k c", p=P)) for l in range(L)]
            assert len(loads) == PRM_LOADS
            for dst, a in loads:
                act.dma_start(dst, a).then_inc(prm_loaded, 16)
            free(act.activation(prm[:, :], src(("params",))[:, 0:128], ACT.Copy), ("params",))

            for l in range(L):
                for s in timeline[0][l]:
                    kind = s[0]
                    if s in unit_no:
                        split_to(unit_no[s] + AHEAD)
                    if kind == "norm":
                        norm_step(*s[1:])
                    elif kind == "evac":
                        j = s[3]
                        if j == 3:
                            for i in range(NT):
                                key = ("proj", 0, l, 3, i)
                                free(act.activation(o_gate[:, i, :, :], src(key)[:, :].rearrange("p (h d) -> p h d", d=P),
                                                    ACT.Sigmoid), key)
                            act.preload_act_table_set(LOG_EXP)
                            continue
                        for i in range(NT):
                            key = ("proj", 0, l, j, i)
                            ps = src(key)
                            if j in FEATURE1:
                                if i == 0 and j == 0:
                                    act.wait_ge(vec_ready, 2 * l + 2)
                                dst = conv_in[:, 4 * j + 2 * i:4 * j + 2 * i + 2, 3:3 + T]
                                free(act.activation(dst, ps[:, :].rearrange("p (c t) -> p c t", c=2), ACT.Copy), key)
                            elif j == 2:
                                free(act.activation(v_aug[:, i, :, 0:P], ps[:, :].rearrange("p (h d) -> p h d", d=P), ACT.Copy), key)
                            else:
                                c0 = 512 * j - REST0
                                n = min(512, COLS1 - 512 * j)
                                free(act.activation(rest[:, i, c0:c0 + n], ps[:, 0:n], ACT.Copy), key)
                        if j == 6:
                            act.activation(n_gate, rest[:, :, 1416:1428], ACT.Sigmoid).then_inc(nsa_gated, 1)
                            act.preload_act_table_set(LOG_EXP)
                    elif kind == "gate_log":
                        act.wait_ge(gate_abs, l + 1)
                        link(act.activation(g_e[:, :, 0:4], g_e[:, :, 0:4], ACT.Exp))
                        act.activation(g_e[:, :, 0:4], g_e[:, :, 0:4], ACT.Ln, bias=1.0).then_inc(gate_log, 1)
                    elif kind in ("vec_a", "vec_b"):
                        v0, v1 = (0, 8) if kind == "vec_a" else (12, 22)
                        if s[2] == 0:
                            act.activation(squares[:, :, v0:v1, :].rearrange("p i s d -> p i (s d)"),
                                           rest[:, :, 8 + HD * v0:8 + HD * v1], ACT.Square).then_inc(squared, 1)
                        elif s[2] == 1:
                            act.wait_ge(vec_ms, 2 * l + (1 if kind == "vec_a" else 2))
                            link(act.activation(v_r[:, :, v0:v1], v_ms[:, :, v0:v1], ACT.Ln))
                            act.activation(v_r[:, :, v0:v1], v_r[:, :, v0:v1], ACT.Exp, scale=-0.5).then_inc(vec_rstd, 1)
                    elif kind == "turn" and s[2] != 4:
                        u = s[2]
                        free(act.activation(vecT[:, 2 * u:2 * u + 2, :], src(s)[:, :].rearrange("p (c t) -> p c t", c=2), ACT.Copy), s)
                    elif kind == "conv_silu":
                        act.wait_ge(conv_done, 4 * (l + 1))
                        act.activation(m_qk, m_qk, ACT.Silu).then_inc(conv_silu, 1)
                        act.preload_act_table_set(LOG_EXP)
                    elif kind == "m_rows":
                        if s[2] == 0:
                            act.wait_ge(m_col_ready, l + 1)
                            act.activation(e_m[:, :, 0:4], m_tok[:, :, 0:4], ACT.Exp).then_inc(stabilizer, 1)
                        u = s[2]
                        act.wait_ge(exponent_ready, 2 * l + u + 1)
                        act.activation(intra[:, 2 * u:2 * u + 2, :], intra[:, 2 * u:2 * u + 2, :], ACT.Exp).then_inc(intra_exp, 1)
                    elif kind == "hidden":
                        ps = src(s)
                        act.activation(hid[:, 0, :, 0:NC_CMP], ps[:, 0:32].rearrange("p (v c) -> p v c", c=16)[:, :, 0:NC_CMP],
                                       ACT.Exp, scale=-1.0).then_inc(hid_exp, 1)
                    elif kind == "cmp_kT":
                        free(act.activation(kcT[:, :], src(s)[:, 0:NC_CMP], ACT.Copy), s)
                    elif kind == "cmp_soft":
                        act.wait_ge(cmp_shifted, l + 1)
                        act.activation(p_cmp[:, :, :, 0:NC_CMP], p_cmp[:, :, :, 0:NC_CMP], ACT.Exp, scale=SCALE).then_inc(cmp_exp, 1)
                    elif kind == "cmp_pT":
                        free(act.activation(p_cmpT[:, :, :], src(s)[:, 0:T].rearrange("p (i t) -> p i t", i=NT), ACT.Copy), s)
                    elif kind == "mlstm" and s[2] == "O":
                        h = s[3]
                        ps = src(s)
                        link(act.activation(h_num[:, :, h, :], ps[:, 0:258].rearrange("p (i d) -> p i d", i=NT), ACT.Copy))
                        for i in range(NT):
                            ins = act.activation(sq_out[:, :], ps[:, 129 * i:129 * i + P], ACT.Square,
                                                 accum_out=h_ss[:, i, h:h + 1])
                            if i == 0:
                                link(ins)
                            else:
                                free(ins, s)
                    elif kind == "att1":
                        softmax_stage(kind, l, s[2], s[3])
                    elif kind == "mix_turn":
                        g, i = s[3], s[4]
                        turned(s, h_hi[:, 4 * g:4 * g + 4, i * P:(i + 1) * P])
                    elif kind == "square":
                        t = s[2]
                        for i in range(2):
                            n = 16 * l + 2 * t + i
                            ps = src(("ff1", l, t, i))
                            if n >= 2:
                                act.wait_ge(u_ready, n - 1)
                            free(act.activation(relu[:, i, :], ps[:, :], ACT.Relu), ("ff1", l, t, i))
                            act.activation(u_hi[t % 2][:, 2 * i:2 * i + 2, :], relu[:, i, :].rearrange("p (c t) -> p c t", c=2),
                                           ACT.Square).then_inc(u_hi_ready, 1)

            for l in range(L):
                for s in timeline[1][l]:
                    kind = s[0]
                    if s in unit_no:
                        split_to(unit_no[s] + AHEAD)
                    if kind == "norm":
                        norm_step(*s[1:])
                    elif kind == "forget_log":
                        act.wait_ge(gate_abs, L + l + 1)
                        link(act.activation(g_e, g_e, ACT.Exp))
                        act.activation(g_e, g_e, ACT.Ln, bias=1.0).then_inc(gate_log, 1)
                        act.wait_ge(lam_dots, l + 1)
                        act.activation(lam[:, 0:2], lam[:, 0:2], ACT.Exp).then_inc(lam_exp, 1)
                    elif kind == "evac":
                        j = s[3]
                        for i in range(NT):
                            key = ("proj", 1, l, j, i)
                            ps = src(key)
                            if j in FEATURE2:
                                c0 = {4: 0, 5: 4, 8: 8, 9: 12}[j] + 2 * i
                                free(act.activation(featT[:, c0:c0 + 2, :], ps[:, :].rearrange("p (c t) -> p c t", c=2), ACT.Copy,
                                                    scale=SCALE if j == 4 else 1.0), key)
                            elif j < 2:
                                free(act.activation(vec[:, i, 8 * j:8 * j + 8, :].rearrange("p s d -> p (s d)"), ps[:, :], ACT.Copy), key)
                            elif j % 4 == 2:
                                free(act.activation(values[:, j // 4, i, :], ps[:, :], ACT.Copy), key)
                            else:
                                free(act.activation(gates[:, i, j // 4, :], ps[:, :], ACT.Silu), key)
                        if j % 4 == 3:
                            act.preload_act_table_set(LOG_EXP)
                    elif kind == "forget_row":
                        free(act.activation(rows[0:8, 0, :], src(s)[0:8, 0:T], ACT.Copy), s)
                    elif kind == "turn2":
                        u = s[2]
                        free(act.activation(vecT[:, 2 * u:2 * u + 2, :], src(s)[:, :].rearrange("p (c t) -> p c t", c=2), ACT.Copy), s)
                        if u == 3:
                            act.dma_start(post_gain, post_norm_2[l].partition_broadcast(P)).then_inc(post_loaded, 16)
                    elif kind in ("diff", "fox"):
                        softmax_stage(kind, l, s[2], s[3])
                    elif kind == "stick" and s[2] == "Z":
                        h = s[3]
                        ps = src(s)
                        if h >= 2:
                            drained(act, ("stick", l, "Z", h - 2))
                        link(act.activation(softp[:, h % 2, :], ps[:, 0:384], ACT.Abs))
                        link(act.activation(softp[:, h % 2, :], softp[:, h % 2, :], ACT.Exp, scale=-1.0))
                        act.activation(softp[:, h % 2, :], softp[:, h % 2, :], ACT.Ln, bias=1.0).then_inc(stick_log, 1)
                    elif kind == "stick" and s[2] == "R":
                        free(act.activation(probs[:, s[3] % 3, :], src(s)[:, 0:384], ACT.Exp), s)
                    elif kind == "mix_turn":
                        g, i = s[3], s[4]
                        turned(s, mixT_hi[g][:, 0:4, i * P:(i + 1) * P])
                    elif kind == "post_norm":
                        for a in range(4):
                            ps = src(("out", 1, l, "acc", a))
                            act.activation(xn[:, a // 2, (a % 2) * 512:(a % 2 + 1) * 512], ps[:, :], ACT.Square,
                                           accum_out=y_ss[:, a:a + 1]).then_inc(y_sumsq, 1)

        @block.gpsimd
        def _(pool):
            step = [0]
            n_split = [0]

            def link(ins):
                step[0] += 1
                ins.then_inc(pool_step, 1)
                pool.wait_ge(pool_step, step[0])

            def split_to(n):
                while n_split[0] <= min(n, len(units) - 1):
                    m = n_split[0]
                    n_split[0] += 1
                    u = units[m]
                    if u["split"] and u["lo_on"] == "pool":
                        pool.wait_ge(hi_ready, u["n_hi"])
                        pool.tensor_tensor(slot(w_lo, u), slot(raw, u), slot(w_hi, u).bitcast(F32), ALU.subtract)\
                            .then_inc(lo_ready["pool"], 1)

            def row_rstd(n, i):
                pool.wait_ge(sumsq_ready, NT * n + i + 1)
                link(pool.tensor_scalar(ms[:, i:i + 1], ss[:, i:i + 1], 1.0 / D, EPS, ALU.mult, ALU.add))
                pool.tensor_tensor(rstd[:, i:i + 1], ms[:, i:i + 1], half_neg[:, 0:1], ALU.pow).then_inc(rstd_ready, 1)

            pool.memset(half_neg, -0.5).then_inc(half_neg_set, 1)
            pool.wait_ge(half_neg_set, 1)
            for l in range(L):
                for s in timeline[0][l]:
                    kind = s[0]
                    if s in unit_no:
                        split_to(unit_no[s] + AHEAD)
                    if kind == "norm" and s[3] == 0:
                        row_rstd(s[1], s[2])
                    elif kind == "m_rows":
                        u = s[2]
                        pool.wait_ge(intra_exp, 2 * l + u + 1)
                        le = const[:, C_LE:C_LE + P]
                        if l == 0 and u == 0:
                            pool.wait_ge(const_loaded, 32)
                        for h in (2 * u, 2 * u + 1):
                            link(pool.tensor_tensor(intra[:, h, 0:P], intra[:, h, 0:P], le, ALU.mult))
                            pool.tensor_tensor(intra[:, h, 2 * P:3 * P], intra[:, h, 2 * P:3 * P], le, ALU.mult).then_inc(intra_masked, 1)
                    elif kind == "cmp_kv":
                        pool.wait_ge(kc_ms, l + 1)
                        pool.tensor_tensor(kc_s[0:NC_CMP, 2:3], kc_s[0:NC_CMP, 1:2], half_neg[0:NC_CMP, 0:1], ALU.pow).then_inc(kc_rstd, 1)
                    elif kind == "evac" and s[3] == 3:
                        for i in range(NT):
                            drained(pool, ("proj", 0, l, 3, i))
                            if l == 0 and i == 0:
                                pool.wait_ge(prm_loaded, 16 * PRM_LOADS)
                            pool.tensor_tensor(o_gate[:, i], o_gate[:, i], m_gain[:, l, :].rearrange("p (h d) -> p h d", d=P),
                                               ALU.mult).then_inc(o_gained, 1)
                    elif kind == "mlstm_end":
                        pool.wait_ge(h_ms_ready, l + 1)
                        pool.tensor_tensor(h_rs.rearrange("p a b -> p (a b)"), h_ms.rearrange("p a b -> p (a b)"), half_neg,
                                           ALU.pow).then_inc(h_rstd_ready, 1)
            for l in range(L):
                for s in timeline[1][l]:
                    kind = s[0]
                    if s in unit_no:
                        split_to(unit_no[s] + AHEAD)
                    if kind == "norm" and s[3] == 0:
                        row_rstd(s[1], s[2])
                    elif s == ("diff", l, "V", 7):
                        pool.wait_ge(h_ms_ready, L + l + 1)
                        for i in range(NT):
                            drained(pool, ("proj", 1, l, 3, i))
                        link(pool.tensor_tensor(h_rs.rearrange("p a b -> p (a b)"), h_ms.rearrange("p a b -> p (a b)"), half_neg, ALU.pow))
                        link(pool.tensor_tensor(y_diff, y_diff, h_rs.unsqueeze(3).broadcast_to([P, NT, MH, P]), ALU.mult))
                        sg = sub_gain[:, l, :]
                        link(pool.tensor_scalar(sg, sg, 1.0 - LAM_INIT[l], None, ALU.mult))
                        for i in range(NT):
                            link(pool.tensor_tensor(y_diff[:, i], y_diff[:, i], sg.unsqueeze(1).broadcast_to([P, MH, P]), ALU.mult))
                        pool.tensor_tensor(mix[:, :, 0:512].rearrange("p i (h d) -> p i h d", d=P), y_diff,
                                           gates[:, :, 0, :].rearrange("p i (h d) -> p i h d", d=P), ALU.mult).then_inc(diff_mixed, 1)
                    elif kind == "post_norm":
                        for i in range(NT):
                            pool.wait_ge(y_ms, NT * l + i + 1)
                            pool.tensor_tensor(rstd[:, i:i + 1], ms[:, i:i + 1], half_neg[:, 0:1], ALU.pow).then_inc(y_rstd, 1)

        @block.vector
        def _(dve):
            step = [0]
            n_split = [0]
            n_turned = [0]

            def link(ins):
                step[0] += 1
                ins.then_inc(vector_step, 1)
                dve.wait_ge(vector_step, step[0])

            def free(ins, key):
                ins.then_inc(bank_freed[bank_of[key]], 1)
                drained(dve, key)

            def split_to(n):
                while n_split[0] <= min(n, len(units) - 1):
                    m = n_split[0]
                    n_split[0] += 1
                    u = units[m]
                    if u["split"] and u["lo_on"] == "vector":
                        dve.wait_ge(hi_ready, u["n_hi"])
                        dve.tensor_tensor(slot(w_lo, u), slot(raw, u), slot(w_hi, u).bitcast(F32), ALU.subtract)\
                            .then_inc(lo_ready["vector"], 1)

            def src(key):
                split_to(at_unit[key] + AHEAD - 1)
                filled(dve, key)
                return bank[bank_of[key]]

            def tt(out, a, b, op):
                link(dve.tensor_tensor(out, a, b, op))

            def signal(sem_):
                dve.tensor_copy(flag[:, 0:1], flag[:, 1:2]).then_inc(sem_, 1)

            def turned(key, hi, lo):
                ps = src(key)
                n_turned[0] += 1
                dve.wait_ge(turned_hi, n_turned[0])
                free(dve.tensor_tensor(lo, ps[:, :].rearrange("p (c t) -> p c t", c=4), hi.bitcast(F32), ALU.subtract), key)

            def norm_step(n, i, u):
                if u == 0:
                    dve.wait_ge(rstd_ready, NT * n + i + 1)
                    if i == 0:
                        dve.wait_ge(gain_loaded, 16 * (n + 1))
                    dve.scalar_tensor_tensor(xn[:, i, :], x_sb[:, i, :], rstd[:, i:i + 1], gain[:, :], ALU.mult, ALU.mult)\
                        .then_inc(xn_ready, 1)
                    return
                for v in range(2):
                    c, t = slice(4 * v, 4 * v + 4), slice(i * P, (i + 1) * P)
                    turned(("norm", n, i, v), h_hi[:, c, t], h_lo[:, c, t])

            def residual(name):
                for a in range(4):
                    ps = src((*name, "acc", a))
                    xs = x_sb[:, a // 2, (a % 2) * 512:(a % 2 + 1) * 512]
                    free(dve.tensor_tensor(xs, xs, ps[:, :], ALU.add), (*name, "acc", a))
                    if a % 2:
                        signal(x_tile_ready)

            def log_sigmoid(n, f, idx):
                dve.scalar_tensor_tensor(g_e[:, :, 0:n], f, -1.0, f, ALU.mult, ALU.min).then_inc(gate_abs, 1)
                dve.wait_ge(gate_log, idx + 1)
                link(dve.tensor_scalar(g_lf[:, :, 0:n], f, 0.0, None, ALU.min))
                dve.tensor_tensor(g_lf[:, :, 0:n], g_lf[:, :, 0:n], g_e[:, :, 0:n], ALU.subtract).then_inc(logf_ready, 1)

            def rope(s0, s1):
                n = s1 - s0
                a, b = vec[:, :, s0:s1, 0:8], vec[:, :, s0:s1, 8:16]
                cos = const[:, C_COS:C_COS + NT * 8].rearrange("p (i d) -> p i d", i=NT).unsqueeze(2).broadcast_to([P, NT, n, 8])
                sin = const[:, C_SIN:C_SIN + NT * 8].rearrange("p (i d) -> p i d", i=NT).unsqueeze(2).broadcast_to([P, NT, n, 8])
                t = [o_tmp[:, 0:256], o_tmp[:, 256:512], softp[:, 0, 0:256], softp[:, 1, 0:256]]
                t = [y[:, 0:NT * n * 8].rearrange("p (i s d) -> p i s d", i=NT, d=8) for y in t]
                tt(t[0], a, cos, ALU.mult)
                tt(t[1], b, sin, ALU.mult)
                tt(t[2], b, cos, ALU.mult)
                tt(t[3], a, sin, ALU.mult)
                tt(a, t[0], t[1], ALU.subtract)
                dve.tensor_tensor(b, t[2], t[3], ALU.add).then_inc(vec_ready, 1)

            def row_max(name, h):
                ps = src((*name, "S", h))
                link(dve.tensor_reduce(row_mx[:, h % 2, 0:1], ps[:, 0:P], AX.X, ALU.max))
                link(dve.tensor_reduce(row_mx[:, h % 2, 1:2], ps[:, P:3 * P], AX.X, ALU.max))
                dve.tensor_scalar(row_nb[:, h % 2, :], row_mx[:, h % 2, :], -SCALE, None, ALU.mult).then_inc(max_ready, 1)

            link(dve.memset(flag[:, :], 1.0))
            dve.wait_ge(const_loaded, 32)
            for n, c in enumerate((C_ID, C_CAUSAL, C_CHUNK, C_STRICT)):
                link(dve.tensor_copy(masks[:, n * P:(n + 1) * P], const[:, c:c + P]))

            for l in range(L):
                rv = rest[:, :, 8:8 + NVEC * HD].rearrange("p i (s d) -> p i s d", d=HD)

                def scaled(dst, s0, n, g):
                    o = vec[:, :, dst:dst + n, :]
                    tt(o, rv[:, :, s0:s0 + n, :], v_r[:, :, s0:s0 + n].unsqueeze(3).broadcast_to([P, NT, n, HD]), ALU.mult)
                    tt(o, o, g_vec[:, l, g, :].unsqueeze(1).unsqueeze(1).broadcast_to([P, NT, n, HD]), ALU.mult)

                def mean_squares(v0, v1, idx):
                    dve.wait_ge(squared, idx)
                    link(dve.tensor_reduce(v_ss[:, :, v0:v1], squares[:, :, v0:v1, :], AX.X, ALU.add))
                    dve.tensor_scalar(v_ms[:, :, v0:v1], v_ss[:, :, v0:v1], 1.0 / HD, EPS, ALU.mult, ALU.add).then_inc(vec_ms, 1)

                def refine(v0, v1, idx):
                    r, v, t = v_r[:, :, v0:v1], v_ms[:, :, v0:v1], v_t[:, :, v0:v1]
                    dve.wait_ge(vec_rstd, idx)
                    tt(t, r, r, ALU.mult)
                    tt(t, t, v, ALU.mult)
                    link(dve.tensor_scalar(t, t, -0.5, 1.5, ALU.mult, ALU.add))
                    tt(r, r, t, ALU.mult)

                def epilogue1(g):
                    name = ("att1", l, "O", g)
                    ps = src(name)
                    ov = ps[:, :].rearrange("p (h i d) -> p h i d", h=4, i=NT)
                    link(dve.reciprocal(row_inv, row_sum[:, g % 2]))
                    lo = 512 if g == 0 else 768
                    dst = mix[:, :, lo:lo + 256].rearrange("p i (h d) -> p h i d", d=HD)
                    if g:
                        tt(row_inv, row_inv, n_gate[:, :, 4 * g:4 * g + 4].rearrange("p i h -> p h i"), ALU.mult)
                    f = row_inv.unsqueeze(3).broadcast_to([P, 4, NT, HD])
                    if g < 2:
                        free(dve.tensor_tensor(dst, ov, f, ALU.mult), name)
                        return
                    t = o_tmp[:, :].rearrange("p (h i d) -> p h i d", h=4, i=NT)
                    free(dve.tensor_tensor(t, ov, f, ALU.mult), name)
                    dve.tensor_tensor(dst, dst, t, ALU.add).then_inc(mix_ready, 1)

                for s in timeline[0][l]:
                    kind = s[0]
                    if s in unit_no:
                        split_to(unit_no[s] + AHEAD)
                    if kind == "norm":
                        norm_step(*s[1:])
                        if s == ("norm", 0, NT - 1, 1):
                            link(dve.memset(vc_diag[:, :, :], 0.0))
                            link(dve.memset(p_cmp[:, :, :, :], 0.0))
                            dve.wait_ge(prm_loaded, 16 * PRM_LOADS)
                            drained(dve, ("params",))
                            link(dve.tensor_copy(ff_hi[:, :, :, :].rearrange("p l k c -> p (l k c)"), ff_w[:, :]))
                            link(dve.tensor_tensor(ff_lo[:, :, :, :].rearrange("p l k c -> p (l k c)"), ff_w[:, :],
                                                   ff_hi[:, :, :, :].rearrange("p l k c -> p (l k c)").bitcast(F32), ALU.subtract))
                    elif kind == "gate_log":
                        for i in range(NT):
                            drained(dve, ("proj", 0, l, 4, i))
                        link(dve.memset(v_aug[:, :, :, 128:130], 1.0))
                        tt(gif, rest[:, :, 0:8], bif[:, l, :].unsqueeze(1).broadcast_to([P, NT, 8]), ALU.add)
                        log_sigmoid(4, gif[:, :, 4:8], l)
                    elif kind == "gate_sum":
                        Fv = src(s)[:, 0:8].rearrange("p (i h) -> p i h", i=NT)
                        link(dve.tensor_copy(g_F[:, :, 0:4], Fv))
                        free(dve.tensor_tensor(g_a[:, :, 0:4], gif[:, :, 0:4], Fv, ALU.subtract), s)
                        signal(a_ready)
                    elif kind == "gate_row":
                        free(dve.tensor_copy(rows[0:4, 2, :], src(s)[0:4, 0:T]), s)
                        link(dve.tensor_tensor_scan(rows[0:4, 0, :], rows[0:4, 2, :], rows[0:4, 2, :], 0.0, ALU.max, ALU.max))
                        dve.tensor_scalar(rows[0:4, 1, :], rows[0:4, 0, :], -1.0, None, ALU.mult).then_inc(m_ready, 1)
                    elif kind == "vec_a":
                        if s[2] == 0:
                            mean_squares(0, 8, 2 * l + 1)
                        elif s[2] == 1:
                            refine(0, 8, 2 * l + 1)
                            scaled(0, 0, 4, 0)
                        else:
                            scaled(4, 4, 4, 1)
                            rope(0, 8)
                    elif kind == "vec_b":
                        if s[2] == 0:
                            mean_squares(12, 22, 2 * l + 2)
                        elif s[2] == 1:
                            refine(12, 22, 2 * l + 2)
                            scaled(20, 12, 4, 2)
                            link(dve.tensor_copy(vec[:, :, 8:12, :], vec[:, :, 20:24, :]))
                        elif s[2] == 2:
                            scaled(12, 18, 1, 4)
                            scaled(14, 20, 1, 5)
                            link(dve.tensor_copy(vec[:, :, 13, :], vec[:, :, 12, :]))
                            link(dve.tensor_copy(vec[:, :, 15, :], vec[:, :, 14, :]))
                        else:
                            for c in range(4):
                                link(dve.tensor_copy(vec[:, :, 16 + c, :], rv[:, :, 16 + c // 2, :]))
                            link(dve.memset(conv_in[:, :, 0:3], 0.0))
                            rope(8, 16)
                    elif kind == "turn" and s[2] == 4:
                        ps = src(s)
                        for v in range(2):
                            for half in range(2):
                                lo = HD * half
                                t = ps[lo:lo + HD, v * T:(v + 1) * T]
                                pe_col = prm[lo:lo + HD, 64 + (l * 2 + v) * 16:64 + (l * 2 + v) * 16 + 16]
                                for r in range(2):
                                    tok = t[:, 16 * r:16 * r + 240].rearrange("p (c a b) -> p a c b", a=8, b=2)[:, :, :, half]
                                    ins = dve.tensor_tensor(blocksT[lo:lo + HD, v, 8 * r:8 * r + 8, :], tok,
                                                            pe_col[:, 8 * r:8 * r + 8].unsqueeze(2).broadcast_to([HD, 8, NC_CMP]), ALU.add)
                                    if v and half and r:
                                        free(ins, s)
                                    else:
                                        link(ins)
                        signal(blocks_ready)
                    elif kind == "m_col":
                        free(dve.tensor_tensor(m_tok[:, :, 0:4], src(s)[:, 0:8].rearrange("p (i h) -> p i h", i=NT),
                                               g_F[:, :, 0:4], ALU.subtract), s)
                        signal(m_col_ready)
                    elif kind == "m_rows":
                        for c in range(2):
                            h = 2 * s[2] + c
                            ps = src(s)[:, c * T:(c + 1) * T]
                            link(dve.tensor_scalar(intra[:, h, 0:T], ps, g_a[:, 0, h:h + 1], 0.0, ALU.add, ALU.min))
                            ins = dve.tensor_scalar(intra[:, h, T:T + P], ps[:, P:T], g_a[:, 1, h:h + 1], 0.0, ALU.add, ALU.min)
                            if c == 1:
                                free(ins, s)
                            else:
                                link(ins)
                        signal(exponent_ready)
                    elif kind == "conv":
                        j, i = divmod(s[2], 2)
                        drained(dve, ("proj", 0, l, j, i))
                        for c in (2 * s[2], 2 * s[2] + 1):
                            acc = m_qk[:, c, :]
                            link(dve.tensor_scalar(acc, conv_in[:, c, 0:T], conv_col(l, 0, c), None, ALU.mult))
                            for tap in range(1, 4):
                                ins = dve.scalar_tensor_tensor(acc, conv_in[:, c, tap:tap + T], conv_col(l, tap, c), acc,
                                                               ALU.mult, ALU.add)
                                if tap == 3 and c % 2 == 1:
                                    ins.then_inc(conv_done, 1)
                                else:
                                    link(ins)
                    elif kind == "hidden":
                        ps = src(s)
                        dve.wait_ge(hid_exp, l + 1)
                        link(dve.tensor_scalar(hid[:, 0, :, 0:NC_CMP], hid[:, 0, :, 0:NC_CMP], 1.0, None, ALU.add))
                        link(dve.reciprocal(hid[:, 0, :, 0:NC_CMP], hid[:, 0, :, 0:NC_CMP]))
                        free(dve.tensor_tensor(hid[:, 1, :, 0:NC_CMP], hid[:, 0, :, 0:NC_CMP],
                                               ps[:, 0:32].rearrange("p (v c) -> p v c", c=16)[:, :, 0:NC_CMP], ALU.mult), s)
                        signal(hid_ready)
                    elif kind == "cmp_kv":
                        ps = src(s)
                        link(dve.tensor_copy(kc_n[:, 0, :], ps[0:NC_CMP, 0:HD]))
                        for h in range(4):
                            ins = dve.tensor_copy(vc_diag[32 * h:32 * h + NC_CMP, h, :], ps[0:NC_CMP, HD:2 * HD])
                            if h < 3:
                                link(ins)
                            else:
                                free(ins, s)
                        tt(kc_n[:, 1, :], kc_n[:, 0, :], kc_n[:, 0, :], ALU.mult)
                        link(dve.tensor_reduce(kc_s[0:NC_CMP, 0:1], kc_n[:, 1, :], AX.X, ALU.add))
                        dve.tensor_scalar(kc_s[0:NC_CMP, 1:2], kc_s[0:NC_CMP, 0:1], 1.0 / HD, EPS, ALU.mult, ALU.add).then_inc(kc_ms, 1)
                        dve.wait_ge(kc_rstd, l + 1)
                        link(dve.tensor_scalar(kc_n[:, 0, :], kc_n[:, 0, :], kc_s[0:NC_CMP, 2:3], None, ALU.mult))
                        tt(kc_n[:, 0, :], kc_n[:, 0, :], g_vec[0:NC_CMP, l, 3, :], ALU.mult)
                        dve.tensor_copy(kc_n[:, 1, :], kc_n[:, 0, :]).then_inc(kc_ready, 1)
                    elif kind == "cmp_s":
                        odd = s[2]
                        mask = const[:, C_CNEG:C_CNEG + NT * NC_CMP].rearrange("p (i c) -> p i c", i=NT)
                        free(dve.tensor_tensor(p_cmp[:, :, odd:4:2, 0:NC_CMP],
                                               src(s)[:, 0:64].rearrange("p (i h c) -> p i h c", i=NT, h=2)[:, :, :, 0:NC_CMP],
                                               mask.unsqueeze(2).broadcast_to([P, NT, 2, NC_CMP]), ALU.add), s)
                    elif kind == "cmp_soft":
                        pc = p_cmp[:, :, :, 0:NC_CMP]
                        seen_ = const[:, C_C01:C_C01 + NT * NC_CMP].rearrange("p (i c) -> p i c", i=NT)
                        link(dve.tensor_reduce(c_mx, pc, AX.X, ALU.max))
                        dve.tensor_tensor(pc, pc, c_mx.unsqueeze(3).broadcast_to([P, NT, 4, NC_CMP]), ALU.subtract).then_inc(cmp_shifted, 1)
                        dve.wait_ge(cmp_exp, l + 1)
                        link(dve.tensor_reduce(c_sum, pc, AX.X, ALU.add))
                        link(dve.reciprocal(c_sum, c_sum))
                        dve.wait_ge(nsa_gated, l + 1)
                        tt(c_sum, c_sum, n_gate[:, :, 0:4], ALU.mult)
                        tt(pc, pc, c_sum.unsqueeze(3).broadcast_to([P, NT, 4, NC_CMP]), ALU.mult)
                        dve.tensor_tensor(pc, pc, seen_.unsqueeze(2).broadcast_to([P, NT, 4, NC_CMP]), ALU.mult).then_inc(cmp_ready, 1)
                    elif kind == "cmp_o":
                        dst = mix[:, :, 1024:1280]
                        free(dve.tensor_copy(dst, src(s)[:, :].rearrange("p (i c) -> p i c", i=NT)), s)
                    elif kind == "mlstm" and s[2] == "S":
                        h = s[3]
                        ps = src(s)
                        dve.wait_ge(intra_masked, MH * l + h + 1)
                        free(dve.scalar_tensor_tensor(m_probs[:, h % 2, :], ps[:, 0:384], M_SCALE, intra[:, h, :],
                                                      ALU.mult, ALU.mult), s)
                    elif kind == "att1":
                        if s[2] == "S":
                            row_max(("att1", l), s[3])
                        elif s[2] == "V" and s[3] % 4 == 3:
                            g = s[3] // 4
                            if g == 2:
                                tt(mix[:, :, 768:1024], mix[:, :, 768:1024], mix[:, :, 1024:1280], ALU.add)
                            epilogue1(g)
                    elif kind == "mlstm_end":
                        for h in range(MH):
                            drained(dve, ("mlstm", l, "O", h))
                        dve.wait_ge(stabilizer, l + 1)
                        den, d, inv = h_num[:, :, :, 128], m_den[:, :, 0:4], m_den[:, :, 4:8]
                        link(dve.scalar_tensor_tensor(d, den, -1.0, den, ALU.mult, ALU.max))
                        tt(d, d, e_m[:, :, 0:4], ALU.max)
                        link(dve.reciprocal(inv, d))
                        tt(h_ms, h_ss, inv, ALU.mult)
                        tt(h_ms, h_ms, inv, ALU.mult)
                        dve.tensor_scalar(h_ms, h_ms, 1.0 / P, EPS, ALU.mult, ALU.add).then_inc(h_ms_ready, 1)
                        dve.wait_ge(h_rstd_ready, l + 1)
                        tt(inv, inv, h_rs, ALU.mult)
                        dve.wait_ge(o_gained, NT * (l + 1))
                        hn = h_num[:, :, :, 0:P]
                        tt(hn, hn, inv.unsqueeze(3).broadcast_to([P, NT, MH, P]), ALU.mult)
                        dve.tensor_tensor(mix[:, :, 0:512].rearrange("p i (h d) -> p i h d", d=P), hn, o_gate, ALU.mult)\
                            .then_inc(mix_ready, 1)
                    elif kind == "mix_turn":
                        c, t = slice(4 * s[3], 4 * s[3] + 4), slice(s[4] * P, (s[4] + 1) * P)
                        turned(s, h_hi[:, c, t], h_lo[:, c, t])
                    elif kind == "residual":
                        residual(s[1])
                    elif kind == "square":
                        t = s[2]
                        for i in range(2):
                            n = 16 * l + 2 * t + i
                            split_to(at_unit[("ff1", l, t, i)] + AHEAD - 1)
                            drained(dve, ("ff1", l, t, i))
                            r = relu[:, i, :]
                            tt(u_full[:, i, :], r, r, ALU.mult)
                            dve.wait_ge(u_hi_ready, n + 1)
                            b = slice(2 * i, 2 * i + 2)
                            dve.tensor_tensor(u_lo[t % 2][:, b, :], u_full[:, i, :].rearrange("p (c t) -> p c t", c=2),
                                              u_hi[t % 2][:, b, :].bitcast(F32), ALU.subtract).then_inc(u_ready, 1)

            for l in range(L):
                def epilogue_diff(g):
                    name = ("diff", l, "O", g)
                    ov = src(name)[:, :].rearrange("p (c i d) -> p c i d", c=2, i=NT)
                    inv = row_inv[:, 0:2, :]
                    link(dve.reciprocal(inv, row_sum[:, g % 2, 0:2, :]))
                    link(dve.tensor_scalar(inv[:, 1, :], inv[:, 1, :], lam[:, 3:4], None, ALU.mult))
                    t = o_tmp[:, :].rearrange("p (c i d) -> p c i d", c=2, i=NT)
                    free(dve.tensor_tensor(t, ov, inv.unsqueeze(3).broadcast_to([P, 2, NT, P]), ALU.mult), name)
                    tt(y_diff[:, :, g, :], t[:, 0], t[:, 1], ALU.add)
                    tt(y_tmp[:, :, g, :], y_diff[:, :, g, :], y_diff[:, :, g, :], ALU.mult)
                    link(dve.tensor_reduce(h_ss[:, :, g:g + 1], y_tmp[:, :, g:g + 1, :], AX.X, ALU.add))
                    if g == 3:
                        dve.tensor_scalar(h_ms, h_ss, 1.0 / P, EPS, ALU.mult, ALU.add).then_inc(h_ms_ready, 1)

                def gated(name, p, g, weights):
                    ov = src(name)[:, :].rearrange("p (h i d) -> p h i d", h=4, i=NT)
                    lo = 512 * p + 256 * g
                    dst = mix[:, :, lo:lo + 256].rearrange("p i (h d) -> p h i d", d=HD)
                    gate = gates[:, :, p, 256 * g:256 * g + 256].rearrange("p i (h d) -> p h i d", d=HD)
                    if g == 0:
                        for i in range(NT):
                            drained(dve, ("proj", 1, l, 4 * p + 3, i))
                    if weights is None:
                        free(dve.tensor_tensor(dst, ov, gate, ALU.mult), name)
                        if g == 1:
                            signal(mix_ready)
                        return
                    link(dve.reciprocal(row_inv, weights))
                    t = o_tmp[:, :].rearrange("p (h i d) -> p h i d", h=4, i=NT)
                    free(dve.tensor_tensor(t, ov, row_inv.unsqueeze(3).broadcast_to([P, 4, NT, HD]), ALU.mult), name)
                    if g == 1:
                        dve.tensor_tensor(dst, t, gate, ALU.mult).then_inc(mix_ready, 1)
                    else:
                        tt(dst, t, gate, ALU.mult)

                for s in timeline[1][l]:
                    kind = s[0]
                    if s in unit_no:
                        split_to(unit_no[s] + AHEAD)
                    if kind == "norm":
                        norm_step(*s[1:])
                    elif kind == "forget_f":
                        free(dve.tensor_tensor(gif, src(s)[:, 0:16].rearrange("p (i h) -> p i h", i=NT),
                                               f_bias[:, l, :].unsqueeze(1).broadcast_to([P, NT, 8]), ALU.add), s)
                    elif kind == "forget_log":
                        log_sigmoid(8, gif, L + l)
                        prod = o_tmp[:, 0:2 * HD].rearrange("p (a d) -> p a d", a=2)
                        lv = lam_v[:, l, :, :].rearrange("p (a b) d -> p a b d", b=2)
                        tt(prod, lv[:, :, 0, :], lv[:, :, 1, :], ALU.mult)
                        dve.tensor_reduce(lam[:, 0:2], prod, AX.X, ALU.add).then_inc(lam_dots, 1)
                        dve.wait_ge(lam_exp, l + 1)
                        tt(lam[:, 2:3], lam[:, 1:2], lam[:, 0:1], ALU.subtract)
                        link(dve.tensor_scalar(lam[:, 3:4], lam[:, 2:3], -LAM_INIT[l], None, ALU.add))
                    elif kind == "forget_sum":
                        free(dve.tensor_scalar(g_a, src(s)[:, 0:16].rearrange("p (i h) -> p i h", i=NT), -1.0 / SCALE, None, ALU.mult), s)
                        signal(a_ready)
                    elif kind == "rope2":
                        for j in (0, 1):
                            for i in range(NT):
                                drained(dve, ("proj", 1, l, j, i))
                        rope(0, 16)
                    elif kind in ("diff", "fox"):
                        if s[2] == "S":
                            row_max((kind, l), s[3])
                        elif s[2] == "V" and s[3] % GROUPS[kind] == GROUPS[kind] - 1:
                            g = s[3] // GROUPS[kind]
                            if kind == "diff":
                                epilogue_diff(g)
                            else:
                                gated(("fox", l, "O", g), 2, g, row_sum[:, g % 2])
                    elif kind == "stick" and s[2] == "Z":
                        h = s[3]
                        ps = src(s)
                        dve.wait_ge(stick_log, 8 * l + h + 1)
                        free(dve.scalar_tensor_tensor(keep[:, h % 3, :], ps[:, 0:384], 0.0, softp[:, h % 2, :], ALU.max, ALU.add), s)
                    elif kind == "stick" and s[2] == "V" and s[3] % 4 == 3:
                        gated(("stick", l, "O", s[3] // 4), 1, s[3] // 4, None)
                    elif kind == "mix_turn":
                        g, t = s[3], slice(s[4] * P, (s[4] + 1) * P)
                        turned(s, mixT_hi[g][:, 0:4, t], mixT_lo[g][:, 0:4, t])
                    elif kind == "post_norm":
                        for i in range(NT):
                            dve.wait_ge(y_sumsq, 4 * l + 2 * i + 2)
                            tt(ss[:, i:i + 1], y_ss[:, 2 * i:2 * i + 1], y_ss[:, 2 * i + 1:2 * i + 2], ALU.add)
                            dve.tensor_scalar(ms[:, i:i + 1], ss[:, i:i + 1], 1.0 / D, EPS, ALU.mult, ALU.add).then_inc(y_ms, 1)
                            dve.wait_ge(y_rstd, NT * l + i + 1)
                            if i == 0:
                                dve.wait_ge(post_loaded, 16 * (l + 1))
                            for half in range(2):
                                key = ("out", 1, l, "acc", 2 * i + half)
                                c = slice(half * 512, (half + 1) * 512)
                                ps = src(key)
                                free(dve.scalar_tensor_tensor(o_tmp[:, :], ps[:, :], rstd[:, i:i + 1], post_gain[:, c],
                                                              ALU.mult, ALU.mult), key)
                                ins = dve.tensor_tensor(x_sb[:, i, c], x_sb[:, i, c], o_tmp[:, :], ALU.add)
                                if half:
                                    ins.then_inc(x_tile_ready, 1)
                                else:
                                    link(ins)


PRM_LOADS = 9 + L
PRM_ROW_LOADS = 2

_INS = ['x', 'w_in', 'b_if', 'conv_qk', 'm_norm', 'moba_qk_norm', 'nsa_q_norm', 'nsa_k_norm', 'cmp_pe', 'cmp_w1',
        'cmp_w2', 'w_out', 'norm_mix', 'norm_ffn', 'w_ff1', 'w_ff2', 'w_in_2', 'forget_bias_2', 'diff_lambda_2',
        'diff_subln_2', 'w_out_2', 'pre_norm_2', 'post_norm_2']


def kernel(**inputs):
    import concourse.bacc as bacc
    from concourse.bass_utils import run_bass_kernel_spmd

    nc = bacc.Bacc("TRN2", target_bir_lowering=False, num_devices=1)
    table, selector = constants()
    arrays, args = {}, []
    for name, a in [(n, inputs[n]) for n in _INS] + [("consts", table), ("selector", selector)]:
        a = np.ascontiguousarray(a)
        arrays[f"in_{name}"] = a
        args.append(nc.dram_tensor(f"in_{name}", a.shape, mybir.dt.from_np(a.dtype), kind="ExternalInput").ap())
    args.append(nc.dram_tensor("out_x", (1, T, D), F32, kind="ExternalOutput").ap())
    hybrid_blocks(nc, *args)
    r = run_bass_kernel_spmd(nc, [arrays], core_ids=[0])
    return r.results[0]["out_x"]
```

```python
from contextlib import ExitStack

import numpy as np

import concourse.bass as bass
from concourse import mybir

F32 = mybir.dt.float32
F32R = mybir.dt.float32r
BF16 = mybir.dt.bfloat16
ALU = mybir.AluOpType
ACT = mybir.ActivationFunctionType
AX = mybir.AxisListType
LOG_EXP = "natural_log_exp_and_others"

P = 128
T = 256
NT = T // P
D = 1024
KD = D // P
L = 2
HD = 64
EPS = 1e-6
NEG = -1e30
SCALE = HD ** -0.5
M_SCALE = 128 ** -0.5
MH = 4
NC_CMP = 15
COLS1 = 3476
REST0 = 2048
RESTW = COLS1 - REST0
NVEC = 22
KMIX2 = 12
SLOTS = 4
UNIT = 1024
AHEAD = 3
ARENA = 10240
PROJ1 = [4, 5, 6, 0, 1, 2, 3]
PROJ2 = list(range(12))
FEATURE1 = (0, 1)
FEATURE2 = (4, 5, 8, 9)
LAM_INIT = [0.8 - 0.6 * float(np.exp(-0.3 * l)) for l in range(L)]

C_ID, C_CAUSAL, C_CHUNK, C_STRICT, C_LE, C_RTRI, C_ONES, C_NONES = (128 * n for n in range(8))
C_COS = 1024
C_SIN = C_COS + NT * 8
C_CNEG = C_SIN + NT * 8
C_C01 = C_CNEG + NT * NC_CMP
C_END = C_C01 + NT * NC_CMP


def constants():
    c = np.zeros((P, C_END), np.float32)
    a, b = np.arange(P)[:, None], np.arange(P)[None, :]
    c[:, C_ID:C_ID + P] = a == b
    c[:, C_CAUSAL:C_CAUSAL + P] = np.where(b > a, np.float32(NEG), 0)
    c[:, C_CHUNK:C_CHUNK + P] = np.where(b // 64 > a // 64, np.float32(NEG), 0)
    c[:, C_STRICT:C_STRICT + P] = np.where(a >= b, np.float32(NEG), 0)
    c[:, C_LE:C_LE + P] = a <= b
    c[:, C_RTRI:C_RTRI + P] = np.where(a >= b, -1, 0)
    c[:, C_ONES:C_ONES + P] = 1
    c[:, C_NONES:C_NONES + P] = -1
    freq = np.exp(np.float32(-np.log(500000.0)) * np.arange(8, dtype=np.float32) * np.float32(2.0 / 16))
    tok = (np.arange(NT)[None, :] * P + np.arange(P)[:, None]).astype(np.float32)
    ang = (tok[:, :, None] * freq.astype(np.float32)).astype(np.float32)
    c[:, C_COS:C_COS + NT * 8] = np.cos(ang).reshape(P, -1)
    c[:, C_SIN:C_SIN + NT * 8] = np.sin(ang).reshape(P, -1)
    seen = (np.arange(NC_CMP) * 16 + 31)[None, None, :] <= tok[:, :, None]
    c[:, C_CNEG:C_CNEG + NT * NC_CMP] = np.where(seen, 0, np.float32(NEG)).reshape(P, -1)
    c[:, C_C01:C_C01 + NT * NC_CMP] = seen.reshape(P, -1)
    sel = np.zeros((8, 8 * P), np.float32)
    for h in range(8):
        sel[h, h * P:(h + 1) * P] = 1
    return c, sel


def hybrid_blocks(nc, x, w_in, b_if, conv_qk, m_norm, moba_qk_norm, nsa_q_norm, nsa_k_norm, cmp_pe,
                  cmp_w1, cmp_w2, w_out, norm_mix, norm_ffn, w_ff1, w_ff2, w_in_2, forget_bias_2,
                  diff_lambda_2, diff_subln_2, w_out_2, pre_norm_2, post_norm_2, consts, selector, out):
    bank_of, nth, at_unit, uses = {}, {}, {}, [0] * 8
    units, unit_no = [], {}
    counts = {"unit": 0}
    timeline = [[[] for _ in range(L)] for _ in range(2)]
    steps = None
    R_ROWS = [2 * l for l in range(L)] + [4 + l for l in range(L)]

    def use(key, bank):
        bank_of[key], nth[key] = bank, uses[bank]
        uses[bank] += 1
        at_unit[key] = len(units)

    def done(key):
        at_unit[key] = len(units)

    def unit(key, src, split=True, closes=None, lo_on="vector", place=True):
        if closes is None:
            counts["unit"] += 1
        unit_no[key] = len(units)
        units.append(dict(key=key, src=src, split=split, closes=closes, n_done=counts["unit"], lo_on=lo_on))
        if place:
            steps.append(key)

    def step(*key):
        steps.append(key)

    def norm_turn(n, i, u):
        use(("norm", n, i, u), 4 + 2 * u + i)
        step("norm", n, i, u)

    def order_in_norm(n, i, u):
        return 2 * i + u if n == 5 else 2 * u + i

    def proj_unit(b, l, w, j, bp, q, cols, lo_on, place=True):
        n = min(512, cols - 512 * j)
        src = w[256 * q:256 * q + 256, 512 * j:512 * j + n].rearrange("(k p) c -> p k c", p=P)
        for i in range(2):
            if q == 0:
                use(("proj", b, l, j, i), 2 * (bp % 2) + i)
        unit(("proj", b, l, j, q), src, closes=("proj", b, l, j, 1) if q == 3 else None, lo_on=lo_on, place=place)
        if q == 3:
            done(("proj", b, l, j, 0))
            done(("proj", b, l, j, 1))

    def out_unit(name, w, f, first, last, place=True):
        if first:
            for a in range(4):
                use((*name, "acc", a), a)
        unit((*name, "unit", f), w[P * f:P * f + P, :].unsqueeze(1), closes=(*name, "acc", 3) if last else None, place=place)

    def tail(name, w, fs, n, order):
        first = len(units)
        for f in fs:
            out_unit(name, w, f, False, f == fs[-1], place=False)
        for c, a in enumerate(order):
            step("tail", *name, a)
            at_unit[(*name, "acc", a)] = first + 1 if c < 3 else len(units)
            if n is not None:
                step("to_norm", *name, a, n)
                if 1 <= c < 3:
                    norm_turn(n, order[c - 1] // 2, order[c - 1] % 2)
                    at_unit[steps[-1]] = first + 1
        if n is not None:
            norm_turn(n, order[2] // 2, order[2] % 2)

    def head_steps(name, h, stage, groups_of):
        if stage == "S":
            use((*name, "S", h), 4 + h % 2)
        elif stage == "T":
            use((*name, "T", h), 6)
        elif stage == "V":
            g, r = divmod(h, groups_of)
            if r == 0:
                use((*name, "O", g), 7)
            if r == groups_of - 1:
                done((*name, "O", g))
        step(*name, stage, h)

    def stick_steps(l, h, stage):
        if stage == "Z":
            use(("stick", l, "Z", h), 4 + h % 3)
        elif stage == "R":
            use(("stick", l, "R", h), 4 + h % 3)
        elif stage == "V":
            if h % 4 == 0:
                use(("stick", l, "O", h // 4), 7)
            if h % 4 == 3:
                done(("stick", l, "O", h // 4))
        step("stick", l, stage, h)

    def single(bank, *key):
        use(key, bank)
        step(*key)

    for l in range(L):
        steps = timeline[0][l]
        if l == 0:
            for (i, u), n in (((0, 0), -AHEAD), ((1, 0), -AHEAD), ((0, 1), 1 - AHEAD)):
                norm_turn(0, i, u)
                at_unit[steps[-1]] = n
        start = [13, 14, 15, 16] + list(range(18, 26))

        CONV_AT = {16: (0,), 17: (1, 2), 18: (3,), 20: (4,), 21: (5, 6), 22: (7,)}

        def heads1(p):
            for stage, lag in (("V", 4), ("T", 2), ("E", 1), ("S", 0)):
                for h in range(12):
                    if stage == "V" and h > 8:
                        lag = 3
                    if start[h] + lag == p:
                        head_steps(("att1", l), h, stage, 4)

        def m_scores(h, b):
            single(b, "mlstm", l, "S", h)

        def m_values(h, b):
            single(b, "mlstm", l, "O", h)

        def cmp_unit(v, half):
            w1 = cmp_w1[l, v].rearrange("(a p) e -> p a e", p=P)
            unit(("cmp", l, v, half), w1[:, 8 * half:8 * half + 8, :], split=False,
                 closes=("hidden", l) if v and half else None)

        for bp, j in enumerate(PROJ1):
            for q in range(4):
                p = 4 * bp + q
                if p == 1:
                    norm_turn(2 * l, 1, 1)
                proj_unit(0, l, w_in[l], j, bp, q, COLS1, "pool" if (p % 3 and p >= 13) or p in (9, 11) else "vector")
                if q == 3:
                    step("evac", 0, l, j)
                heads1(p)
                if p == 1:
                    step("stats", 2 * l)
                if p == 3:
                    if l == 0:
                        single(2, "params")
                    step("gate_log", l)
                if p == 5:
                    single(0, "gate_sum", l)
                if p == 6:
                    single(1, "r_row", 2 * l)
                    single(0, "gate_row", l)
                if p == 7:
                    step("vec_a", l, 0)
                if p == 8:
                    single(2, "m_col", l)
                    step("vec_a", l, 1)
                if p == 9:
                    single(3, "m_rows", l, 0)
                    step("vec_a", l, 2)
                if p == 11:
                    step("vec_b", l, "copy")
                if p == 12:
                    single(4, "turn", l, 0)
                    single(5, "turn", l, 1)
                    step("vec_b", l, 0)
                    step("m_exp", l, 0)
                if p == 13:
                    single(0, "turn", l, 4)
                    step("vec_b", l, 1)
                    single(1, "m_rows", l, 1)
                if p == 14:
                    step("vec_b", l, 2)
                    step("m_exp", l, 1)
                if p == 15:
                    step("vec_b", l, 3)
                if p == 16:
                    use(("hidden", l), 2)
                    cmp_unit(0, 0)
                if p == 17:
                    single(3, "turn", l, 2)
                    cmp_unit(0, 1)
                    cmp_unit(1, 0)
                    single(3, "turn", l, 3)
                if p == 18:
                    cmp_unit(1, 1)
                    done(("hidden", l))
                    single(3, "turn", l, 5)
                    step("hidden", l)
                if p == 20:
                    single(0, "cmp_kv", l)
                if p == 21:
                    single(1, "cmp_kT", l)
                    single(0, "mix_turn", 0, l, 2)
                if p == 22:
                    single(0, "cmp_s", l, 0)
                    single(1, "cmp_s", l, 1)
                    step("cmp_soft", l)
                if p == 24:
                    single(3, "cmp_pT", l)
                if p == 25:
                    single(3, "cmp_o", l)
                    m_scores(0, 2)
                if p == 26:
                    m_scores(1, 2)
                    m_values(0, 3)
                if p == 27:
                    m_scores(2, 4)
                    m_values(1, 5)
                for c in CONV_AT.get(p, ()):
                    step("conv", l, c)
                if p == 23:
                    step("conv_silu", l)
        for p, f in enumerate((4, 5, 6, 7, 0), 28):
            out_unit(("out", 0, l), w_out[l], f, f == 4, False)
            heads1(p)
            if p == 28:
                m_scores(3, 4)
                m_values(2, 5)
            if p == 29:
                single(6, "mix_turn", 0, l, 3)
                m_values(3, 5)
                step("mlstm_end", l, 0)
            if p == 30:
                step("mlstm_end", l, 1)
            if p == 31:
                single(7, "mix_turn", 0, l, 0)
                single(5, "mix_turn", 0, l, 1)
        tail(("out", 0, l), w_out[l], (1, 2, 3), 2 * l + 1, (0, 2, 1, 3))

        def ff1(t):
            for i in range(2):
                use(("ff1", l, t, i), 4 + 2 * (t % 2) + i)
            for q in range(4):
                if t == 0 and q == 1:
                    norm_turn(2 * l + 1, 1, 1)
                if t == 0 and q == 2:
                    step("stats", 2 * l + 1)
                src = w_ff1[l][256 * q:256 * q + 256, 512 * t:512 * t + 512].rearrange("(k p) c -> p k c", p=P)
                unit(("ff1", l, t, q), src, closes=("ff1", l, t, 1) if q == 3 else None)
            for i in range(2):
                done(("ff1", l, t, i))
            step("square", l, t)

        def ff2(t):
            for f in range(4 * t, 4 * t + (4 if t < 7 else 1)):
                out_unit(("ff2", l), w_ff2[l], f, f == 0, False)

        ff1(0)
        for t in range(1, 8):
            ff1(t)
            ff2(t - 1)
        ff2(7)
        tail(("ff2", l), w_ff2[l], (29, 30, 31), 2 * l + 2, (0, 2, 1, 3))

    for l in range(L):
        steps = timeline[1][l]
        if l > 0:
            norm_turn(5, 0, 0)
            norm_turn(5, 0, 1)
            first = len(units)
            for q in range(3):
                proj_unit(1, l, w_in_2[l], 0, 0, q, 6144, "vector", place=False)
            step("proj_tile", 1, l, 0)
            step("post_norm", l - 1, 1)
            for u in range(2):
                norm_turn(5, 1, u)
                at_unit[steps[-1]] = first + 1
            step("proj_tile", 1, l, 1)

        V_LAG = {"diff": 4, "fox": 3}

        def side2(p):
            for name, first, sp, groups_of in ((("diff", l), 12, 1.5, 2), (("fox", l), 41, 1.25, 4)):
                for stage, lag in (("V", V_LAG[name[0]]), ("T", 2), ("E", 1), ("S", 0)):
                    for h in range(8):
                        if int(first + sp * h) + lag == p:
                            head_steps(name, h, stage, groups_of)
            for stage, lag in (("V", 4), ("R", 3), ("K", 1), ("Z", 0)):
                for h in range(8):
                    if int(26 + 1.5 * h) + lag == p:
                        stick_steps(l, h, stage)
            if p == 1:
                step("stats", 4 + l)
            if p == 5:
                single(0, "r_row", 4 + l)
            if p == 6:
                single(1, "forget_f", l)
                step("forget_log", l)
            if p == 8:
                step("rope2", l)
            if p == 11:
                for u in range(4):
                    single(4 + u, "turn2", l, u)
            if p == 44:
                for i in range(NT):
                    single(i, "mix_turn", 1, l, 0, i)
            if p == 46:
                for i in range(NT):
                    single(i, "mix_turn", 1, l, 1, i)
            if p == 54:
                for i in range(NT):
                    single(4 + i, "mix_turn", 1, l, 2, i)

        for bp, j in enumerate(PROJ2):
            for q in range(4):
                if l == 0 and bp == 0 and q == 1:
                    norm_turn(4, 1, 1)
                if l == 0 or bp or q == 3:
                    proj_unit(1, l, w_in_2[l], j, bp, q, 6144, "vector")
                if q == 3:
                    step("evac", 1, l, j)
                side2(4 * bp + q)
        for f in range(KMIX2 - 3):
            out_unit(("out", 1, l), w_out_2[l], f, f == 0, False)
            side2(48 + f)
        tail(("out", 1, l), w_out_2[l], (9, 10, 11), None, (0, 1, 2, 3))
        step("post_norm", l, 0)
        if l + 1 == L:
            step("post_norm", l, 1)

    seen = {"vector": 0, "pool": 0, "hi": 0}
    for u in units:
        if u["split"]:
            seen["hi"] += 1
            seen[u["lo_on"]] += 1
            u["n_hi"], u["n_lo"] = seen["hi"], seen[u["lo_on"]]

    with ExitStack() as ctx:
        def sb(name, shape, dt=F32):
            return ctx.enter_context(nc.sbuf_tensor(name, shape, dt))

        def sem(name):
            return ctx.enter_context(nc.semaphore(name))

        bank = [ctx.enter_context(nc.psum_tensor(f"bank{b}", [P, 512], F32)) for b in range(8)]
        bank_filled = [sem(f"bank_filled{b}") for b in range(8)]
        bank_freed = [sem(f"bank_freed{b}") for b in range(8)]

        raw = sb("raw", [P, SLOTS, UNIT])
        w_hi = sb("w_hi", [P, SLOTS, UNIT], F32R)
        w_lo = sb("w_lo", [P, SLOTS, UNIT], F32R)
        h_hi = sb("h_hi", [P, KD, T], F32R)
        h_lo = sb("h_lo", [P, KD, T], F32R)
        const = sb("const", [P, C_END])
        sel = sb("sel", [8, 8 * P], F32R)
        masks = sb("masks", [P, 4 * P], BF16)
        x_sb = sb("x_sb", [P, NT, D])
        xn = sb("xn", [P, NT, D])
        mix = sb("mix", [P, NT, KMIX2 * P])
        gain = sb("gain", [P, D])
        arena = sb("arena", [P, ARENA])
        arena_at = nc.sbuf_base - 4 * ARENA
        vecs = sb("vecs", [P, 2 * 3072])
        vecs_at = nc.sbuf_base - 4 * 2 * 3072
        vec = vecs[:, 0:3072].rearrange("p (i s d) -> p i s d", i=NT, d=HD)
        vecT = vecs[:, 3072:6144].rearrange("p (s t) -> p s t", t=T)
        probs = sb("probs", [P, 3, 384])
        probsT = sb("probsT", [P, 3, 384])
        prm = sb("prm", [P, 128])
        bif = sb("bif", [P, L, 8])
        g_vec = sb("g_vec", [P, L, 6, HD])
        m_gain = sb("m_gain", [P, L, 512])
        w2c = sb("w2c", [P, L, 2, HD])
        ff_w = sb("ff_w", [P, L * KD * 8])
        ff_hi = sb("ff_hi", [P, L, KD, 8], F32R)
        ff_lo = sb("ff_lo", [P, L, KD, 8], F32R)
        f_bias = sb("f_bias", [8, L])
        lam_v = sb("lam_v", [P, L, 4, HD])
        sub_gain = sb("sub_gain", [P, L, P])
        blocksT = sb("blocksT", [P, 2, 16, NC_CMP])
        kc_n = sb("kc_n", [NC_CMP, 2, HD])
        kcT = sb("kcT", [P, NC_CMP])
        vc_diag = sb("vc_diag", [P, 4, HD])
        p_cmp = sb("p_cmp", [P, NT, 4, 32])
        hid = sb("hid", [P, 2, 2, 16])
        small = sb("small", [P, 512])
        rows = sb("rows", [8, 3, T])
        suffix = sb("suffix", [P, 2, P], F32R)
        row_hi = sb("row_hi", [8, T], F32R)
        row_lo = sb("row_lo", [8, T], F32R)
        o_tmp = sb("o_tmp", [P, 512])
        flag = sb("flag", [P, 2])
        sq_out = sb("sq_out", [P, P])
        r_row = sb("r_row", [P, T])
        at = [0]

        def shaped(a, shape):
            if len(shape) == 1:
                return a
            names = "abcd"[:len(shape)]
            return a.rearrange(f"p ({' '.join(names)}) -> p {' '.join(names)}", **{names[k]: shape[k] for k in range(1, len(shape))})

        def few(*shape):
            n = int(np.prod(shape))
            a = small[:, at[0]:at[0] + n]
            at[0] += n
            return shaped(a, shape)

        def part(lo, *shape):
            return shaped(arena[:, lo:lo + int(np.prod(shape))], shape)

        def exact(name, base, lo, *shape):
            return nc.alloc_sbuf_tensor_at(name, [P, *shape], F32R, offset=base + 4 * lo)

        ss, ms, rstd = few(3 * L, NT), few(3 * L, NT), few(3 * L, NT)
        y_sum, y_mean, y_rs = few(NT), few(NT), few(NT)
        half_neg = few(8)
        v_ss, v_ms, v_r, v_t = few(NT, NVEC), few(NT, NVEC), few(NT, NVEC), few(NT, NVEC)
        gif, g_e, g_lf, g_F, g_a, m_tok, e_m, m_den = (few(NT, 8) for _ in range(8))
        n_gate = few(NT, 12)
        row_nb, row_mx = few(2, NT), few(2, NT)
        row_sum, row_inv = few(2, 4, NT), few(4, NT)
        kc_s = few(4)
        c_mx, c_sum = few(NT, 4), few(NT, 4)
        h_ss, h_ms, h_rs = few(NT, MH), few(NT, MH), few(NT, MH)
        lam, y_ss = few(4), few(4)

        r_diag = part(6144, NT, P)
        rest = part(0, NT, RESTW)
        squares = part(2856, NT, NVEC, HD)
        conv_in = part(2856, KD, T + 3)
        h_num = part(2856, NT, MH, 129)
        m_probs = part(3888, 2, 384)
        p_cmpT = part(4928, NT, P)
        intra = part(5672, MH, 384)
        o_gate = part(7208, NT, MH, P)
        v_aug = part(8232, NT, MH, 130)
        m_qk = xn[:, :, :].rearrange("p i (c t) -> p (i c) t", t=T)
        u_hi = [exact(f"u_hi{b}", arena_at, 2048 * b, 4, T) for b in range(2)]
        u_lo = [exact(f"u_lo{b}", arena_at, 2048 * b + 1024, 4, T) for b in range(2)]
        u_full = part(4096, 2, 512)
        relu = part(5120, 2, 512)
        mixT1_hi = [exact(f"mixT1_hi{g}", arena_at, lo, 4, T) for g, lo in enumerate((2856, 0))]
        mixT1_lo = [exact(f"mixT1_lo{g}", arena_at, lo, 4, T) for g, lo in enumerate((3880, 1440))]
        values = part(0, 3, NT, 512)
        gates = part(3072, NT, 3, 512)
        featT = part(6144, 16, T)
        y_diff = xn[:, :, 0:512].rearrange("p i (h d) -> p i h d", d=P)
        y_tmp = xn[:, :, 512:1024].rearrange("p i (h d) -> p i h d", d=P)
        mixT_hi = [exact("mixT_hi0", vecs_at, 3072, 4, T), exact("mixT_hi1", arena_at, 6144, 4, T), h_hi]
        mixT_lo = [exact("mixT_lo0", vecs_at, 4096, 4, T), exact("mixT_lo1", arena_at, 7168, 4, T), h_lo]
        softp = vecs[:, 3072 + 2048:3072 + 2048 + 768].rearrange("p (b t) -> p b t", b=2)
        keep_hi, keep_lo = exact("keep_hi", vecs_at, 0, 2, 384), exact("keep_lo", vecs_at, 768, 2, 384)
        post_gain = vecs[:, 1536:1536 + D]
        prm_rows = o_tmp[:, 0:2 * P]

        ident = const[:, C_ID:C_ID + P]
        ident_b, causal_b, chunk_b, strict_b = (masks[:, n * P:(n + 1) * P] for n in range(4))

        def conv_col(l, tap, c):
            n = (l * 4 + tap) * 8 + c
            return prm[:, n:n + 1]

        raw_arrived = [sem(f"raw_arrived{s}") for s in range(SLOTS)]
        unit_done = sem("unit_done")
        hi_ready = sem("hi_ready")
        lo_ready = {"vector": sem("lo_ready_vector"), "pool": sem("lo_ready_pool")}
        x_loaded = [sem(f"x_loaded{h}") for h in range(2)]
        prm_loaded, prm_rows_loaded, post_loaded = sem("prm_loaded"), sem("prm_rows_loaded"), sem("post_loaded")
        const_loaded, ident_loaded, gain_loaded = sem("const_loaded"), sem("ident_loaded"), sem("gain_loaded")
        diag_ready = sem("diag_ready")
        half_neg_set = sem("half_neg_set")
        out_stored = sem("out_stored")
        vector_step, scalar_step, pool_step = sem("vector_step"), sem("scalar_step"), sem("pool_step")
        x_tile_ready, sumsq_ready, rstd_ready, xn_ready = sem("x_tile_ready"), sem("sumsq_ready"), sem("rstd_ready"), sem("xn_ready")
        turned_hi = sem("turned_hi")
        gate_abs, gate_log = sem("gate_abs"), sem("gate_log")
        squared, vec_ms, vec_rstd, vec_ready = sem("squared"), sem("vec_ms"), sem("vec_rstd"), sem("vec_ready")
        logf_ready, a_ready, m_ready = sem("logf_ready"), sem("a_ready"), sem("m_ready")
        conv_done, conv_silu = sem("conv_done"), sem("conv_silu")
        exponent_ready, intra_exp, intra_masked = sem("exponent_ready"), sem("intra_exp"), sem("intra_masked")
        m_col_ready, stabilizer = sem("m_col_ready"), sem("stabilizer")
        blocks_ready, hid_exp, hid_ready = sem("blocks_ready"), sem("hid_exp"), sem("hid_ready")
        kc_ms, kc_rstd, kc_ready = sem("kc_ms"), sem("kc_rstd"), sem("kc_ready")
        cmp_shifted, cmp_exp, cmp_ready = sem("cmp_shifted"), sem("cmp_exp"), sem("cmp_ready")
        nsa_exp, o_gained = sem("nsa_exp"), sem("o_gained")
        max_ready = sem("max_ready")
        h_ms_ready, h_rstd_ready = sem("h_ms_ready"), sem("h_rstd_ready")
        diff_mixed = sem("diff_mixed")
        mix_ready = sem("mix_ready")
        u_hi_ready, u_ready = sem("u_hi_ready"), sem("u_ready")
        keep_ready = sem("keep_ready")
        copied, sel_ready = sem("copied"), sem("sel_ready")
        lam_dots, lam_exp = sem("lam_dots"), sem("lam_exp")
        stick_log = sem("stick_log")
        y_sumsq, y_ms, y_rstd = sem("y_sumsq"), sem("y_ms"), sem("y_rstd")

        def filled(eng, key):
            eng.wait_ge(bank_filled[bank_of[key]], nth[key] + 1)

        def drained(eng, key):
            eng.wait_ge(bank_freed[bank_of[key]], nth[key] + 1)

        def released(eng, n):
            u = units[n]
            if u["closes"] is None:
                eng.wait_ge(unit_done, u["n_done"])
            else:
                filled(eng, u["closes"])

        def slot(store, u):
            n, k, c = unit_no[u["key"]], u["src"].shape[1], u["src"].shape[2]
            return store[:, n % SLOTS, 0:k * c].rearrange("p (k c) -> p k c", c=c)

        def heads_of(kind, l):
            def pair(t, p, h):
                b = HD * (h % 2)
                return t[b:b + HD, p, :]

            if kind == "att1":
                def col(c):
                    return lambda i: rest[:, i, c:c + HD]
                moba = [(pair(vecT, h // 2, h), pair(vecT, 2 + h // 2, h), causal_b, col(520 + HD * h), HD, None) for h in range(4)]
                nsa = [(pair(vecT, 4 + h // 2, h), pair(vecT, p, h), causal_b, col(c), HD, None)
                       for p, c in ((6, 1224), (7, 1352)) for h in range(4)]
                return moba + nsa
            if kind == "diff":
                return [(pair(vecT, h // 2, h), pair(vecT, 4 + h // 2, h), chunk_b,
                         (lambda c: lambda i: values[:, 0, i, c:c + P])(P * (h // 2)), P, None) for h in range(8)]
            return [(pair(featT, 8 + h // 2, h), pair(featT, 12 + h // 2, h), causal_b,
                     (lambda c: lambda i: values[:, 2, i, c:c + HD])(HD * h), HD, h) for h in range(8)]

        GROUPS = {"att1": 4, "diff": 2, "fox": 4}

        block = ctx.enter_context(nc.Block())

        @block.sync
        def _(sp):
            def wide(a):
                return a.partition_broadcast(P)

            def load_parameters():
                sp.dma_start(const[:, C_ID + P:C_END], consts[:, C_ID + P:C_END]).then_inc(const_loaded, 16)
                sp.dma_start(mix[0:8, :, D:D + 512], selector.rearrange("h (i c) -> h i c", i=NT)).then_inc(const_loaded, 16)
                row_loads = [(prm_rows[0:64, 0:P], conv_qk.rearrange("l w (k p) -> (l w k) p", p=P)),
                             (prm_rows[0:64, P:2 * P], cmp_pe.rearrange("l v (a b) d -> (l v a) (b d)", b=2))]
                assert len(row_loads) == PRM_ROW_LOADS
                for dst, a in row_loads:
                    sp.dma_start(dst, a).then_inc(prm_rows_loaded, 16)
                loads = [(bif[:, :, :], wide(b_if)),
                         (g_vec[:, :, 0:2, :], wide(moba_qk_norm)), (g_vec[:, :, 2, :], wide(nsa_q_norm)),
                         (g_vec[:, :, 3:6, :], wide(nsa_k_norm)), (m_gain[:, :, :], wide(m_norm)),
                         (w2c[:, :, :, :], cmp_w2.rearrange("l v e d -> e l v d")),
                         (lam_v[:, :, :, :], wide(diff_lambda_2)),
                         (sub_gain[:, :, :], wide(diff_subln_2))]
                loads += [(f_bias[:, l:l + 1], forget_bias_2[l].unsqueeze(1)) for l in range(L)]
                loads += [(ff_w[:, 64 * l:64 * l + 64].rearrange("p (k c) -> p k c", c=8),
                           w_in_2[l][:, 6144:6152].rearrange("(k p) c -> p k c", p=P)) for l in range(L)]
                assert len(loads) == PRM_LOADS
                for dst, a in loads:
                    sp.dma_start(dst, a).then_inc(prm_loaded, 16)

            for half in range(2):
                c = slice(half * 512, half * 512 + 512)
                sp.dma_start(x_sb[:, :, c], x.rearrange("b (i p) d -> p (b i) d", p=P)[:, :, c]).then_inc(x_loaded[half], 16)
            for n, u in enumerate(units):
                if n >= SLOTS:
                    old = units[n - SLOTS]
                    if old["split"]:
                        sp.wait_ge(lo_ready[old["lo_on"]], old["n_lo"])
                    else:
                        released(sp, n - SLOTS)
                sp.dma_start(slot(raw, u), u["src"]).then_inc(raw_arrived[n % SLOTS], 16)
                if n == SLOTS - 1:
                    load_parameters()
            for i in range(NT):
                sp.wait_ge(x_tile_ready, NT * (3 * L - 1) + i + 1)
                sp.dma_start(out[0, i * P:(i + 1) * P, :], x_sb[:, i, :]).then_inc(out_stored, 16)
            sp.wait_ge(out_stored, 16 * NT)

        @block.tensor
        def _(pe):
            def open_bank(key):
                if nth[key]:
                    pe.wait_ge(bank_freed[bank_of[key]], nth[key])
                return bank[bank_of[key]]

            def close(mm, key):
                mm.then_inc(bank_filled[bank_of[key]], 1)

            def weights(key):
                u = units[unit_no[key]]
                pe.wait_ge(lo_ready[u["lo_on"]], u["n_lo"])
                return slot(w_hi, u), slot(w_lo, u)

            def finish_unit(mm, key):
                if units[unit_no[key]]["closes"] is None:
                    mm.then_inc(unit_done, 1)
                else:
                    close(mm, units[unit_no[key]]["closes"])

            def exact_product(out_ap, stat, mov, start, stop, **kw):
                (s_hi, s_lo), (m_hi, m_lo) = stat, mov
                pe.matmul(out_ap, s_hi, m_hi, start=start, stop=False, **kw)
                pe.matmul(out_ap, s_hi, m_lo, start=False, stop=False, **kw)
                return pe.matmul(out_ap, s_lo, m_hi, start=False, stop=stop, **kw)

            def features_there(n):
                def there(i, k):
                    drained(pe, ("norm", n, i, k // 4))
                return there

            def token_products(key, uses_of, q, there, i):
                hi, lo = weights(key)
                n = hi.shape[2]
                ps = open_bank(uses_of[i]) if q == 0 else bank[bank_of[uses_of[i]]]
                for kk in range(2):
                    k = 2 * q + kk
                    if there and k % 4 == 0:
                        there(i, k)
                    t = slice(i * P, (i + 1) * P)
                    mm = exact_product(ps[:, 0:n], (h_hi[:, k, t], h_lo[:, k, t]), (hi[:, kk, :], lo[:, kk, :]),
                                       k == 0, k == KD - 1)
                return mm

            def token_unit(key, uses_of, q, there):
                for i in range(NT):
                    mm = token_products(key, uses_of, q, there, i)
                    if q == 3 and i == 0:
                        close(mm, uses_of[0])
                finish_unit(mm, key)

            def feature_unit(key, uses_of, q, there):
                hi, lo = weights(key)
                for c in range(4):
                    ps = open_bank(uses_of[c // 2]) if q == 0 and c % 2 == 0 else bank[bank_of[uses_of[c // 2]]]
                    for kk in range(2):
                        k = 2 * q + kk
                        if there and k % 4 == 0 and c == 0:
                            there(0, k)
                            there(1, k)
                        f = slice(c * P, (c + 1) * P)
                        mm = exact_product(ps[:, (c % 2) * T:(c % 2 + 1) * T], (hi[:, kk, f], lo[:, kk, f]),
                                           (h_hi[:, k, :], h_lo[:, k, :]), k == 0 and c % 2 == 0, k == KD - 1,
                                           skip_group_check=True)
                    if q == 3 and c == 1:
                        close(mm, uses_of[0])
                finish_unit(mm, key)

            def out_unit_products(key, name, hi_f, lo_f, first, last=False, accs=range(4)):
                hi, lo = weights(key)
                for a in accs:
                    i, half = divmod(a, 2)
                    ps = open_bank((*name, "acc", a)) if first else bank[bank_of[(*name, "acc", a)]]
                    t, c = slice(i * P, (i + 1) * P), slice(half * 512, (half + 1) * 512)
                    mm = exact_product(ps[:, :], (hi_f[:, t], lo_f[:, t]), (hi[:, 0, c], lo[:, 0, c]), first, last)
                return mm

            def tail_products(name, a, features):
                for f, hi_f, lo_f in features:
                    key = (*name, "unit", f)
                    last = f == features[-1][0]
                    mm = out_unit_products(key, name, hi_f, lo_f, False, last, (a,))
                    if a == 3:
                        finish_unit(mm, key)
                    elif last:
                        close(mm, (*name, "acc", a))

            def turn(key, src, chunks):
                ps = open_bank(key)
                for n, (k, i) in enumerate(chunks):
                    mm = pe.transpose(ps[:, n * P:(n + 1) * P], src[:, i, k * P:(k + 1) * P], ident)
                close(mm, key)

            def running_sum(key, src, n):
                ps = open_bank(key)
                le, ones = const[:, C_LE:C_LE + P], const[:, C_ONES:C_ONES + P]
                pe.matmul(ps[:, 0:n], le, src[:, 0, 0:n], start=True, stop=True)
                pe.matmul(ps[:, n:2 * n], ones, src[:, 0, 0:n], start=True, stop=False)
                close(pe.matmul(ps[:, n:2 * n], le, src[:, 1, 0:n], start=False, stop=True), key)

            def head_inputs(kind, l, stage, h):
                both = range(NT)
                inputs = {
                    ("att1", "S", 0): [("turn", l, 0), ("turn", l, 1)],
                    ("att1", "S", 4): [("turn", l, 2), ("turn", l, 3)],
                    ("att1", "V", 0): [("proj", 0, l, j, i) for j in (5, 6) for i in both],
                    ("diff", "S", 0): [("turn2", l, u) for u in range(4)],
                    ("diff", "V", 0): [("proj", 1, l, 2, i) for i in both],
                    ("stick", "Z", 0): [("proj", 1, l, j, i) for j in (4, 5) for i in both],
                    ("stick", "V", 0): [("proj", 1, l, 6, i) for i in both],
                    ("fox", "S", 0): [("proj", 1, l, j, i) for j in (8, 9) for i in both],
                    ("fox", "V", 0): [("proj", 1, l, 10, i) for i in both]}
                for key in inputs.get((kind, stage, h), []):
                    drained(pe, key)
                if (kind, stage, h) == ("fox", "S", 0):
                    pe.wait_ge(a_ready, L + l + 1)

            def head_stage(kind, l, stage, h):
                name = (kind, l)
                if stage == "E":
                    return
                head_inputs(kind, l, stage, h)
                q, k, mask, value, width, extra = heads_of(kind, l)[h]
                if stage == "S":
                    ps = open_bank((*name, "S", h))
                    for lo, i in ((0, 0), (P, 1)):
                        cols = (i + 1) * P
                        pe.matmul(ps[:, lo:lo + cols], q[:, i * P:(i + 1) * P], k[:, 0:cols], start=True, stop=False)
                        if extra is not None:
                            for row_part in (row_hi, row_lo):
                                pe.matmul(ps[:, lo:lo + cols], sel[0:8, extra * P:(extra + 1) * P], row_part[0:8, 0:cols],
                                          start=False, stop=False)
                        mm = pe.matmul(ps[:, lo + cols - P:lo + cols], ident_b, mask, start=False, stop=True)
                    close(mm, (*name, "S", h))
                elif stage == "T":
                    drained(pe, (*name, "S", h))
                    ps = open_bank((*name, "T", h))
                    for b in range(3):
                        mm = pe.transpose(ps[:, b * P:(b + 1) * P], probs[:, h % 3, b * P:(b + 1) * P], ident)
                    close(mm, (*name, "T", h))
                else:
                    g, r = divmod(h, GROUPS[kind])
                    drained(pe, (*name, "T", h))
                    ps = open_bank((*name, "O", g)) if r == 0 else bank[bank_of[(*name, "O", g)]]
                    lo = r * 2 * width
                    pe.matmul(ps[:, lo:lo + width], probsT[:, h % 3, 0:P], value(0), start=True, stop=True)
                    pe.matmul(ps[:, lo + width:lo + 2 * width], probsT[:, h % 3, P:2 * P], value(0), start=True, stop=False)
                    mm = pe.matmul(ps[:, lo + width:lo + 2 * width], probsT[:, h % 3, 2 * P:3 * P], value(1), start=False, stop=True)
                    if r == GROUPS[kind] - 1:
                        close(mm, (*name, "O", g))

            def turn_normed(s):
                _, n, i, u = s
                pe.wait_ge(xn_ready, 4 * n + order_in_norm(n, i, u) + 1)
                turn(s, xn, [(4 * u + c, i) for c in range(4)])

            def factor_row(s):
                pe.wait_ge(diag_ready, R_ROWS.index(s[1]) + 1)
                ps = open_bank(s)
                for i in range(NT):
                    mm = pe.matmul(ps[:, i * P:(i + 1) * P], const[:, C_ONES:C_ONES + P], r_diag[:, i, :], start=True, stop=True)
                close(mm, s)

            pe.wait_ge(ident_loaded, 16)

            for l in range(L):
                n0 = 2 * l
                for s in timeline[0][l]:
                    kind = s[0]
                    if kind == "norm":
                        turn_normed(s)
                    elif kind == "r_row":
                        factor_row(s)
                    elif kind == "proj":
                        _, b, _, j, q = s
                        both = [("proj", b, l, j, i) for i in range(2)]
                        there = features_there(n0) if j == PROJ1[0] else None
                        (feature_unit if j in FEATURE1 else token_unit)(s, both, q, there)
                    elif kind == "params":
                        pe.wait_ge(const_loaded, 32)
                        pe.wait_ge(prm_rows_loaded, 16 * PRM_ROW_LOADS)
                        ps = open_bank(s)
                        pe.transpose(ps[:, 0:64], prm_rows[0:64, 0:P], const[0:64, C_ID:C_ID + 64])
                        close(pe.transpose(ps[:, 64:128], prm_rows[0:64, P:2 * P], const[0:64, C_ID:C_ID + 64]), s)
                    elif kind == "gate_sum":
                        pe.wait_ge(logf_ready, l + 1)
                        running_sum(s, g_lf, 4)
                    elif kind == "gate_row":
                        pe.wait_ge(a_ready, l + 1)
                        ps = open_bank(s)
                        for i in range(NT):
                            mm = pe.transpose(ps[0:4, i * P:(i + 1) * P], g_a[:, i, 0:4], ident)
                        close(mm, s)
                    elif kind == "turn":
                        if s[2] == 4:
                            pe.wait_ge(copied, l + 1)
                        else:
                            pe.wait_ge(vec_ready, 2 * l + (1 if s[2] < 2 else 2))
                        turn(s, vec[:, :, :, :].rearrange("p i s d -> p i (s d)"),
                             [(2 * s[2] + c, i) for c in range(2) for i in range(NT)])
                    elif kind == "m_col":
                        pe.wait_ge(m_ready, l + 1)
                        ps = open_bank(s)
                        for i in range(NT):
                            mm = pe.transpose(ps[:, 4 * i:4 * i + 4], rows[0:4, 1, i * P:(i + 1) * P], ident[0:4, 0:4])
                        close(mm, s)
                    elif kind == "m_rows":
                        if l == 0 and s[2] == 0:
                            pe.wait_ge(sel_ready, 1)
                        ps = open_bank(s)
                        for c in range(2):
                            h = 2 * s[2] + c
                            pe.matmul(ps[:, c * T:(c + 1) * T], sel[0:4, h * P:(h + 1) * P], row_hi[0:4, :],
                                      start=True, stop=False)
                            mm = pe.matmul(ps[:, c * T:(c + 1) * T], sel[0:4, h * P:(h + 1) * P], row_lo[0:4, :],
                                           start=False, stop=True)
                        close(mm, s)
                    elif kind == "cmp":
                        _, _, v, half = s
                        u = units[unit_no[s]]
                        if v == 0 and half == 0:
                            ps = open_bank(("hidden", l))
                            pe.wait_ge(blocks_ready, l + 1)
                        pe.wait_ge(raw_arrived[unit_no[s] % SLOTS], 16 * (unit_no[s] // SLOTS + 1))
                        w = slot(raw, u)
                        for a in range(8):
                            mm = pe.matmul(ps[:, 16 * v:16 * v + NC_CMP], w[:, a, :], blocksT[:, v, 8 * half + a, :],
                                           start=(half == 0 and a == 0), stop=(half == 1 and a == 7))
                        finish_unit(mm, s)
                    elif kind == "cmp_kv":
                        ps = open_bank(s)
                        pe.wait_ge(hid_ready, l + 1)
                        for v in range(2):
                            mm = pe.matmul(ps[0:NC_CMP, v * HD:(v + 1) * HD], hid[:, 1, v, 0:NC_CMP], w2c[:, l, v, :],
                                           start=True, stop=True)
                        close(mm, s)
                    elif kind == "cmp_kT":
                        ps = open_bank(s)
                        pe.wait_ge(kc_ready, l + 1)
                        close(pe.transpose(ps[:, 0:NC_CMP], kc_n[:, :, :].rearrange("c r d -> c (r d)"),
                                           ident[0:NC_CMP, 0:NC_CMP]), s)
                    elif kind == "cmp_s":
                        if s[2] == 0:
                            drained(pe, ("turn", l, 5))
                            drained(pe, ("cmp_kT", l))
                        ps = open_bank(s)
                        b = HD * s[2]
                        for i in range(NT):
                            for h in range(2):
                                lo = (i * 2 + h) * 16
                                mm = pe.matmul(ps[:, lo:lo + NC_CMP], vecT[b:b + HD, 10 + h, i * P:(i + 1) * P],
                                               kcT[b:b + HD, :], start=True, stop=True)
                        close(mm, s)
                    elif kind == "cmp_pT":
                        ps = open_bank(s)
                        pe.wait_ge(cmp_ready, l + 1)
                        for i in range(NT):
                            mm = pe.transpose(ps[:, i * P:(i + 1) * P], p_cmp[:, i, :, :].rearrange("p h c -> p (h c)"), ident)
                        close(mm, s)
                    elif kind == "cmp_o":
                        drained(pe, ("cmp_pT", l))
                        ps = open_bank(s)
                        for i in range(NT):
                            mm = pe.matmul(ps[:, i * T:(i + 1) * T], p_cmpT[:, i, :],
                                           vc_diag[:, :, :].rearrange("p h d -> p (h d)"), start=True, stop=True)
                        close(mm, s)
                    elif kind == "mlstm" and s[2] == "S":
                        h = s[3]
                        if h == 0:
                            pe.wait_ge(conv_silu, l + 1)
                        q, k = m_qk[:, h, :], m_qk[:, MH + h, :]
                        ps = open_bank(s)
                        pe.matmul(ps[:, 0:T], k[:, 0:P], q, start=True, stop=True)
                        close(pe.matmul(ps[:, T:T + P], k[:, P:T], q[:, P:T], start=True, stop=True), s)
                    elif kind == "mlstm":
                        h = s[3]
                        drained(pe, ("mlstm", l, "S", h))
                        if h == 0:
                            drained(pe, ("proj", 0, l, 2, 0))
                            drained(pe, ("proj", 0, l, 2, 1))
                        ps = open_bank(s)
                        p = m_probs[:, h % 2, :]
                        pe.matmul(ps[:, 0:129], p[:, 0:P], v_aug[:, 0, h, 0:129], start=True, stop=True)
                        pe.matmul(ps[:, 129:258], p[:, P:T], v_aug[:, 0, h, 0:129], start=True, stop=False)
                        close(pe.matmul(ps[:, 129:258], p[:, T:T + P], v_aug[:, 1, h, 0:129], start=False, stop=True), s)
                    elif kind == "att1":
                        head_stage(kind, l, s[2], s[3])
                    elif kind == "mix_turn":
                        pair = s[3]
                        pe.wait_ge(mix_ready, 3 * l + {2: 1, 3: 2, 0: 3, 1: 3}[pair])
                        turn(s, mix, [(2 * pair + c, i) for c in range(2) for i in range(NT)])
                    elif kind == "out":
                        f = s[4]
                        if f % 2 == 0:
                            drained(pe, ("mix_turn", 0, l, f // 2))
                        finish_unit(out_unit_products(s, ("out", 0, l), mixT1_hi[f // 4][:, f % 4, :], mixT1_lo[f // 4][:, f % 4, :],
                                                      f == 4), s)
                    elif kind == "tail" and s[1] == "out":
                        drained(pe, ("mix_turn", 0, l, 1))
                        tail_products(("out", 0, l), s[-1], [(f, mixT1_hi[0][:, f, :], mixT1_lo[0][:, f, :]) for f in (1, 2, 3)])
                    elif kind == "tail":
                        pe.wait_ge(u_ready, 16 * (l + 1))
                        tail_products(("ff2", l), s[-1], [(28 + c, u_hi[1][:, c, :], u_lo[1][:, c, :]) for c in (1, 2, 3)])
                    elif kind == "ff1":
                        _, _, t, q = s
                        there = features_there(n0 + 1) if t == 0 else None
                        feature_unit(s, [("ff1", l, t, i) for i in range(2)], q, there)
                    elif kind == "ff2":
                        f = s[3]
                        if f % 2 == 0:
                            pe.wait_ge(u_ready, 16 * l + f // 2 + 1)
                        t = f // 4
                        finish_unit(out_unit_products(s, ("ff2", l), u_hi[t % 2][:, f % 4, :], u_lo[t % 2][:, f % 4, :], f == 0), s)

            for l in range(L):
                for s in timeline[1][l]:
                    kind = s[0]
                    if kind == "norm":
                        turn_normed(s)
                    elif kind == "r_row":
                        factor_row(s)
                    elif kind == "proj":
                        _, b, _, j, q = s
                        both = [("proj", b, l, j, i) for i in range(2)]
                        there = features_there(4 + l) if j == PROJ2[0] else None
                        (feature_unit if j in FEATURE2 else token_unit)(s, both, q, there)
                    elif kind == "proj_tile":
                        i, uses_of = s[3], [("proj", 1, l, 0, c) for c in range(2)]
                        for q in range(3):
                            mm = token_products(("proj", 1, l, 0, q), uses_of, q, features_there(4 + l), i)
                            if i == NT - 1:
                                finish_unit(mm, ("proj", 1, l, 0, q))
                    elif kind == "forget_f":
                        ps = open_bank(s)
                        for k in range(KD):
                            mm = exact_product(ps[0:8, 0:T], (ff_hi[:, l, k, :], ff_lo[:, l, k, :]),
                                               (h_hi[:, k, :], h_lo[:, k, :]), k == 0, k == KD - 1)
                        close(mm, s)
                    elif kind == "turn2":
                        pe.wait_ge(vec_ready, 2 * L + l + 1)
                        turn(s, vec[:, :, :, :].rearrange("p i s d -> p i (s d)"),
                             [(2 * s[2] + c, i) for c in range(2) for i in range(NT)])
                    elif kind in ("diff", "fox"):
                        head_stage(kind, l, s[2], s[3])
                    elif kind == "stick" and s[2] == "Z":
                        h = s[3]
                        head_inputs(kind, l, "Z", h)
                        b = HD * (h % 2)
                        q, k = featT[b:b + HD, h // 2, :], featT[b:b + HD, 4 + h // 2, :]
                        ps = open_bank(("stick", l, "Z", h))
                        pe.matmul(ps[:, 0:T], k[:, 0:P], q, start=True, stop=False, skip_group_check=True)
                        pe.matmul(ps[:, T:T + P], k[:, P:T], q[:, P:T], start=False, stop=False, skip_group_check=True)
                        pe.matmul(ps[:, 0:P], ident_b, strict_b, start=False, stop=False, skip_group_check=True)
                        close(pe.matmul(ps[:, T:T + P], ident_b, strict_b, start=False, stop=False, skip_group_check=True), s)
                    elif kind == "stick" and s[2] == "R":
                        h = s[3]
                        pe.wait_ge(keep_ready, 8 * l + h + 1)
                        ps = open_bank(("stick", l, "R", h))
                        for kp in (keep_hi[:, h % 2, :], keep_lo[:, h % 2, :]):
                            pe.matmul(ps[:, 0:T], suffix[:, 0, :], kp[:, 0:T], start=False, stop=False, skip_group_check=True)
                            pe.matmul(ps[:, P:T], suffix[:, 1, :], kp[:, T:T + P], start=False, stop=False, skip_group_check=True)
                            mm = pe.matmul(ps[:, T:T + P], suffix[:, 0, :], kp[:, T:T + P], start=False, stop=False,
                                           skip_group_check=True)
                        close(mm, s)
                    elif kind == "stick" and s[2] == "V":
                        h = s[3]
                        g, r = divmod(h, 4)
                        head_inputs(kind, l, "V", h)
                        drained(pe, ("stick", l, "R", h))
                        ps = open_bank(("stick", l, "O", g)) if r == 0 else bank[bank_of[("stick", l, "O", g)]]
                        a, lo = probs[:, h % 3, :], r * 2 * HD
                        v0, v1 = (values[:, 1, i, HD * h:HD * (h + 1)] for i in range(2))
                        pe.matmul(ps[:, lo:lo + HD], a[:, 0:P], v0, start=True, stop=True)
                        pe.matmul(ps[:, lo + HD:lo + 2 * HD], a[:, P:T], v0, start=True, stop=False)
                        mm = pe.matmul(ps[:, lo + HD:lo + 2 * HD], a[:, T:T + P], v1, start=False, stop=True)
                        if r == 3:
                            close(mm, ("stick", l, "O", g))
                    elif kind == "mix_turn":
                        _, _, _, g, i = s
                        if g == 0:
                            pe.wait_ge(diff_mixed, l + 1)
                        else:
                            pe.wait_ge(mix_ready, 3 * L + 2 * l + g)
                        turn(s, mix, [(4 * g + c, i) for c in range(4)])
                    elif kind == "out":
                        f = s[4]
                        if f % 4 == 0:
                            for i in range(NT):
                                drained(pe, ("mix_turn", 1, l, f // 4, i))
                        g = f // 4
                        finish_unit(out_unit_products(s, ("out", 1, l), mixT_hi[g][:, f % 4, :], mixT_lo[g][:, f % 4, :],
                                                      f == 0), s)
                    elif kind == "tail":
                        tail_products(("out", 1, l), s[-1], [(8 + c, mixT_hi[2][:, c, :], mixT_lo[2][:, c, :]) for c in (1, 2, 3)])

        @block.scalar
        def _(act):
            step = [0]
            n_split = [0]
            n_heads = [0]

            def link(ins):
                step[0] += 1
                ins.then_inc(scalar_step, 1)
                act.wait_ge(scalar_step, step[0])

            def free(ins, key):
                ins.then_inc(bank_freed[bank_of[key]], 1)
                drained(act, key)

            def split_to(n):
                while n_split[0] <= min(n, len(units) - 1):
                    m = n_split[0]
                    n_split[0] += 1
                    u = units[m]
                    if not u["split"]:
                        continue
                    act.wait_ge(raw_arrived[m % SLOTS], 16 * (m // SLOTS + 1))
                    if m >= SLOTS:
                        released(act, m - SLOTS)
                    act.activation(slot(w_hi, u), slot(raw, u), ACT.Copy).then_inc(hi_ready, 1)

            def src(key):
                split_to(at_unit[key] + AHEAD - 1)
                filled(act, key)
                return bank[bank_of[key]]

            def turned(key, dst):
                ps = src(key)
                act.activation(dst, ps[:, :].rearrange("p (c t) -> p c t", c=dst.shape[1]), ACT.Copy).then_inc(turned_hi, 1)

            def norm_step(n, i, u):
                turned(("norm", n, i, u), h_hi[:, 4 * u:4 * u + 4, i * P:(i + 1) * P])
                if i == NT - 1 and u == 1 and n + 1 < 3 * L:
                    act.dma_start(gain[:, :], GAINS[n + 1].partition_broadcast(P)).then_inc(gain_loaded, 16)

            def row_squares(n):
                for i in range(NT):
                    if n == 0:
                        for half in range(2):
                            act.wait_ge(x_loaded[half], 16)
                    else:
                        act.wait_ge(x_tile_ready, NT * (n - 1) + i + 1)
                    act.activation(mix[:, i, 0:D], x_sb[:, i, :], ACT.Square, accum_out=ss[:, n, i:i + 1]).then_inc(sumsq_ready, 1)

            def softmax_stage(kind, l, stage, h):
                name = (kind, l)
                if stage == "E":
                    ps = src((*name, "S", h))
                    n_heads[0] += 1
                    act.wait_ge(max_ready, n_heads[0])
                    g, r = divmod(h, GROUPS[kind])
                    link(act.activation(probs[:, h % 3, 0:P], ps[:, 0:P], ACT.Exp, scale=SCALE,
                                        bias=row_nb[:, h % 2, 0:1], accum_out=row_sum[:, g % 2, r, 0:1]))
                    free(act.activation(probs[:, h % 3, P:3 * P], ps[:, P:3 * P], ACT.Exp, scale=SCALE,
                                        bias=row_nb[:, h % 2, 1:2], accum_out=row_sum[:, g % 2, r, 1:2]), (*name, "S", h))
                elif stage == "T":
                    ps = src((*name, "T", h))
                    free(act.activation(probsT[:, h % 3, :], ps[:, 0:384], ACT.Copy), (*name, "T", h))

            GAINS = []
            for l in range(L):
                GAINS += [norm_mix[l], norm_ffn[l]]
            GAINS += [pre_norm_2[l] for l in range(L)]

            act.dma_start(const[:, C_ID:C_ID + P], consts[:, C_ID:C_ID + P]).then_inc(ident_loaded, 16)
            act.dma_start(gain[:, :], GAINS[0].partition_broadcast(P)).then_inc(gain_loaded, 16)
            act.preload_act_table_set(LOG_EXP)

            for l in range(L):
                for s in timeline[0][l]:
                    kind = s[0]
                    if s in unit_no:
                        split_to(unit_no[s] + AHEAD)
                    elif kind == "proj_tile":
                        split_to(unit_no["proj", 1, l, 0, 2] + s[3])
                    if kind == "norm":
                        norm_step(*s[1:])
                    elif kind == "stats":
                        row_squares(s[1])
                    elif kind == "r_row":
                        free(act.activation(r_row[:, :], src(s)[:, 0:T], ACT.Copy), s)
                    elif kind == "params":
                        act.wait_ge(const_loaded, 32)
                        act.activation(sel[:, :].rearrange("h (i c) -> h i c", i=NT), mix[0:8, :, D:D + 512], ACT.Copy).then_inc(sel_ready, 1)
                        free(act.activation(prm[:, :], src(s)[:, 0:128], ACT.Copy), s)
                    elif kind == "evac":
                        j = s[3]
                        if j == PROJ1[0]:
                            act.wait_ge(rstd_ready, 4 * l + NT)
                        if j == 3:
                            for i in range(NT):
                                key = ("proj", 0, l, 3, i)
                                free(act.activation(o_gate[:, i, :, :], src(key)[:, :].rearrange("p (h d) -> p h d", d=P),
                                                    ACT.Sigmoid, scale=rstd[:, 2 * l, i:i + 1]), key)
                            act.preload_act_table_set(LOG_EXP)
                            continue
                        for i in range(NT):
                            key = ("proj", 0, l, j, i)
                            if j in FEATURE1:
                                continue
                            ps = src(key)
                            r = rstd[:, 2 * l, i:i + 1]
                            if j == 2:
                                free(act.activation(v_aug[:, i, :, 0:P], ps[:, :].rearrange("p (h d) -> p h d", d=P), ACT.Copy,
                                                    scale=r), key)
                            else:
                                c0 = 512 * j - REST0
                                n = min(512, COLS1 - 512 * j)
                                free(act.activation(rest[:, i, c0:c0 + n], ps[:, 0:n], ACT.Copy, scale=r), key)
                        if j == 6:
                            act.activation(n_gate, rest[:, :, 1416:1428], ACT.Exp, scale=-1.0).then_inc(nsa_exp, 1)
                    elif kind == "gate_log":
                        act.wait_ge(gate_abs, l + 1)
                        link(act.activation(g_e[:, :, 0:4], g_e[:, :, 0:4], ACT.Exp))
                        act.activation(g_e[:, :, 0:4], g_e[:, :, 0:4], ACT.Ln, bias=1.0).then_inc(gate_log, 1)
                    elif kind in ("vec_a", "vec_b"):
                        v0, v1 = (0, 8) if kind == "vec_a" else (12, 22)
                        if s[2] == 0:
                            act.activation(squares[:, :, v0:v1, :].rearrange("p i s d -> p i (s d)"),
                                           rest[:, :, 8 + HD * v0:8 + HD * v1], ACT.Square).then_inc(squared, 1)
                        elif s[2] == 1:
                            act.wait_ge(vec_ms, 2 * l + (1 if kind == "vec_a" else 2))
                            link(act.activation(v_r[:, :, v0:v1], v_ms[:, :, v0:v1], ACT.Ln))
                            act.activation(v_r[:, :, v0:v1], v_r[:, :, v0:v1], ACT.Exp, scale=-0.5).then_inc(vec_rstd, 1)
                    elif kind == "turn" and s[2] != 4:
                        u = s[2]
                        free(act.activation(vecT[:, 2 * u:2 * u + 2, :], src(s)[:, :].rearrange("p (c t) -> p c t", c=2), ACT.Copy), s)
                    elif kind == "conv_silu":
                        act.wait_ge(conv_done, 8 * (l + 1))
                        act.activation(m_qk, m_qk, ACT.Silu).then_inc(conv_silu, 1)
                        act.preload_act_table_set(LOG_EXP)
                    elif kind == "m_exp":
                        if s[2] == 0:
                            act.wait_ge(m_col_ready, l + 1)
                            act.activation(e_m[:, :, 0:4], m_tok[:, :, 0:4], ACT.Exp).then_inc(stabilizer, 1)
                        u = s[2]
                        act.wait_ge(exponent_ready, 2 * l + u + 1)
                        act.activation(intra[:, 2 * u:2 * u + 2, :], intra[:, 2 * u:2 * u + 2, :], ACT.Exp).then_inc(intra_exp, 1)
                    elif kind == "hidden":
                        ps = src(s)
                        act.activation(hid[:, 0, :, 0:NC_CMP], ps[:, 0:32].rearrange("p (v c) -> p v c", c=16)[:, :, 0:NC_CMP],
                                       ACT.Exp, scale=-1.0).then_inc(hid_exp, 1)
                    elif kind == "cmp_kT":
                        free(act.activation(kcT[:, :], src(s)[:, 0:NC_CMP], ACT.Copy), s)
                    elif kind == "cmp_soft":
                        act.wait_ge(cmp_shifted, l + 1)
                        act.activation(p_cmp[:, :, :, 0:NC_CMP], p_cmp[:, :, :, 0:NC_CMP], ACT.Exp, scale=SCALE).then_inc(cmp_exp, 1)
                    elif kind == "cmp_pT":
                        free(act.activation(p_cmpT[:, :, :], src(s)[:, 0:T].rearrange("p (i t) -> p i t", i=NT), ACT.Copy), s)
                    elif kind == "mlstm" and s[2] == "O":
                        h = s[3]
                        ps = src(s)
                        link(act.activation(h_num[:, :, h, :], ps[:, 0:258].rearrange("p (i d) -> p i d", i=NT), ACT.Copy))
                        for i in range(NT):
                            ins = act.activation(sq_out[:, :], ps[:, 129 * i:129 * i + P], ACT.Square,
                                                 accum_out=h_ss[:, i, h:h + 1])
                            if i == 0:
                                link(ins)
                            else:
                                free(ins, s)
                    elif kind == "att1":
                        softmax_stage(kind, l, s[2], s[3])
                    elif kind == "mix_turn":
                        g, c = divmod(2 * s[3], 4)
                        turned(s, mixT1_hi[g][:, c:c + 2, :])
                    elif kind == "square":
                        t = s[2]
                        for i in range(2):
                            n = 16 * l + 2 * t + i
                            ps = src(("ff1", l, t, i))
                            if n >= 2:
                                act.wait_ge(u_ready, n - 1)
                            free(act.activation(relu[:, i, :], ps[:, :], ACT.Relu), ("ff1", l, t, i))
                            act.activation(u_hi[t % 2][:, 2 * i:2 * i + 2, :], relu[:, i, :].rearrange("p (c t) -> p c t", c=2),
                                           ACT.Square).then_inc(u_hi_ready, 1)

            for l in range(L):
                for s in timeline[1][l]:
                    kind = s[0]
                    if s in unit_no:
                        split_to(unit_no[s] + AHEAD)
                    elif kind == "proj_tile":
                        split_to(unit_no["proj", 1, l, 0, 2] + s[3])
                    if kind == "norm":
                        norm_step(*s[1:])
                    elif kind == "stats":
                        row_squares(s[1])
                    elif kind == "r_row":
                        free(act.activation(r_row[:, :], src(s)[:, 0:T], ACT.Copy), s)
                    elif kind == "forget_log":
                        act.wait_ge(gate_abs, L + l + 1)
                        link(act.activation(rows[0:8, 1, :], rows[0:8, 1, :], ACT.Exp))
                        act.activation(rows[0:8, 1, :], rows[0:8, 1, :], ACT.Ln, bias=1.0).then_inc(gate_log, 1)
                        act.wait_ge(lam_dots, l + 1)
                        act.activation(lam[:, 0:2], lam[:, 0:2], ACT.Exp).then_inc(lam_exp, 1)
                    elif kind == "evac":
                        j = s[3]
                        if j == 0:
                            act.wait_ge(rstd_ready, NT * (4 + l) + NT)
                        for i in range(NT):
                            key = ("proj", 1, l, j, i)
                            if j in FEATURE2:
                                continue
                            ps = src(key)
                            r = rstd[:, 4 + l, i:i + 1]
                            if j < 2:
                                free(act.activation(vec[:, i, 8 * j:8 * j + 8, :].rearrange("p s d -> p (s d)"), ps[:, :], ACT.Copy,
                                                    scale=r), key)
                            elif j % 4 == 2:
                                free(act.activation(values[:, j // 4, i, :], ps[:, :], ACT.Copy, scale=r), key)
                            else:
                                free(act.activation(gates[:, i, j // 4, :], ps[:, :], ACT.Silu, scale=r), key)
                        if j % 4 == 3:
                            act.preload_act_table_set(LOG_EXP)
                    elif kind == "turn2":
                        u = s[2]
                        free(act.activation(vecT[:, 2 * u:2 * u + 2, :], src(s)[:, :].rearrange("p (c t) -> p c t", c=2), ACT.Copy), s)
                        if u == 3:
                            act.dma_start(post_gain, post_norm_2[l].partition_broadcast(P)).then_inc(post_loaded, 16)
                    elif kind in ("diff", "fox"):
                        softmax_stage(kind, l, s[2], s[3])
                    elif kind == "stick" and s[2] == "Z":
                        h = s[3]
                        ps = src(s)
                        if h >= 2:
                            act.wait_ge(keep_ready, 8 * l + h - 1)
                        link(act.activation(softp[:, h % 2, :], ps[:, 0:384], ACT.Abs))
                        link(act.activation(softp[:, h % 2, :], softp[:, h % 2, :], ACT.Exp, scale=-1.0))
                        act.activation(softp[:, h % 2, :], softp[:, h % 2, :], ACT.Ln, bias=1.0).then_inc(stick_log, 1)
                    elif kind == "stick" and s[2] == "R":
                        free(act.activation(probs[:, s[3] % 3, :], src(s)[:, 0:384], ACT.Exp), s)
                    elif kind == "mix_turn":
                        g, i = s[3], s[4]
                        turned(s, mixT_hi[g][:, 0:4, i * P:(i + 1) * P])
                    elif kind == "post_norm" and s[2] == 0:
                        for a in range(4):
                            ps = src(("out", 1, l, "acc", a))
                            act.activation(mix[:, a // 2, (a % 2) * 512:(a % 2 + 1) * 512], ps[:, :], ACT.Square,
                                           accum_out=y_ss[:, a:a + 1]).then_inc(y_sumsq, 1)

        @block.gpsimd
        def _(pool):
            step = [0]
            n_split = [0]

            def link(ins):
                step[0] += 1
                ins.then_inc(pool_step, 1)
                pool.wait_ge(pool_step, step[0])

            def split_to(n):
                while n_split[0] <= min(n, len(units) - 1):
                    m = n_split[0]
                    n_split[0] += 1
                    u = units[m]
                    if u["split"] and u["lo_on"] == "pool":
                        pool.wait_ge(hi_ready, u["n_hi"])
                        pool.tensor_tensor(slot(w_lo, u), slot(raw, u), slot(w_hi, u).bitcast(F32), ALU.subtract)\
                            .then_inc(lo_ready["pool"], 1)

            def row_rstd(n):
                for i in range(NT):
                    pool.wait_ge(sumsq_ready, NT * n + i + 1)
                    r = rstd[:, n, i:i + 1]
                    link(pool.tensor_scalar(ms[:, n, i:i + 1], ss[:, n, i:i + 1], 1.0 / D, EPS, ALU.mult, ALU.add))
                    ins = pool.tensor_tensor(r, ms[:, n, i:i + 1], half_neg[:, 0:1], ALU.pow)
                    if n < 2 * L and n % 2:
                        link(ins)
                        ins = pool.tensor_tensor(r, r, r, ALU.mult)
                    ins.then_inc(rstd_ready, 1)

            pool.memset(half_neg, -0.5).then_inc(half_neg_set, 1)
            pool.wait_ge(half_neg_set, 1)
            for l in range(L):
                for s in timeline[0][l]:
                    kind = s[0]
                    if s in unit_no:
                        split_to(unit_no[s] + AHEAD)
                    elif kind == "proj_tile":
                        split_to(unit_no["proj", 1, l, 0, 2] + s[3])
                    if kind == "stats":
                        row_rstd(s[1])
                    elif kind == "m_exp":
                        u = s[2]
                        pool.wait_ge(intra_exp, 2 * l + u + 1)
                        le = const[:, C_LE:C_LE + P]
                        if l == 0 and u == 0:
                            pool.wait_ge(const_loaded, 32)
                        for h in (2 * u, 2 * u + 1):
                            link(pool.tensor_tensor(intra[:, h, 0:P], intra[:, h, 0:P], le, ALU.mult))
                            pool.tensor_tensor(intra[:, h, 2 * P:3 * P], intra[:, h, 2 * P:3 * P], le, ALU.mult).then_inc(intra_masked, 1)
                    elif kind == "cmp_kv":
                        pool.wait_ge(kc_ms, l + 1)
                        pool.tensor_tensor(kc_s[0:NC_CMP, 2:3], kc_s[0:NC_CMP, 1:2], half_neg[0:NC_CMP, 0:1], ALU.pow).then_inc(kc_rstd, 1)
                    elif kind == "evac" and s[3] == 3:
                        for i in range(NT):
                            drained(pool, ("proj", 0, l, 3, i))
                            if l == 0 and i == 0:
                                pool.wait_ge(prm_loaded, 16 * PRM_LOADS)
                            pool.tensor_tensor(o_gate[:, i], o_gate[:, i], m_gain[:, l, :].rearrange("p (h d) -> p h d", d=P),
                                               ALU.mult).then_inc(o_gained, 1)
                    elif kind == "mlstm_end" and s[2] == 0:
                        pool.wait_ge(h_ms_ready, l + 1)
                        pool.tensor_tensor(h_rs.rearrange("p a b -> p (a b)"), h_ms.rearrange("p a b -> p (a b)"), half_neg,
                                           ALU.pow).then_inc(h_rstd_ready, 1)
            for l in range(L):
                for s in timeline[1][l]:
                    kind = s[0]
                    if s in unit_no:
                        split_to(unit_no[s] + AHEAD)
                    elif kind == "proj_tile":
                        split_to(unit_no["proj", 1, l, 0, 2] + s[3])
                    if kind == "stats":
                        row_rstd(s[1])
                    elif s == ("diff", l, "V", 7):
                        pool.wait_ge(h_ms_ready, L + l + 1)
                        for i in range(NT):
                            drained(pool, ("proj", 1, l, 3, i))
                        link(pool.tensor_tensor(h_rs.rearrange("p a b -> p (a b)"), h_ms.rearrange("p a b -> p (a b)"), half_neg, ALU.pow))
                        link(pool.tensor_tensor(y_diff, y_diff, h_rs.unsqueeze(3).broadcast_to([P, NT, MH, P]), ALU.mult))
                        sg = sub_gain[:, l, :]
                        link(pool.tensor_scalar(sg, sg, 1.0 - LAM_INIT[l], None, ALU.mult))
                        for i in range(NT):
                            link(pool.tensor_tensor(y_diff[:, i], y_diff[:, i], sg.unsqueeze(1).broadcast_to([P, MH, P]), ALU.mult))
                        pool.tensor_tensor(mix[:, :, 0:512].rearrange("p i (h d) -> p i h d", d=P), y_diff,
                                           gates[:, :, 0, :].rearrange("p i (h d) -> p i h d", d=P), ALU.mult).then_inc(diff_mixed, 1)
                    elif kind == "post_norm":
                        i = s[2]
                        pool.wait_ge(y_ms, NT * s[1] + i + 1)
                        pool.tensor_tensor(y_rs[:, i:i + 1], y_mean[:, i:i + 1], half_neg[:, 0:1], ALU.pow).then_inc(y_rstd, 1)

        @block.vector
        def _(dve):
            step = [0]
            n_split = [0]
            n_turned = [0]

            def link(ins):
                step[0] += 1
                ins.then_inc(vector_step, 1)
                dve.wait_ge(vector_step, step[0])

            def free(ins, key):
                ins.then_inc(bank_freed[bank_of[key]], 1)
                drained(dve, key)

            def split_to(n):
                while n_split[0] <= min(n, len(units) - 1):
                    m = n_split[0]
                    n_split[0] += 1
                    u = units[m]
                    if u["split"] and u["lo_on"] == "vector":
                        dve.wait_ge(hi_ready, u["n_hi"])
                        dve.tensor_tensor(slot(w_lo, u), slot(raw, u), slot(w_hi, u).bitcast(F32), ALU.subtract)\
                            .then_inc(lo_ready["vector"], 1)

            def src(key):
                split_to(at_unit[key] + AHEAD - 1)
                filled(dve, key)
                return bank[bank_of[key]]

            def tt(out, a, b, op):
                link(dve.tensor_tensor(out, a, b, op))

            def signal(sem_):
                dve.tensor_copy(flag[:, 0:1], flag[:, 1:2]).then_inc(sem_, 1)

            def turned(key, hi, lo):
                ps = src(key)
                n_turned[0] += 1
                dve.wait_ge(turned_hi, n_turned[0])
                free(dve.tensor_tensor(lo, ps[:, :].rearrange("p (c t) -> p c t", c=lo.shape[1]), hi.bitcast(F32), ALU.subtract), key)

            def norm_step(n, i, u):
                c, t = slice(4 * u, 4 * u + 4), slice(i * P, (i + 1) * P)
                turned(("norm", n, i, u), h_hi[:, c, t], h_lo[:, c, t])

            def gained(n, i, half):
                c = slice(half * 512, half * 512 + 512)
                if i == 0 and half == 0:
                    dve.wait_ge(gain_loaded, 16 * (n + 1))
                dve.tensor_tensor(xn[:, i, c], x_sb[:, i, c], gain[:, c], ALU.mult).then_inc(xn_ready, 1)

            def residual(name, a, n):
                i, half = divmod(a, 2)
                key = (*name, "acc", a)
                ps = src(key)
                xs = x_sb[:, i, half * 512:(half + 1) * 512]
                if name[0] == "out":
                    free(dve.tensor_tensor(xs, xs, ps[:, :], ALU.add), key)
                else:
                    dve.wait_ge(rstd_ready, NT * n)
                    free(dve.scalar_tensor_tensor(xs, ps[:, :], rstd[:, n - 1, i:i + 1], xs, ALU.mult, ALU.add), key)
                gained(n, i, half)
                if half:
                    signal(x_tile_ready)

            def factor_diag(n):
                dve.wait_ge(rstd_ready, NT * n + NT)
                for i in range(NT):
                    ins = dve.tensor_scalar(r_diag[:, i, :], ident, rstd[:, n, i:i + 1], None, ALU.mult)
                    if i == 0:
                        link(ins)
                    else:
                        ins.then_inc(diag_ready, 1)

            def rope(s0, s1):
                n = s1 - s0
                a, b = vec[:, :, s0:s1, 0:8], vec[:, :, s0:s1, 8:16]
                cos = const[:, C_COS:C_COS + NT * 8].rearrange("p (i d) -> p i d", i=NT).unsqueeze(2).broadcast_to([P, NT, n, 8])
                sin = const[:, C_SIN:C_SIN + NT * 8].rearrange("p (i d) -> p i d", i=NT).unsqueeze(2).broadcast_to([P, NT, n, 8])
                t = [o_tmp[:, 0:256], o_tmp[:, 256:512], softp[:, 0, 0:256], softp[:, 1, 0:256]]
                t = [y[:, 0:NT * n * 8].rearrange("p (i s d) -> p i s d", i=NT, d=8) for y in t]
                tt(t[0], a, cos, ALU.mult)
                tt(t[1], b, sin, ALU.mult)
                tt(t[2], b, cos, ALU.mult)
                tt(t[3], a, sin, ALU.mult)
                tt(a, t[0], t[1], ALU.subtract)
                dve.tensor_tensor(b, t[2], t[3], ALU.add).then_inc(vec_ready, 1)

            def row_max(name, h):
                ps = src((*name, "S", h))
                link(dve.tensor_reduce(row_mx[:, h % 2, 0:1], ps[:, 0:P], AX.X, ALU.max))
                link(dve.tensor_reduce(row_mx[:, h % 2, 1:2], ps[:, P:3 * P], AX.X, ALU.max))
                dve.tensor_scalar(row_nb[:, h % 2, :], row_mx[:, h % 2, :], -SCALE, None, ALU.mult).then_inc(max_ready, 1)

            link(dve.memset(flag[:, :], 1.0))
            for half in range(2):
                dve.wait_ge(x_loaded[half], 16)
                for i in range(NT):
                    gained(0, i, half)

            for l in range(L):
                rv = rest[:, :, 8:8 + NVEC * HD].rearrange("p i (s d) -> p i s d", d=HD)

                def scaled(dst, s0, n, g):
                    o = vec[:, :, dst:dst + n, :]
                    tt(o, rv[:, :, s0:s0 + n, :], v_r[:, :, s0:s0 + n].unsqueeze(3).broadcast_to([P, NT, n, HD]), ALU.mult)
                    tt(o, o, g_vec[:, l, g, :].unsqueeze(1).unsqueeze(1).broadcast_to([P, NT, n, HD]), ALU.mult)

                def mean_squares(v0, v1, idx):
                    dve.wait_ge(squared, idx)
                    link(dve.tensor_reduce(v_ss[:, :, v0:v1], squares[:, :, v0:v1, :], AX.X, ALU.add))
                    dve.tensor_scalar(v_ms[:, :, v0:v1], v_ss[:, :, v0:v1], 1.0 / HD, EPS, ALU.mult, ALU.add).then_inc(vec_ms, 1)

                def refine(v0, v1, idx):
                    r, v, t = v_r[:, :, v0:v1], v_ms[:, :, v0:v1], v_t[:, :, v0:v1]
                    dve.wait_ge(vec_rstd, idx)
                    tt(t, r, r, ALU.mult)
                    tt(t, t, v, ALU.mult)
                    link(dve.tensor_scalar(t, t, -0.5, 1.5, ALU.mult, ALU.add))
                    tt(r, r, t, ALU.mult)

                def epilogue1(g):
                    name = ("att1", l, "O", g)
                    ps = src(name)
                    ov = ps[:, :].rearrange("p (h i d) -> p h i d", h=4, i=NT)
                    link(dve.reciprocal(row_inv, row_sum[:, g % 2]))
                    lo = 512 if g == 0 else 768
                    dst = mix[:, :, lo:lo + 256].rearrange("p i (h d) -> p h i d", d=HD)
                    if g:
                        tt(row_inv, row_inv, n_gate[:, :, 4 * g:4 * g + 4].rearrange("p i h -> p h i"), ALU.mult)
                    f = row_inv.unsqueeze(3).broadcast_to([P, 4, NT, HD])
                    if g < 2:
                        free(dve.tensor_tensor(dst, ov, f, ALU.mult), name)
                        if g == 0:
                            signal(mix_ready)
                        return
                    t = o_tmp[:, :].rearrange("p (h i d) -> p h i d", h=4, i=NT)
                    free(dve.tensor_tensor(t, ov, f, ALU.mult), name)
                    dve.tensor_tensor(dst, dst, t, ALU.add).then_inc(mix_ready, 1)

                for s in timeline[0][l]:
                    kind = s[0]
                    if s in unit_no:
                        split_to(unit_no[s] + AHEAD)
                    elif kind == "proj_tile":
                        split_to(unit_no["proj", 1, l, 0, 2] + s[3])
                    if kind == "norm":
                        norm_step(*s[1:])
                    elif kind == "r_row":
                        factor_diag(s[1])
                    elif kind == "to_norm":
                        residual(s[1:-2], s[-2], s[-1])
                    elif kind == "params":
                        dve.wait_ge(ident_loaded, 16)
                        dve.wait_ge(const_loaded, 32)
                        for n, c in enumerate((C_ID, C_CAUSAL, C_CHUNK, C_STRICT)):
                            link(dve.tensor_copy(masks[:, n * P:(n + 1) * P], const[:, c:c + P]))
                        link(dve.tensor_copy(suffix[:, 0, :], const[:, C_RTRI:C_RTRI + P]))
                        link(dve.tensor_copy(suffix[:, 1, :], const[:, C_NONES:C_NONES + P]))
                        link(dve.memset(vc_diag[:, :, :], 0.0))
                        link(dve.memset(p_cmp[:, :, :, :], 0.0))
                        dve.wait_ge(prm_loaded, 16 * PRM_LOADS)
                        link(dve.tensor_copy(ff_hi[:, :, :, :].rearrange("p l k c -> p (l k c)"), ff_w[:, :]))
                        link(dve.tensor_tensor(ff_lo[:, :, :, :].rearrange("p l k c -> p (l k c)"), ff_w[:, :],
                                               ff_hi[:, :, :, :].rearrange("p l k c -> p (l k c)").bitcast(F32), ALU.subtract))
                    elif kind == "gate_log":
                        for i in range(NT):
                            drained(dve, ("proj", 0, l, 4, i))
                        link(dve.memset(v_aug[:, :, :, 128:130], 1.0))
                        tt(gif, rest[:, :, 0:8], bif[:, l, :].unsqueeze(1).broadcast_to([P, NT, 8]), ALU.add)
                        f, e, lf = gif[:, :, 4:8], g_e[:, :, 0:4], g_lf[:, :, 0:4]
                        dve.scalar_tensor_tensor(e, f, -1.0, f, ALU.mult, ALU.min).then_inc(gate_abs, 1)
                        dve.wait_ge(gate_log, l + 1)
                        link(dve.tensor_scalar(lf, f, 0.0, None, ALU.min))
                        dve.tensor_tensor(lf, lf, e, ALU.subtract).then_inc(logf_ready, 1)
                    elif kind == "gate_sum":
                        Fv = src(s)[:, 0:8].rearrange("p (i h) -> p i h", i=NT)
                        link(dve.tensor_copy(g_F[:, :, 0:4], Fv))
                        free(dve.tensor_tensor(g_a[:, :, 0:4], gif[:, :, 0:4], Fv, ALU.subtract), s)
                        signal(a_ready)
                    elif kind == "gate_row":
                        free(dve.tensor_copy(rows[0:4, 2, :], src(s)[0:4, 0:T]), s)
                        link(dve.tensor_tensor_scan(rows[0:4, 0, :], rows[0:4, 2, :], rows[0:4, 2, :], 0.0, ALU.max, ALU.max))
                        link(dve.tensor_scalar(rows[0:4, 1, :], rows[0:4, 0, :], -1.0, None, ALU.mult))
                        link(dve.tensor_copy(row_hi[0:4, :], rows[0:4, 1, :]))
                        dve.tensor_tensor(row_lo[0:4, :], rows[0:4, 1, :], row_hi[0:4, :].bitcast(F32), ALU.subtract)\
                            .then_inc(m_ready, 1)
                    elif kind == "vec_a":
                        if s[2] == 0:
                            mean_squares(0, 8, 2 * l + 1)
                        elif s[2] == 1:
                            refine(0, 8, 2 * l + 1)
                            scaled(0, 0, 4, 0)
                        else:
                            scaled(4, 4, 4, 1)
                            rope(0, 8)
                    elif kind == "vec_b":
                        if s[2] == 0:
                            mean_squares(12, 22, 2 * l + 2)
                        elif s[2] == 1:
                            refine(12, 22, 2 * l + 2)
                            scaled(20, 12, 4, 2)
                            link(dve.tensor_copy(vec[:, :, 8:12, :], vec[:, :, 20:24, :]))
                        elif s[2] == 2:
                            scaled(12, 18, 1, 4)
                            scaled(14, 20, 1, 5)
                            link(dve.tensor_copy(vec[:, :, 13, :], vec[:, :, 12, :]))
                            link(dve.tensor_copy(vec[:, :, 15, :], vec[:, :, 14, :]))
                        elif s[2] == 3:
                            rope(8, 16)
                        else:
                            for j in (5, 6):
                                for i in range(NT):
                                    drained(dve, ("proj", 0, l, j, i))
                            for c in range(4):
                                ins = dve.tensor_copy(vec[:, :, 16 + c, :], rv[:, :, 16 + c // 2, :])
                                if c < 3:
                                    link(ins)
                            ins.then_inc(copied, 1)
                    elif kind == "turn" and s[2] == 4:
                        drained(dve, ("params",))
                        ps = src(s)
                        for v in range(2):
                            for half in range(2):
                                lo = HD * half
                                t = ps[lo:lo + HD, v * T:(v + 1) * T]
                                pe_col = prm[lo:lo + HD, 64 + (l * 2 + v) * 16:64 + (l * 2 + v) * 16 + 16]
                                for r in range(2):
                                    tok = t[:, 16 * r:16 * r + 240].rearrange("p (c a b) -> p a c b", a=8, b=2)[:, :, :, half]
                                    ins = dve.tensor_tensor(blocksT[lo:lo + HD, v, 8 * r:8 * r + 8, :], tok,
                                                            pe_col[:, 8 * r:8 * r + 8].unsqueeze(2).broadcast_to([HD, 8, NC_CMP]), ALU.add)
                                    if v and half and r:
                                        free(ins, s)
                                    else:
                                        link(ins)
                        signal(blocks_ready)
                    elif kind == "m_col":
                        free(dve.tensor_tensor(m_tok[:, :, 0:4], src(s)[:, 0:8].rearrange("p (i h) -> p i h", i=NT),
                                               g_F[:, :, 0:4], ALU.subtract), s)
                        signal(m_col_ready)
                    elif kind == "m_rows":
                        for c in range(2):
                            h = 2 * s[2] + c
                            ps = src(s)[:, c * T:(c + 1) * T]
                            link(dve.tensor_scalar(intra[:, h, 0:T], ps, g_a[:, 0, h:h + 1], 0.0, ALU.add, ALU.min))
                            ins = dve.tensor_scalar(intra[:, h, T:T + P], ps[:, P:T], g_a[:, 1, h:h + 1], 0.0, ALU.add, ALU.min)
                            if c == 1:
                                free(ins, s)
                            else:
                                link(ins)
                        signal(exponent_ready)
                    elif kind == "evac" and s[3] == 6:
                        dve.wait_ge(nsa_exp, l + 1)
                        link(dve.tensor_scalar(n_gate, n_gate, 1.0, None, ALU.add))
                        link(dve.reciprocal(n_gate, n_gate))
                    elif kind == "evac" and s[3] in FEATURE1:
                        if s[3] == 0:
                            drained(dve, ("r_row", 2 * l))
                            link(dve.memset(conv_in[:, :, 0:3], 0.0))
                        for i in range(NT):
                            key = ("proj", 0, l, s[3], i)
                            c = 4 * s[3] + 2 * i
                            free(dve.tensor_tensor(conv_in[:, c:c + 2, 3:3 + T], src(key)[:, :].rearrange("p (c t) -> p c t", c=2),
                                                   r_row[:, :].unsqueeze(1).broadcast_to([P, 2, T]), ALU.mult), key)
                    elif kind == "conv":
                        c = s[2]
                        acc = m_qk[:, c, :]
                        link(dve.tensor_scalar(acc, conv_in[:, c, 0:T], conv_col(l, 0, c), None, ALU.mult))
                        for tap in range(1, 4):
                            ins = dve.scalar_tensor_tensor(acc, conv_in[:, c, tap:tap + T], conv_col(l, tap, c), acc,
                                                           ALU.mult, ALU.add)
                            if tap == 3:
                                ins.then_inc(conv_done, 1)
                            else:
                                link(ins)
                    elif kind == "hidden":
                        ps = src(s)
                        dve.wait_ge(hid_exp, l + 1)
                        link(dve.tensor_scalar(hid[:, 0, :, 0:NC_CMP], hid[:, 0, :, 0:NC_CMP], 1.0, None, ALU.add))
                        link(dve.reciprocal(hid[:, 0, :, 0:NC_CMP], hid[:, 0, :, 0:NC_CMP]))
                        free(dve.tensor_tensor(hid[:, 1, :, 0:NC_CMP], hid[:, 0, :, 0:NC_CMP],
                                               ps[:, 0:32].rearrange("p (v c) -> p v c", c=16)[:, :, 0:NC_CMP], ALU.mult), s)
                        signal(hid_ready)
                    elif kind == "cmp_kv":
                        ps = src(s)
                        link(dve.tensor_copy(kc_n[:, 0, :], ps[0:NC_CMP, 0:HD]))
                        for h in range(4):
                            ins = dve.tensor_copy(vc_diag[32 * h:32 * h + NC_CMP, h, :], ps[0:NC_CMP, HD:2 * HD])
                            if h < 3:
                                link(ins)
                            else:
                                free(ins, s)
                        tt(kc_n[:, 1, :], kc_n[:, 0, :], kc_n[:, 0, :], ALU.mult)
                        link(dve.tensor_reduce(kc_s[0:NC_CMP, 0:1], kc_n[:, 1, :], AX.X, ALU.add))
                        dve.tensor_scalar(kc_s[0:NC_CMP, 1:2], kc_s[0:NC_CMP, 0:1], 1.0 / HD, EPS, ALU.mult, ALU.add).then_inc(kc_ms, 1)
                        dve.wait_ge(kc_rstd, l + 1)
                        link(dve.tensor_scalar(kc_n[:, 0, :], kc_n[:, 0, :], kc_s[0:NC_CMP, 2:3], None, ALU.mult))
                        tt(kc_n[:, 0, :], kc_n[:, 0, :], g_vec[0:NC_CMP, l, 3, :], ALU.mult)
                        dve.tensor_copy(kc_n[:, 1, :], kc_n[:, 0, :]).then_inc(kc_ready, 1)
                    elif kind == "cmp_s":
                        odd = s[2]
                        mask = const[:, C_CNEG:C_CNEG + NT * NC_CMP].rearrange("p (i c) -> p i c", i=NT)
                        free(dve.tensor_tensor(p_cmp[:, :, odd:4:2, 0:NC_CMP],
                                               src(s)[:, 0:64].rearrange("p (i h c) -> p i h c", i=NT, h=2)[:, :, :, 0:NC_CMP],
                                               mask.unsqueeze(2).broadcast_to([P, NT, 2, NC_CMP]), ALU.add), s)
                    elif kind == "cmp_soft":
                        pc = p_cmp[:, :, :, 0:NC_CMP]
                        seen_ = const[:, C_C01:C_C01 + NT * NC_CMP].rearrange("p (i c) -> p i c", i=NT)
                        link(dve.tensor_reduce(c_mx, pc, AX.X, ALU.max))
                        dve.tensor_tensor(pc, pc, c_mx.unsqueeze(3).broadcast_to([P, NT, 4, NC_CMP]), ALU.subtract).then_inc(cmp_shifted, 1)
                        dve.wait_ge(cmp_exp, l + 1)
                        link(dve.tensor_reduce(c_sum, pc, AX.X, ALU.add))
                        link(dve.reciprocal(c_sum, c_sum))
                        tt(c_sum, c_sum, n_gate[:, :, 0:4], ALU.mult)
                        tt(pc, pc, c_sum.unsqueeze(3).broadcast_to([P, NT, 4, NC_CMP]), ALU.mult)
                        dve.tensor_tensor(pc, pc, seen_.unsqueeze(2).broadcast_to([P, NT, 4, NC_CMP]), ALU.mult).then_inc(cmp_ready, 1)
                    elif kind == "cmp_o":
                        dst = mix[:, :, 1024:1280]
                        free(dve.tensor_copy(dst, src(s)[:, :].rearrange("p (i c) -> p i c", i=NT)), s)
                    elif kind == "mlstm" and s[2] == "S":
                        h = s[3]
                        ps = src(s)
                        dve.wait_ge(intra_masked, MH * l + h + 1)
                        free(dve.scalar_tensor_tensor(m_probs[:, h % 2, :], ps[:, 0:384], M_SCALE, intra[:, h, :],
                                                      ALU.mult, ALU.mult), s)
                    elif kind == "att1":
                        if s[2] == "S":
                            row_max(("att1", l), s[3])
                        elif s[2] == "V" and s[3] % 4 == 3:
                            g = s[3] // 4
                            if g == 2:
                                tt(mix[:, :, 768:1024], mix[:, :, 768:1024], mix[:, :, 1024:1280], ALU.add)
                            epilogue1(g)
                    elif kind == "mlstm_end" and s[2] == 0:
                        for h in range(MH):
                            drained(dve, ("mlstm", l, "O", h))
                        dve.wait_ge(stabilizer, l + 1)
                        den, d, inv = h_num[:, :, :, 128], m_den[:, :, 0:4], m_den[:, :, 4:8]
                        link(dve.scalar_tensor_tensor(d, den, -1.0, den, ALU.mult, ALU.max))
                        tt(d, d, e_m[:, :, 0:4], ALU.max)
                        link(dve.reciprocal(inv, d))
                        tt(h_ms, h_ss, inv, ALU.mult)
                        tt(h_ms, h_ms, inv, ALU.mult)
                        dve.tensor_scalar(h_ms, h_ms, 1.0 / P, EPS, ALU.mult, ALU.add).then_inc(h_ms_ready, 1)
                    elif kind == "mlstm_end":
                        inv = m_den[:, :, 4:8]
                        dve.wait_ge(h_rstd_ready, l + 1)
                        tt(inv, inv, h_rs, ALU.mult)
                        dve.wait_ge(o_gained, NT * (l + 1))
                        hn = h_num[:, :, :, 0:P]
                        tt(hn, hn, inv.unsqueeze(3).broadcast_to([P, NT, MH, P]), ALU.mult)
                        dve.tensor_tensor(mix[:, :, 0:512].rearrange("p i (h d) -> p i h d", d=P), hn, o_gate, ALU.mult)\
                            .then_inc(mix_ready, 1)
                    elif kind == "mix_turn":
                        g, c = divmod(2 * s[3], 4)
                        turned(s, mixT1_hi[g][:, c:c + 2, :], mixT1_lo[g][:, c:c + 2, :])
                    elif kind == "square":
                        t = s[2]
                        for i in range(2):
                            n = 16 * l + 2 * t + i
                            split_to(at_unit[("ff1", l, t, i)] + AHEAD - 1)
                            drained(dve, ("ff1", l, t, i))
                            r = relu[:, i, :]
                            tt(u_full[:, i, :], r, r, ALU.mult)
                            dve.wait_ge(u_hi_ready, n + 1)
                            b = slice(2 * i, 2 * i + 2)
                            dve.tensor_tensor(u_lo[t % 2][:, b, :], u_full[:, i, :].rearrange("p (c t) -> p c t", c=2),
                                              u_hi[t % 2][:, b, :].bitcast(F32), ALU.subtract).then_inc(u_ready, 1)

            for l in range(L):
                def epilogue_diff(g):
                    name = ("diff", l, "O", g)
                    ov = src(name)[:, :].rearrange("p (c i d) -> p c i d", c=2, i=NT)
                    inv = row_inv[:, 0:2, :]
                    link(dve.reciprocal(inv, row_sum[:, g % 2, 0:2, :]))
                    link(dve.tensor_scalar(inv[:, 1, :], inv[:, 1, :], lam[:, 3:4], None, ALU.mult))
                    t = o_tmp[:, :].rearrange("p (c i d) -> p c i d", c=2, i=NT)
                    free(dve.tensor_tensor(t, ov, inv.unsqueeze(3).broadcast_to([P, 2, NT, P]), ALU.mult), name)
                    tt(y_diff[:, :, g, :], t[:, 0], t[:, 1], ALU.add)
                    tt(y_tmp[:, :, g, :], y_diff[:, :, g, :], y_diff[:, :, g, :], ALU.mult)
                    link(dve.tensor_reduce(h_ss[:, :, g:g + 1], y_tmp[:, :, g:g + 1, :], AX.X, ALU.add))
                    if g == 3:
                        dve.tensor_scalar(h_ms, h_ss, 1.0 / P, EPS, ALU.mult, ALU.add).then_inc(h_ms_ready, 1)

                def gated(name, p, g, weights):
                    ov = src(name)[:, :].rearrange("p (h i d) -> p h i d", h=4, i=NT)
                    lo = 512 * p + 256 * g
                    dst = mix[:, :, lo:lo + 256].rearrange("p i (h d) -> p h i d", d=HD)
                    gate = gates[:, :, p, 256 * g:256 * g + 256].rearrange("p i (h d) -> p h i d", d=HD)
                    if g == 0:
                        for i in range(NT):
                            drained(dve, ("proj", 1, l, 4 * p + 3, i))
                    if weights is None:
                        free(dve.tensor_tensor(dst, ov, gate, ALU.mult), name)
                        if g == 1:
                            signal(mix_ready)
                        return
                    link(dve.reciprocal(row_inv, weights))
                    t = o_tmp[:, :].rearrange("p (h i d) -> p h i d", h=4, i=NT)
                    free(dve.tensor_tensor(t, ov, row_inv.unsqueeze(3).broadcast_to([P, 4, NT, HD]), ALU.mult), name)
                    if g == 1:
                        dve.tensor_tensor(dst, t, gate, ALU.mult).then_inc(mix_ready, 1)
                    else:
                        tt(dst, t, gate, ALU.mult)

                for s in timeline[1][l]:
                    kind = s[0]
                    if s in unit_no:
                        split_to(unit_no[s] + AHEAD)
                    elif kind == "proj_tile":
                        split_to(unit_no["proj", 1, l, 0, 2] + s[3])
                    if kind == "norm":
                        norm_step(*s[1:])
                    elif kind == "r_row":
                        factor_diag(s[1])
                    elif kind == "evac" and s[3] in FEATURE2:
                        if s[3] == 4:
                            drained(dve, ("r_row", 4 + l))
                        for i in range(NT):
                            key = ("proj", 1, l, s[3], i)
                            c = {4: 0, 5: 4, 8: 8, 9: 12}[s[3]] + 2 * i
                            free(dve.scalar_tensor_tensor(featT[:, c:c + 2, :], src(key)[:, :].rearrange("p (c t) -> p c t", c=2),
                                                          SCALE if s[3] == 4 else 1.0,
                                                          r_row[:, :].unsqueeze(1).broadcast_to([P, 2, T]), ALU.mult, ALU.mult), key)
                    elif kind == "forget_f":
                        drained(dve, ("r_row", 4 + l))
                        free(dve.tensor_tensor(rows[0:8, 2, :], src(s)[0:8, 0:T], r_row[0:8, :], ALU.mult), s)
                        link(dve.tensor_scalar(rows[0:8, 2, :], rows[0:8, 2, :], f_bias[:, l:l + 1], None, ALU.add))
                    elif kind == "forget_log":
                        f, e = rows[0:8, 2, :], rows[0:8, 1, :]
                        dve.scalar_tensor_tensor(e, f, -1.0, f, ALU.mult, ALU.min).then_inc(gate_abs, 1)
                        dve.wait_ge(gate_log, L + l + 1)
                        link(dve.scalar_tensor_tensor(f, f, 0.0, e, ALU.min, ALU.subtract))
                        link(dve.tensor_scalar(f, f, -0.5 / SCALE, None, ALU.mult))
                        link(dve.tensor_tensor_scan(rows[0:8, 0, :], f, f, 0.0, ALU.add, ALU.add))
                        link(dve.tensor_copy(row_hi[:, :], rows[0:8, 0, :]))
                        dve.tensor_tensor(row_lo[:, :], rows[0:8, 0, :], row_hi[:, :].bitcast(F32), ALU.subtract).then_inc(a_ready, 1)
                        prod = o_tmp[:, 0:2 * HD].rearrange("p (a d) -> p a d", a=2)
                        lv = lam_v[:, l, :, :].rearrange("p (a b) d -> p a b d", b=2)
                        tt(prod, lv[:, :, 0, :], lv[:, :, 1, :], ALU.mult)
                        dve.tensor_reduce(lam[:, 0:2], prod, AX.X, ALU.add).then_inc(lam_dots, 1)
                        dve.wait_ge(lam_exp, l + 1)
                        tt(lam[:, 2:3], lam[:, 1:2], lam[:, 0:1], ALU.subtract)
                        link(dve.tensor_scalar(lam[:, 3:4], lam[:, 2:3], -LAM_INIT[l], None, ALU.add))
                    elif kind == "rope2":
                        for j in (0, 1):
                            for i in range(NT):
                                drained(dve, ("proj", 1, l, j, i))
                        rope(0, 16)
                    elif kind in ("diff", "fox"):
                        if s[2] == "S":
                            row_max((kind, l), s[3])
                        elif s[2] == "V" and s[3] % GROUPS[kind] == GROUPS[kind] - 1:
                            g = s[3] // GROUPS[kind]
                            if kind == "diff":
                                epilogue_diff(g)
                            else:
                                gated(("fox", l, "O", g), 2, g, row_sum[:, g % 2])
                    elif kind == "stick" and s[2] == "K":
                        h = s[3]
                        z = ("stick", l, "Z", h)
                        ps = src(z)
                        dve.wait_ge(stick_log, 8 * l + h + 1)
                        free(dve.scalar_tensor_tensor(softp[:, h % 2, :], ps[:, 0:384], 0.0, softp[:, h % 2, :], ALU.max, ALU.add), z)
                        if h >= 2:
                            filled(dve, ("stick", l, "R", h - 2))
                        link(dve.tensor_copy(keep_hi[:, h % 2, :], softp[:, h % 2, :]))
                        dve.tensor_tensor(keep_lo[:, h % 2, :], softp[:, h % 2, :], keep_hi[:, h % 2, :].bitcast(F32),
                                          ALU.subtract).then_inc(keep_ready, 1)
                    elif kind == "stick" and s[2] == "V" and s[3] % 4 == 3:
                        gated(("stick", l, "O", s[3] // 4), 1, s[3] // 4, None)
                    elif kind == "mix_turn":
                        g, t = s[3], slice(s[4] * P, (s[4] + 1) * P)
                        turned(s, mixT_hi[g][:, 0:4, t], mixT_lo[g][:, 0:4, t])
                    elif kind == "post_norm":
                        _, m, i = s
                        dve.wait_ge(y_sumsq, 4 * m + 2 * i + 2)
                        tt(y_sum[:, i:i + 1], y_ss[:, 2 * i:2 * i + 1], y_ss[:, 2 * i + 1:2 * i + 2], ALU.add)
                        dve.tensor_scalar(y_mean[:, i:i + 1], y_sum[:, i:i + 1], 1.0 / D, EPS, ALU.mult, ALU.add).then_inc(y_ms, 1)
                        dve.wait_ge(y_rstd, NT * m + i + 1)
                        if i == 0:
                            dve.wait_ge(post_loaded, 16 * (m + 1))
                        for half in range(2):
                            key = ("out", 1, m, "acc", 2 * i + half)
                            c = slice(half * 512, (half + 1) * 512)
                            ps = src(key)
                            free(dve.scalar_tensor_tensor(o_tmp[:, :], ps[:, :], y_rs[:, i:i + 1], post_gain[:, c],
                                                          ALU.mult, ALU.mult), key)
                            ins = dve.tensor_tensor(x_sb[:, i, c], x_sb[:, i, c], o_tmp[:, :], ALU.add)
                            link(ins)
                            if m + 1 < L:
                                gained(5, i, half)
                        signal(x_tile_ready)


PRM_LOADS = 8 + 2 * L
PRM_ROW_LOADS = 2

_INS = ['x', 'w_in', 'b_if', 'conv_qk', 'm_norm', 'moba_qk_norm', 'nsa_q_norm', 'nsa_k_norm', 'cmp_pe', 'cmp_w1',
        'cmp_w2', 'w_out', 'norm_mix', 'norm_ffn', 'w_ff1', 'w_ff2', 'w_in_2', 'forget_bias_2', 'diff_lambda_2',
        'diff_subln_2', 'w_out_2', 'pre_norm_2', 'post_norm_2']


def kernel(**inputs):
    import concourse.bacc as bacc
    from concourse.bass_utils import run_bass_kernel_spmd

    nc = bacc.Bacc("TRN2", target_bir_lowering=False, num_devices=1)
    table, selector = constants()
    arrays, args = {}, []
    for name, a in [(n, inputs[n]) for n in _INS] + [("consts", table), ("selector", selector)]:
        a = np.ascontiguousarray(a)
        arrays[f"in_{name}"] = a
        args.append(nc.dram_tensor(f"in_{name}", a.shape, mybir.dt.from_np(a.dtype), kind="ExternalInput").ap())
    args.append(nc.dram_tensor("out_x", (1, T, D), F32, kind="ExternalOutput").ap())
    hybrid_blocks(nc, *args)
    r = run_bass_kernel_spmd(nc, [arrays], core_ids=[0])
    return r.results[0]["out_x"]
```
